# Optimizing a Trainium2 kernel written in Bass

```python
import math
import jax, jax.numpy as jnp
from jax import lax
import numpy as np

D_MODEL = 2048
BATCH = 1
SEQ = 256
DEPTH = 1
DEC_BATCH = 8
DEC_SEQ = 4
PAST_LEN = 2048
PAGE_SIZE = 128

D_MIX = D_MODEL
D_CONV = D_MIX // 2
CONV_GROUPS = 8
CONV_WIDTH = 31
D_ATTN = D_MIX - D_CONV
HEAD_DIM = 128
N_HEADS = D_ATTN // HEAD_DIM
N_KV_HEADS = 2
GQA_GROUP = N_HEADS // N_KV_HEADS
D_KV = N_KV_HEADS * HEAD_DIM
WINDOW = 128
BLOCK_Q = 128
SCALE = 1.0 / math.sqrt(HEAD_DIM)
N_EXPERT_GROUPS = 4
EXPERTS_PER_GROUP = 8
N_EXPERTS = N_EXPERT_GROUPS * EXPERTS_PER_GROUP
TOP_K = 2
D_EXPERT = D_MODEL // 4
MOE_BLOCK = 128
D_IN = 2 * D_CONV + D_ATTN + 2 * D_KV
EPS = 1e-6

kernel_name = 'hymba_conformer_swa_hiermoe_step'

def rms_norm(x, g):
    xf = x.astype(jnp.float32)
    y = xf * lax.rsqrt(jnp.mean(xf * xf, axis=-1, keepdims=True) + EPS)
    return (y * g.astype(jnp.float32)).astype(x.dtype)

def layer_norm(x, g, b):
    xf = x.astype(jnp.float32)
    xc = xf - jnp.mean(xf, axis=-1, keepdims=True)
    var = jnp.mean(xc * xc, axis=-1, keepdims=True)
    y = xc * lax.rsqrt(var + EPS) * g.astype(jnp.float32) + b.astype(jnp.float32)
    return y.astype(x.dtype)

def alibi_slopes():
    h = jnp.arange(1, N_HEADS + 1, dtype=jnp.float32)
    return jnp.exp2(-8.0 * h / N_HEADS).reshape(N_KV_HEADS, GQA_GROUP)

def sink_softmax(logits, valid, sink):
    logits = jnp.where(valid, logits, -jnp.inf)
    m = jnp.maximum(jnp.max(logits, axis=-1, keepdims=True), sink)
    p = jnp.exp(logits - m)
    return p / (jnp.sum(p, axis=-1, keepdims=True) + jnp.exp(sink - m))

def window_attention_prompt(q, k, v, sinks):
    B, T = q.shape[:2]
    nb = T // BLOCK_Q
    qb = q.reshape(B, nb, BLOCK_Q, N_KV_HEADS, GQA_GROUP, HEAD_DIM)
    kb = k.reshape(B, nb, BLOCK_Q, N_KV_HEADS, HEAD_DIM)
    vb = v.reshape(B, nb, BLOCK_Q, N_KV_HEADS, HEAD_DIM)
    pad = ((0, 0), (1, 0), (0, 0), (0, 0), (0, 0))
    kk = jnp.concatenate([jnp.pad(kb, pad)[:, :-1], kb], axis=2)
    vv = jnp.concatenate([jnp.pad(vb, pad)[:, :-1], vb], axis=2)
    q_rel = jnp.arange(BLOCK_Q) + BLOCK_Q
    k_rel = jnp.arange(2 * BLOCK_Q)
    dist = q_rel[:, None] - k_rel[None, :]
    k_abs = (jnp.arange(nb) * BLOCK_Q - BLOCK_Q)[:, None] + k_rel[None, :]
    valid = ((dist >= 0) & (dist < WINDOW))[None] & (k_abs >= 0)[:, None, :]
    s = jnp.einsum('bnqkgd,bnskd->bnkgqs', qb, kk).astype(jnp.float32) * SCALE
    s = s - alibi_slopes()[:, :, None, None] * dist.astype(jnp.float32)
    sink = sinks.astype(jnp.float32).reshape(N_KV_HEADS, GQA_GROUP, 1, 1)
    p = sink_softmax(s, valid[None, :, None, None], sink)
    o = jnp.einsum('bnkgqs,bnskd->bnqkgd', p.astype(v.dtype), vv)
    return o.reshape(B, T, D_ATTN), k[:, T - WINDOW:], v[:, T - WINDOW:]

def window_attention_sample(q, k, v, k_past, v_past, sinks):
    B, T = q.shape[:2]
    W = k_past.shape[1]
    kk = jnp.concatenate([k_past, k], axis=1)
    vv = jnp.concatenate([v_past, v], axis=1)
    q_abs = PAST_LEN + jnp.arange(T)
    k_abs = PAST_LEN - W + jnp.arange(W + T)
    dist = q_abs[:, None] - k_abs[None, :]
    valid = (dist >= 0) & (dist < WINDOW)
    qg = q.reshape(B, T, N_KV_HEADS, GQA_GROUP, HEAD_DIM)
    s = jnp.einsum('bqkgd,bskd->bkgqs', qg, kk).astype(jnp.float32) * SCALE
    s = s - alibi_slopes()[:, :, None, None] * dist.astype(jnp.float32)
    sink = sinks.astype(jnp.float32).reshape(N_KV_HEADS, GQA_GROUP, 1, 1)
    p = sink_softmax(s, valid, sink)
    o = jnp.einsum('bkgqs,bskd->bqkgd', p.astype(v.dtype), vv)
    return o.reshape(B, T, D_ATTN), kk[:, T:], vv[:, T:]

def causal_depthwise_conv(u_ext, conv_w, conv_b):
    out = lax.conv_general_dilated(u_ext, conv_w[:, None, :], window_strides=(1,), padding='VALID',
                                   dimension_numbers=('NWC', 'WIO', 'NWC'),
                                   feature_group_count=D_CONV)
    return out + conv_b

def hier_moe(x2, w_rg, b_rg, w_re, b_re, w1, w3, w2):
    N = x2.shape[0]
    g_prob = jax.nn.softmax((x2 @ w_rg).astype(jnp.float32) + b_rg.astype(jnp.float32), axis=-1)
    g_top, g_idx = lax.top_k(g_prob, 1)
    e_logits = ((x2 @ w_re).astype(jnp.float32) + b_re.astype(jnp.float32)).reshape(
        N, N_EXPERT_GROUPS, EXPERTS_PER_GROUP)
    e_in = jnp.take_along_axis(e_logits, g_idx[:, :, None], axis=1)[:, 0]
    e_top, e_loc = lax.top_k(jax.nn.softmax(e_in, axis=-1), TOP_K)
    gate = (g_top * e_top / jnp.sum(e_top, axis=-1, keepdims=True)).reshape(-1)
    eid = (g_idx * EXPERTS_PER_GROUP + e_loc).reshape(-1).astype(jnp.int32)
    tok = jnp.repeat(jnp.arange(N, dtype=jnp.int32), TOP_K)
    A = N * TOP_K
    order = jnp.argsort(eid)
    se, stok, sg = eid[order], tok[order], gate[order]
    counts = jnp.bincount(eid, length=N_EXPERTS).astype(jnp.int32)
    start = jnp.cumsum(counts) - counts
    pcounts = (counts + MOE_BLOCK - 1) // MOE_BLOCK * MOE_BLOCK
    pend = jnp.cumsum(pcounts)
    pstart = pend - pcounts
    dest = pstart[se] + (jnp.arange(A, dtype=jnp.int32) - start[se])
    nb = -(-A // MOE_BLOCK) + N_EXPERTS
    P = nb * MOE_BLOCK
    buf_tok = jnp.full((P,), N, dtype=jnp.int32).at[dest].set(stok)
    buf_gate = jnp.zeros((P,), jnp.float32).at[dest].set(sg)
    blk_start = jnp.arange(nb, dtype=jnp.int32) * MOE_BLOCK
    blk_exp = jnp.minimum(jnp.searchsorted(pend, blk_start, side='right'), N_EXPERTS - 1)
    x_pad = jnp.concatenate([x2, jnp.zeros((1, x2.shape[1]), x2.dtype)], axis=0)

    def run_block(args):
        rows, e = args
        xb = x_pad[rows]
        hdn = jax.nn.silu(xb @ w1[e]) * (xb @ w3[e])
        return hdn @ w2[e]

    out = lax.map(run_block, (buf_tok.reshape(nb, MOE_BLOCK), blk_exp)).reshape(P, -1)
    out = out * buf_gate[:, None].astype(out.dtype)
    return jax.ops.segment_sum(out, buf_tok, num_segments=N + 1)[:N]

def hybrid_layer(x, conv_past, k_past, v_past, norm1_g, w_in, conv_w, conv_b, conv_norm_g,
                 conv_norm_b, q_norm_g, k_norm_g, attn_sinks, w_out, norm2_g, w_rg, b_rg,
                 w_re, b_re, w1, w3, w2):
    B, T, _ = x.shape
    n = rms_norm(x, norm1_g)
    a, gt, q, k, v = jnp.split(n @ w_in, [D_CONV, 2 * D_CONV, 2 * D_CONV + D_ATTN,
                                          2 * D_CONV + D_ATTN + D_KV], axis=-1)
    u = a * jax.nn.sigmoid(gt)
    if conv_past is None:
        conv_past = jnp.zeros((B, CONV_WIDTH - 1, D_CONV), u.dtype)
    u_ext = jnp.concatenate([conv_past, u], axis=1)
    c = causal_depthwise_conv(u_ext, conv_w, conv_b)
    c = jax.nn.silu(layer_norm(c, conv_norm_g, conv_norm_b))
    new_conv = u_ext[:, -(CONV_WIDTH - 1):]
    q = rms_norm(q.reshape(B, T, N_HEADS, HEAD_DIM), q_norm_g)
    k = rms_norm(k.reshape(B, T, N_KV_HEADS, HEAD_DIM), k_norm_g)
    v = v.reshape(B, T, N_KV_HEADS, HEAD_DIM)
    if k_past is None:
        o, new_k, new_v = window_attention_prompt(q, k, v, attn_sinks)
    else:
        o, new_k, new_v = window_attention_sample(q, k, v, k_past, v_past, attn_sinks)
    x = x + jnp.concatenate([c, o], axis=-1) @ w_out
    h2 = rms_norm(x, norm2_g).reshape(B * T, D_MODEL)
    y = x + hier_moe(h2, w_rg, b_rg, w_re, b_re, w1, w3, w2).reshape(B, T, D_MODEL)
    return y, new_conv, new_k, new_v

def setup_inputs(seed: int = 0) -> dict:
    key = jax.random.key(seed)
    ks = jax.random.split(key, 24)
    f32 = jnp.float32

    def nrm(k, shape, scale):
        return jax.random.normal(k, shape, f32) * scale

    wbuf = min(WINDOW, PAST_LEN)
    return {
        'x_prompt': nrm(ks[0], (BATCH, SEQ, D_MODEL), 1.0),
        'x_sample': nrm(ks[1], (DEC_BATCH, DEC_SEQ, D_MODEL), 1.0),
        'state_conv': nrm(ks[2], (DEPTH, DEC_BATCH, CONV_WIDTH - 1, D_CONV), 0.5),
        'cache_k': nrm(ks[3], (DEPTH, DEC_BATCH, wbuf, N_KV_HEADS, HEAD_DIM), 1.0),
        'cache_v': nrm(ks[4], (DEPTH, DEC_BATCH, wbuf, N_KV_HEADS, HEAD_DIM), 1.0),
        'norm1_g': 1.0 + nrm(ks[5], (DEPTH, D_MODEL), 0.02),
        'w_in': nrm(ks[6], (DEPTH, D_MODEL, D_IN), D_MODEL ** -0.5),
        'conv_w': nrm(ks[7], (DEPTH, CONV_WIDTH, D_CONV), CONV_WIDTH ** -0.5),
        'conv_b': nrm(ks[8], (DEPTH, D_CONV), 0.02),
        'conv_norm_g': 1.0 + nrm(ks[9], (DEPTH, D_CONV), 0.02),
        'conv_norm_b': nrm(ks[10], (DEPTH, D_CONV), 0.02),
        'q_norm_g': 1.0 + nrm(ks[11], (DEPTH, HEAD_DIM), 0.02),
        'k_norm_g': 1.0 + nrm(ks[12], (DEPTH, HEAD_DIM), 0.02),
        'attn_sinks': nrm(ks[13], (DEPTH, N_HEADS), 1.0),
        'w_out': nrm(ks[14], (DEPTH, D_MIX, D_MODEL), D_MIX ** -0.5),
        'norm2_g': 1.0 + nrm(ks[15], (DEPTH, D_MODEL), 0.02),
        'w_router_group': nrm(ks[16], (DEPTH, D_MODEL, N_EXPERT_GROUPS), D_MODEL ** -0.5),
        'b_router_group': nrm(ks[17], (DEPTH, N_EXPERT_GROUPS), 0.01),
        'w_router_expert': nrm(ks[18], (DEPTH, D_MODEL, N_EXPERTS), D_MODEL ** -0.5),
        'b_router_expert': nrm(ks[19], (DEPTH, N_EXPERTS), 0.01),
        'w1': nrm(ks[20], (DEPTH, N_EXPERTS, D_MODEL, D_EXPERT), D_MODEL ** -0.5),
        'w3': nrm(ks[21], (DEPTH, N_EXPERTS, D_MODEL, D_EXPERT), D_MODEL ** -0.5),
        'w2': nrm(ks[22], (DEPTH, N_EXPERTS, D_EXPERT, D_MODEL), D_EXPERT ** -0.5),
    }

def reference(x_prompt, x_sample, state_conv, cache_k, cache_v, norm1_g, w_in, conv_w, conv_b,
              conv_norm_g, conv_norm_b, q_norm_g, k_norm_g, attn_sinks, w_out, norm2_g,
              w_router_group, b_router_group, w_router_expert, b_router_expert, w1, w3, w2):
    yp, ys = x_prompt, x_sample
    conv_p, k_p, v_p, conv_s, k_s, v_s = [], [], [], [], [], []
    for l in range(DEPTH):
        params = (norm1_g[l], w_in[l], conv_w[l], conv_b[l], conv_norm_g[l], conv_norm_b[l],
                  q_norm_g[l], k_norm_g[l], attn_sinks[l], w_out[l], norm2_g[l],
                  w_router_group[l], b_router_group[l], w_router_expert[l], b_router_expert[l],
                  w1[l], w3[l], w2[l])
        yp, c, kn, vn = hybrid_layer(yp, None, None, None, *params)
        conv_p.append(c)
        k_p.append(kn)
        v_p.append(vn)
        ys, c, kn, vn = hybrid_layer(ys, state_conv[l], cache_k[l], cache_v[l], *params)
        conv_s.append(c)
        k_s.append(kn)
        v_s.append(vn)
    return (yp, ys, jnp.stack(conv_p), jnp.stack(k_p), jnp.stack(v_p),
            jnp.stack(conv_s), jnp.stack(k_s), jnp.stack(v_s))


_drawn_inputs = setup_inputs


def setup_inputs(seed=0):
    import zlib

    import numpy as np

    out = dict(_drawn_inputs(seed))
    spreads = {}
    factors = {'conv_norm_g': 9.119,
     'q_norm_g': 3.94,
     'k_norm_g': 3.043,
     'b_router_group': 21.866,
     'b_router_expert': 12.732,
     'conv_norm_b': 3.357,
     'attn_sinks': 8.0,
     'norm2_g': 2.828}
    for name, (base, spread) in spreads.items():
        noise = np.random.default_rng([zlib.crc32(name.encode()), seed]).standard_normal(out[name].shape)
        drawn = base * np.exp(spread * noise) if base else spread * noise
        out[name] = __import__('jax').numpy.asarray(drawn.astype(out[name].dtype))
    for name, factor in factors.items():
        out[name] = (out[name] * factor).astype(out[name].dtype)
    return out
```

```python
from contextlib import ExitStack

import concourse.bass as bass
import numpy as np
from concourse import mybir

F32 = mybir.dt.float32
I32 = mybir.dt.int32
U32 = mybir.dt.uint32
ALU = mybir.AluOpType
ACT = mybir.ActivationFunctionType
AX = mybir.AxisListType

P = 128
D = 2048
KT = D // P
DC = 1024
CJ = DC // P
CW = 31
PAST = CW - 1
NH, NKV, HD = 8, 2, 128
GQA = NH // NKV
W = 128
TP = 256
NB, TB = 8, 4
TS = NB * TB
T = TP + TS
TILES = [(0, P), (P, P), (TP, TS)]
NG, EG = 4, 8
NE = NG * EG
DE = 512
NA = 2 * T
BLK = 64
NSTEP = NE + NA // BLK - 1
XW = NA + BLK
GC = 512
CK = 4
NCH = KT // CK
EPS = 1e-6
SCALE = 1.0 / float(np.sqrt(HD))
MASKED = -1e30
NKS = NKV * W + NKV * TS


def shape_constants():
    cs = np.zeros((P, C_SIZE), np.float32)
    cs[:, C_ID:C_ID + P] = np.eye(P)
    cs[:, C_ONE:C_ONE + P] = 1.0
    cs[:, C_TRI:C_TRI + P] = np.triu(np.ones((P, P)), 1)
    cs[:, C_ROW:C_ROW + NA] = np.arange(NA)
    cs[:, C_COL] = np.arange(P)
    rows = np.arange(P)
    cs[rows, C_HSEL + (rows % 32) // TB] = 1.0
    slope = 2.0 ** (-8.0 * np.arange(1, NH + 1) / NH)
    dist = np.arange(P)[:, None] + P - np.arange(2 * P)[None, :]
    ok = (dist >= 0) & (dist < W)
    prompt = np.where(ok[:, None], -slope[None, :, None] * dist[:, None], MASKED)
    sample = np.full((P, 2, NKS), MASKED)
    for r in range(P):
        h, t = (r % 32) // TB, r % TB
        kv = h // GQA
        for i in range(2):
            b = 4 * i + r // 32
            for c in range(W):
                if W + t - c < W:
                    sample[r, i, kv * W + c] = -slope[h] * (W + t - c)
            for u in range(t + 1):
                sample[r, i, NKV * W + kv * TS + TB * b + u] = -slope[h] * (t - u)
    ca = np.concatenate([prompt.reshape(P, -1), sample.reshape(P, -1)], 1).astype(np.float32)
    return cs, ca


C_ID, C_ONE, C_TRI = 0, P, 2 * P
C_ROW = 3 * P
C_COL = C_ROW + NA
C_HSEL = C_COL + 1
C_SIZE = C_HSEL + NH
CA_SIZE = NH * 2 * P + 2 * NKS


def hybrid_layer(nc, x_prompt, x_sample, state_conv, cache_k, cache_v, norm1_g, w_in, conv_w, conv_b,
                 conv_norm_g, conv_norm_b, q_norm_g, k_norm_g, attn_sinks, w_out, norm2_g,
                 w_router_group, b_router_group, w_router_expert, b_router_expert, w1, w3, w2,
                 const_small, const_attn,
                 y_prompt, y_sample, conv_prompt, k_prompt, v_prompt, conv_sample, k_sample, v_sample):
    with ExitStack() as ctx:
        def sem(name):
            return ctx.enter_context(nc.semaphore(name))

        def sb(name, n, dt=F32):
            return ctx.enter_context(nc.sbuf_tensor(name, [P, n], dt))

        wbuf = [sb(f"wbuf{b}", KT * GC) for b in range(3)]
        x_sb = sb("x_sb", 3 * D)
        cst = sb("cst", C_SIZE)
        small = sb("small", 32 + CJ * CW + NH)
        gains = sb("gains", 2 * KT)
        wr = sb("wr", KT * (NG + NE))
        rbias = sb("rbias", NG + NE)
        misc = sb("misc", 200)
        ktok_all = sb("ktok", 2 * NKV * HD)[:, :]
        ktok = ktok_all.rearrange("p (i c) -> p i c", i=2)
        ui = sb("ui", 64, U32)
        steps_i = sb("steps_i", 2 * 64 + 1, I32)
        R_SIZE = 2 * KT * T + (NH + NKV) * T + CJ * (PAST + TP) + CJ * NB * (PAST + TB) + 8 * T + NKV * T
        reg = sb("reg", R_SIZE)

        def view(t, at, *dims):
            n = int(np.prod(dims))
            v = t[:, at:at + n]
            if len(dims) == 1:
                return v
            names = "abc"[:len(dims)]
            return v.rearrange(f"p ({' '.join(names)}) -> p {' '.join(names)}", **dict(zip(names, dims)))

        x3 = view(x_sb, 0, 3, D)
        ident = cst[:, C_ID:C_ID + P]
        ones = cst[:, C_ONE:C_ONE + P]
        tri = cst[:, C_TRI:C_TRI + P]
        row = cst[:, C_ROW:C_ROW + NA]
        col = cst[:, C_COL:C_COL + 1]
        hsel = cst[:, C_HSEL:C_HSEL + NH]
        taps = view(small, 32, CJ, CW)
        sinks = small[:, 32 + CJ * CW:32 + CJ * CW + NH]
        convb, lng, lnb = (small[:, CJ * i:CJ * i + CJ] for i in range(3))
        qg, kg = small[:, 24:25], small[:, 25:26]
        g1, g2 = gains[:, 0:KT], gains[:, KT:2 * KT]
        wr3 = view(wr, 0, KT, NG + NE)
        o = 0
        nT = view(reg, o, KT, T)
        a_bias, a_P, a_V = o, o + CA_SIZE, o + CA_SIZE + 1024
        o += KT * T
        mixT = view(reg, o, KT, T)
        xn = view(reg, o, 3, D)
        o += KT * T
        qkT = view(reg, o, NH + NKV, T)
        o += (NH + NKV) * T
        up = view(reg, o, CJ, PAST + TP)
        utok = view(reg, o, 2, DC)
        o += CJ * (PAST + TP)
        us = view(reg, o, CJ, NB * (PAST + TB))
        rows_cw = reg[0:CW, o:o + DC]
        rows_vec = reg[0:26, o + DC:o + DC + P]
        row_sink = reg[0:1, o + DC + P:o + DC + P + NH]
        o += CJ * NB * (PAST + TB)
        aT, sgT = view(reg, o, 4, T), view(reg, o + 4 * T, 4, T)
        state = view(reg, o, 2, DC)
        PT = view(reg, o, 2, 512)
        PTs = view(reg, o + 1024, 2, 512)
        o += 8 * T
        vT = view(reg, o, NKV, T)
        o += NKV * T
        assert o <= R_SIZE
        abias = view(reg, a_bias, NH, 2 * P)
        sbias = view(reg, a_bias + NH * 2 * P, 2, NKS)
        prob = view(reg, a_P, 2, 512)
        vtok = view(reg, a_V, 3, NKV * HD)
        assert a_V + 3 * NKV * HD <= KT * T
        kc = view(x_sb, 0, NB, NKV * HD)
        vc = view(x_sb, 2048, NB, NKV * HD)
        keysT = view(x_sb, 4096, NB, NKV * W)
        sq = view(x_sb, 0, 2, T)
        rr = view(x_sb, 2 * T, 2, T)
        probs = view(x_sb, 4 * T, 2, NKS)
        qs = view(x_sb, 4 * T + 2 * NKS, NB, NH * TB)
        lsq = view(reg, a_bias, CJ, T)
        lmean, lrstd = view(reg, a_bias + CJ * T, T), view(reg, a_bias + CJ * T + T, T)
        yT = view(reg, 4 * 0, 4, T)
        h2 = view(reg, 0, 3, D)
        xd = view(reg, 3 * D, KT, XW)
        h2T = view(reg, 3 * D, KT, T)
        pick = view(reg, 3 * D + KT * XW, 3, NA)
        o = 3 * D + KT * XW
        ystage = reg[:, o:o + 1024]
        h1s = view(reg, o + 1024, 4, BLK)
        hT = view(reg, o + 1280, 4, BLK)
        got = view(reg, 0, 6, D)
        eps = misc[:, 0:1]
        rt0 = 3 * D + KT * XW + 3 * NA
        at = [0]

        def part(*dims):
            at[0] += int(np.prod(dims))
            assert rt0 + at[0] <= R_SIZE
            return view(reg, rt0 + at[0] - int(np.prod(dims)), *dims)

        expd = part(15)
        lg8, mg = part(3, 8), part(3, 8)
        le, ein, me = part(3, NE), part(3, EG), part(3, 8)
        gf, e1, e2 = part(3), part(3), part(3)
        gone, prod = part(3, NG), part(3, NE)
        hot1, hot2, hot = part(3, NE), part(3, NE), part(3, NE)
        xpos, xslot = part(3, NE), part(3, NE)
        cnt, start, nblk, cum, sid, off = (part(NE) for _ in range(6))
        pos, slot = part(3, 2), part(3, 2)
        tle, tid, tab = part(NE), part(NE), part(2)
        gsum, gate1, gate2 = part(3), part(3), part(3)
        bank = [ctx.enter_context(nc.psum_tensor(f"bank{b}", [P, 512], F32)) for b in range(8)]
        slots_dram = nc.dram_tensor("expert_rows", [NSTEP * BLK, D], F32, kind="Internal").ap()

        def bk(b, *dims, at=0):
            return view(bank[b], at, *dims)

        consts_in, x_in, g_in, rows_in, state_in, kc_in, vc_in, bias_in, wr_in, x_again, outs = (
            sem(n) for n in ("consts_in", "x_in", "g_in", "rows_in", "state_in", "kc_in", "vc_in",
                             "bias_in", "wr_in", "x_again", "outs"))
        w_in_sem = [[sem(f"w_landed{b}{c}") for c in range(NCH)] for b in range(3)]
        w_free = [[sem(f"w_free{b}{c}") for c in range(NCH - 1)] for b in range(3)]
        pool_set, zero_set, rows_zero = sem("pool_set"), sem("zero_set"), sem("rows_zero")
        x_ms, x_rstd, xn_ready = sem("x_ms"), sem("x_rstd"), sem("xn_ready")
        small_ps, small_sb = sem("small_ps"), sem("small_sb")
        nT_ps, nT_sb, st_ps, st_sb = sem("nT_ps"), sem("nT_sb"), sem("st_ps"), sem("st_sb")
        kc_ps, kc_sb = sem("kc_ps"), sem("kc_sb")
        proj_ps, proj_sb, g_sb, u_ready = sem("proj_ps"), sem("proj_sb"), sem("g_sb"), sem("u_ready")
        conv_done = sem("conv_done")
        sq_done, ss_ps, rt_done, qk_ready = sem("sq_done"), sem("ss_ps"), sem("rt_done"), sem("qk_ready")
        tok_ps, tok_sb, utok_ps, utok_sb = sem("tok_ps"), sem("tok_sb"), sem("utok_ps"), sem("utok_sb")
        s_ps, s_sb, s_max, p_exp, p_ready = sem("s_ps"), sem("s_sb"), sem("s_max"), sem("p_exp"), sem("p_ready")
        pt_ps, pt_sb, o_ps, o_sb = sem("pt_ps"), sem("pt_sb"), sem("o_ps"), sem("o_sb")
        ln_ps, ln_sq, ln_rt, ln_n, mix_ready = sem("ln_ps"), sem("ln_sq"), sem("ln_rt"), sem("ln_n"), sem("mix_ready")
        y_ps, yT_sb, yt_ps, x1_part = sem("y_ps"), sem("yT_sb"), sem("yt_ps"), sem("x1_part")
        h2_ms, h2_rt, h2_rec, h2_ready = sem("h2_ms"), sem("h2_rt"), sem("h2_rec"), sem("h2_ready")
        h2T_ps, h2T_sb, lg_ps, r_sub, r_exp = sem("h2T_ps"), sem("h2T_sb"), sem("lg_ps"), sem("r_sub"), sem("r_exp")
        hot_ready, rank_ps, pick_ready, tab_ready, tab_ps, steps_ready = (
            sem(n) for n in ("hot_ready", "rank_ps", "pick_ready", "tab_ready", "tab_ps", "steps_ready"))
        slots_ready, xd_ps, xd_a, xd_v = sem("slots_ready"), sem("xd_ps"), sem("xd_a"), sem("xd_v")
        h1_ps, h3_ps, h1_sb, hT_ready, ye_ps, ye_a, ye_v, ye_out = (
            sem(n) for n in ("h1_ps", "h3_ps", "h1_sb", "hT_ready", "ye_ps", "ye_a", "ye_v", "ye_out"))
        got_in = [sem(f"got_in{i}") for i in range(6)]
        rows_stored, y_ready = sem("rows_stored"), sem("y_ready")
        dchain = sem("vector_chain")
        cchain = sem("conv_chain")

        block = ctx.enter_context(nc.Block())

        def step_count(eng):
            return eng.value_load(steps_i[0:1, 128:129], min_val=1, max_val=NSTEP)

        @block.sync
        def _(sp):
            def group(b, src, first):
                for c in range(NCH):
                    sp.dma_start(view(wbuf[b], c * CK * GC, CK, GC), src(c, first)).then_inc(w_in_sem[b][c], 16)

            def in_cols(c, first):
                return w_in.rearrange("(p k) n -> p k n", k=KT)[:, CK * c:CK * c + CK, bass.ds(first, GC)]

            def out_cols(c, first):
                return w_out.rearrange("(k p) n -> p k n", p=P)[:, CK * c:CK * c + CK, bass.ds(first, GC)]

            sp.wait_ge(x_in, 48)
            for i in range(2):
                for b in range(3):
                    if i:
                        sp.wait_ge(proj_ps, 4 * b + 4)
                    group(b, in_cols, i * GC + 1024 * b)
                if i == 0:
                    sp.wait_ge(zero_set, 1)
                    zero = ktok_all.unsqueeze(1).to_broadcast([P, D // GC, GC])
                    for a in range(NSTEP * BLK // P):
                        sp.dma_start(slots_dram[P * a:P * a + P, :].rearrange("p (r c) -> p r c", c=GC), zero
                                     ).then_inc(rows_zero, 16)
            sp.wait_ge(proj_ps, 16)
            group(0, in_cols, 3072)
            for b in (1, 2):
                sp.wait_ge(proj_ps, 16 + 4 * b)
                group(b, out_cols, GC * (b - 1))

            def expert(b, e, free):
                for c in range(NCH):
                    free(c)
                    if b < 2:
                        src = (w1, w3)[b][bass.ds(e, 1)].rearrange("o (p k) n -> p (o k n)", k=KT)
                        src = src[:, CK * GC * c:CK * GC * c + CK * GC]
                    else:
                        src = w2[bass.ds(e, 1)].rearrange("o (c p) n -> p (o c) n", p=P)[:, c, :]
                    sp.dma_start(view(wbuf[b], c * CK * GC, CK * GC), src).then_inc(w_in_sem[b][c], 16)

            sp.wait_ge(proj_ps, 28)
            expert(0, 0, lambda c: None)
            for b in (1, 2):
                sp.wait_ge(y_ps, 4 * b)
                group(b, out_cols, GC * (b + 1))
            for b in (1, 2):
                sp.wait_ge(y_ps, 8 + 4 * b)
                expert(b, 0, lambda c: None)
            sp.wait_ge(steps_ready, 1)
            n = step_count(sp)
            with sp.Fori(1, NSTEP) as s:
                with sp.If(s < n):
                    e = sp.value_load(steps_i[0:1, bass.ds(s, 1)], min_val=0, max_val=NE - 1)
                    for b in range(3):
                        expert(b, e, lambda c: sp.wait_ge(w_free[b][c] if c < NCH - 1 else (h1_ps, h3_ps, ye_ps)[b], s))

        @block.gpsimd
        def _(pool):
            pool.memset(ktok_all, 0.0).then_inc(zero_set, 1)
            pool.memset(eps, EPS).then_inc(pool_set, 1)
            pool.memset(up[:, :, 0:PAST], 0.0).then_inc(pool_set, 1)
            pool.memset(ui[:, :], 0).then_inc(pool_set, 1)
            pool.wait_ge(yt_ps, 4)
            pool.wait_ge(h2T_sb, 9)
            pool.wait_ge(lg_ps, 1)
            pool.memset(xd[:, :, NA:XW], 0.0).then_inc(pool_set, 1)
            pool.wait_ge(slots_ready, 1)
            n = step_count(pool)
            pool.wait_ge(ye_out, 32 * n + 32)
            pool.sem_inc(rows_stored, 1)
            pool.wait_ge(rows_stored, 1)
            for i, (t0, nt) in enumerate(TILES):
                for c in range(2):
                    pool.indirect_dma_start(got[0:nt, 2 * i + c, :], None, slots_dram,
                                            bass.IndirectOffsetOnAxis(ap=ui[0:nt, 48 + 2 * i + c:49 + 2 * i + c], axis=0)
                                            ).then_inc(got_in[2 * i + c], 16)

        @block.scalar
        def _(act):
            act.sem_inc(proj_sb, 4)
            act.sem_inc(ye_a, 1)
            act.sem_inc(ye_out, 32)
            act.dma_start(x3[:, 0, :], x_prompt[0:P, :]).then_inc(x_in, 16)
            act.dma_start(cst[:, :], const_small).then_inc(consts_in, 16)
            act.dma_start(x3[:, 1, :], x_prompt[P:TP, :]).then_inc(x_in, 16)
            act.dma_start(x3[0:TS, 2, :], x_sample).then_inc(x_in, 16)
            act.dma_start(g1, norm1_g.rearrange("(p k) -> p k", k=KT)).then_inc(g_in, 16)
            act.dma_start(g2, norm2_g.rearrange("(p k) -> p k", k=KT)).then_inc(g_in, 16)
            act.dma_start(rows_cw, conv_w).then_inc(rows_in, 16)
            for i, v in enumerate((conv_b, conv_norm_g, conv_norm_b)):
                act.dma_start(rows_vec[CJ * i:CJ * i + CJ, :], v.rearrange("(j p) -> j p", p=P)).then_inc(rows_in, 16)
            for i, v in enumerate((q_norm_g, k_norm_g)):
                act.dma_start(rows_vec[24 + i:25 + i, :], v.rearrange("(o p) -> o p", o=1)).then_inc(rows_in, 16)
            act.dma_start(row_sink, attn_sinks.rearrange("(o h) -> o h", o=1)).then_inc(rows_in, 16)
            act.dma_start(state[0:4 * PAST, :, :], state_conv.rearrange("(i b) r c -> (b r) i c", i=2)
                          ).then_inc(state_in, 16)
            act.dma_start(wr3[:, :, 0:NG], w_router_group.rearrange("(p k) g -> p k g", k=KT)).then_inc(wr_in, 16)
            act.dma_start(wr3[:, :, NG:], w_router_expert.rearrange("(p k) g -> p k g", k=KT)).then_inc(wr_in, 16)
            act.dma_start(rbias[0:1, 0:NG], b_router_group.rearrange("(o g) -> o g", o=1)).then_inc(wr_in, 16)
            act.dma_start(rbias[0:1, NG:], b_router_expert.rearrange("(o g) -> o g", o=1)).then_inc(wr_in, 16)
            act.dma_start(k_sample[:, 0:W - TB, :], cache_k[:, TB:W, :]).then_inc(outs, 16)
            act.dma_start(v_sample[:, 0:W - TB, :], cache_v[:, TB:W, :]).then_inc(outs, 16)
            act.dma_start(conv_sample[:, 0:PAST - TB, :], state_conv[:, TB:PAST, :]).then_inc(outs, 16)

            for i, (t0, nt) in enumerate(TILES):
                act.wait_ge(x_in, 48)
                act.activation(xn[0:nt, i, :], x3[0:nt, i, :], ACT.Square, accum_out=misc[0:nt, 1 + i:2 + i]
                               ).then_inc(x_ms, 1)
            act.wait_ge(pool_set, 1)
            act.wait_ge(x_ms, 3)
            for i, (t0, nt) in enumerate(TILES):
                act.activation(misc[0:nt, 4 + i:5 + i], misc[0:nt, 1 + i:2 + i], ACT.Sqrt, bias=eps[0:nt],
                               scale=1.0 / D).then_inc(x_rstd, 1)
            for j in range(CJ):
                act.wait_ge(st_ps, j // 2 + 1)
                act.wait_ge(small_sb, 1)
                act.activation(us[:, j, 0:NB * PAST].rearrange("p (r b) -> p b r", b=NB),
                               bk(j // 2, 2, NB, PAST)[:, j % 2], ACT.Copy).then_inc(st_sb, 1)
            act.wait_ge(xn_ready, 3)
            act.dma_start(kc, cache_k.rearrange("b s c -> s b c")).then_inc(kc_in, 16)
            act.dma_start(vc, cache_v.rearrange("b s c -> s b c")).then_inc(vc_in, 16)

            with act.Fori(0, 2) as i:
                act.wait_ge(u_ready, 4 * i + 4)
                for m in range(12):
                    act.wait_ge(proj_ps, 12 * i + m + 1)
                    if m < 4:
                        act.activation(aT[:, m, :], bk(m % 4, T), ACT.Copy).then_inc(proj_sb, 1)
                    elif m < 8:
                        ins = act.activation(sgT[:, m - 4, :], bk(m % 4, T), ACT.Sigmoid)
                        ins.then_inc(proj_sb, 1)
                    else:
                        act.activation(qkT[:, bass.ds(4 * i + m - 8, 1), :].rearrange("p o t -> p (o t)"),
                                       bk(m % 4, T), ACT.Copy).then_inc(proj_sb, 1)
            for q in range(4):
                act.wait_ge(kc_ps, q + 1)
                act.activation(keysT[:, 2 * q:2 * q + 2, :].rearrange("p b k -> p (b k)"), bk(4 + q, 512), ACT.Copy
                               ).then_inc(kc_sb, 1)
            for m in range(4):
                act.wait_ge(proj_ps, 24 + m + 1)
                act.activation(qkT[:, NH + m, :] if m < 2 else vT[:, m - 2, :], bk(m, T), ACT.Copy
                               ).then_inc(proj_sb, 1)
            act.wait_ge(proj_ps, 28)
            act.dma_start(reg[:, a_bias:a_bias + CA_SIZE], const_attn).then_inc(bias_in, 16)
            for h in range(NH + NKV):
                if h == 0:
                    act.wait_ge(proj_sb, 32)
                    act.wait_ge(kc_ps, 4)
                if h >= 2:
                    act.wait_ge(ss_ps, h - 1)
                act.activation(sq[:, h % 2, :], qkT[:, h, :], ACT.Square).then_inc(sq_done, 1)
                if h >= 1:
                    g = h - 1
                    act.wait_ge(ss_ps, g + 1)
                    if g >= 2:
                        act.wait_ge(qk_ready, g - 1)
                    act.activation(rr[:, g % 2, :], bk(4 + g % 2, T), ACT.Sqrt, bias=eps, scale=1.0 / HD
                                   ).then_inc(rt_done, 1)
            g = NH + NKV - 1
            act.wait_ge(ss_ps, g + 1)
            act.wait_ge(qk_ready, g - 1)
            act.activation(rr[:, g % 2, :], bk(4 + g % 2, T), ACT.Sqrt, bias=eps, scale=1.0 / HD).then_inc(rt_done, 1)
            act.wait_ge(tok_ps, 1)
            act.activation(vtok[:, 0:2, :].rearrange("p i c -> p (i c)"), bk(6, 512), ACT.Copy).then_inc(tok_sb, 1)
            act.activation(vtok[0:TS, 2, :], bank[7][0:TS, 0:256], ACT.Copy).then_inc(tok_sb, 1)

            for u in range(10):
                act.wait_ge(s_max, u + 1)
                if u < 8:
                    kw = P * (u // 4 + 1)
                    pv = prob[:, u % 2, 0:2 * kw].rearrange("p (h k) -> p h k", h=2)
                    for j in range(2):
                        act.activation(pv[:, j, :], pv[:, j, :], ACT.Exp, bias=misc[:, 20 + 8 * (u % 2) + j:21 + 8 * (u % 2) + j],
                                       accum_out=misc[:, 22 + 8 * (u % 2) + j:23 + 8 * (u % 2) + j]).then_inc(p_exp, 1)
                    act.activation(misc[:, 24 + 8 * (u % 2):26 + 8 * (u % 2)], misc[:, 26 + 8 * (u % 2):28 + 8 * (u % 2)],
                                   ACT.Exp).then_inc(p_exp, 1)
                else:
                    k = 20 + 8 * (u % 2)
                    act.activation(probs[:, u % 2, :], probs[:, u % 2, :], ACT.Exp, bias=misc[:, k:k + 1],
                                   accum_out=misc[:, k + 2:k + 3]).then_inc(p_exp, 2)
                    act.activation(misc[:, k + 4:k + 5], misc[:, k + 6:k + 7], ACT.Exp).then_inc(p_exp, 1)
                act.wait_ge(pt_ps, u + 1)
                if u < 8:
                    if u >= 2:
                        act.wait_ge(o_ps, u - 1)
                    n = 256 * (u // 4 + 1)
                    act.activation(PT[:, u % 2, 0:n], bk(6, 512)[:, 0:n], ACT.Copy).then_inc(pt_sb, 1)
                else:
                    act.activation(PTs[:, u % 2, 0:256], bk(6, 512)[:, 0:256], ACT.Copy).then_inc(pt_sb, 1)
                    act.activation(PTs[0:TS, u % 2, 256:512], bank[6][0:TS, 256:512], ACT.Copy).then_inc(pt_sb, 1)

            act.wait_ge(ln_n, 1)
            act.activation(lsq.rearrange("p j t -> p (j t)"), mixT[:, 0:CJ, :].rearrange("p j t -> p (j t)"), ACT.Square
                           ).then_inc(ln_sq, 1)
            act.wait_ge(ln_ps, 2)
            act.activation(lrstd, bk(1, T), ACT.Sqrt, bias=eps, scale=1.0 / DC).then_inc(ln_rt, 1)
            act.wait_ge(ln_n, 2)
            for j in range(CJ):
                act.activation(mixT[:, j, :], mixT[:, j, :], ACT.Silu, bias=lnb[:, j:j + 1], scale=lng[:, j:j + 1]
                               ).then_inc(mix_ready, 1)
            act.wait_ge(tok_sb, 6)
            act.dma_start(k_prompt, ktok[:, 0, :]).then_inc(outs, 16)
            act.dma_start(v_prompt, vtok[:, 1, :]).then_inc(outs, 16)
            for b in range(NB):
                act.dma_start(k_sample[b, W - TB:W, :], ktok[TB * b:TB * b + TB, 1, :]).then_inc(outs, 16)
                act.dma_start(v_sample[b, W - TB:W, :], vtok[TB * b:TB * b + TB, 2, :]).then_inc(outs, 16)
            act.wait_ge(utok_sb, 4)
            act.dma_start(conv_prompt, utok[0:PAST, 0, :]).then_inc(outs, 16)
            for t in range(TB):
                act.dma_start(conv_sample[:, PAST - TB + t, :], utok[NB * t:NB * t + NB, 1, :]).then_inc(outs, 16)
            act.wait_ge(o_sb, 10)
            act.dma_start(x3[:, 0, :], x_prompt[0:P, :]).then_inc(x_again, 16)
            act.dma_start(x3[:, 1, :], x_prompt[P:TP, :]).then_inc(x_again, 16)
            act.dma_start(x3[0:TS, 2, :], x_sample).then_inc(x_again, 16)
            for m in range(KT):
                act.wait_ge(y_ps, m + 1)
                if m % 4 == 0 and m:
                    act.wait_ge(yt_ps, m // 4)
                act.activation(yT[:, m % 4, :], bk(m % 4, T), ACT.Copy).then_inc(yT_sb, 1)
            act.wait_ge(outs, OUTS_MIX)
            for i, (t0, nt) in enumerate(TILES):
                act.wait_ge(x1_part, 3 * 3 + i + 1)
                act.activation(h2[0:nt, i, :], x3[0:nt, i, :], ACT.Square, accum_out=misc[0:nt, 7 + i:8 + i]
                               ).then_inc(h2_ms, 1)
            act.wait_ge(h2_ms, 3)
            for i, (t0, nt) in enumerate(TILES):
                act.activation(misc[0:nt, 10 + i:11 + i], misc[0:nt, 7 + i:8 + i], ACT.Sqrt, bias=eps[0:nt],
                               scale=1.0 / D).then_inc(h2_rt, 1)
            for i, (t0, nt) in enumerate(TILES):
                act.wait_ge(h2_rec, 1)
                act.activation(h2[0:nt, i, :].rearrange("t (k p) -> t p k", p=P),
                               x3[0:nt, i, :].rearrange("t (p k) -> t p k", p=P), ACT.Copy,
                               scale=misc[0:nt, 13 + i:14 + i]).then_inc(h2_ready, 1)
            act.wait_ge(r_sub, 1)
            act.activation(expd, expd, ACT.Exp).then_inc(r_exp, 1)
            for k in range(KT):
                act.wait_ge(xd_ps, 2 * k + 1)
                act.activation(xd[:, k, 0:T], bk(2 * (k % 4), T), ACT.Copy, scale=g2[:, k:k + 1]).then_inc(xd_a, 1)
            act.wait_ge(rows_zero, 16 * (NSTEP * BLK // P))
            act.wait_ge(steps_ready, 1)
            n = step_count(act)
            with act.Fori(0, NSTEP) as s:
                with act.If(s < n):
                    act.wait_ge(h1_ps, s + 1)
                    act.wait_ge(hT_ready, s + 1)
                    act.activation(h1s.rearrange("p m t -> p (m t)"), bk(0, 256), ACT.Silu).then_inc(h1_sb, 1)
                    act.wait_ge(ye_ps, s + 1)
                    act.wait_ge(ye_out, 32 * s + 32)
                    act.activation(ystage[:, 0:512], bk(2, 512), ACT.Copy).then_inc(ye_a, 1)
                    act.wait_ge(ye_a, s + 2)
                    act.wait_ge(ye_v, s + 2)
                    for half in range(2):
                        act.dma_start(slots_dram[bass.ds(s * BLK, BLK), 1024 * half:1024 * half + 1024],
                                      ystage[BLK * half:BLK * half + BLK, :]).then_inc(ye_out, 16)
            for i, (t0, nt) in enumerate(TILES):
                act.wait_ge(y_ready, i + 1)
                dst = y_prompt[t0:t0 + nt, :] if i < 2 else y_sample
                act.dma_start(dst, x3[0:nt, i, :]).then_inc(outs, 16)
            act.wait_ge(outs, OUTS_MIX + 48)

        @block.tensor
        def _(pe):
            def turn(out, in_):
                k = in_.shape[0]
                return pe.transpose(out, in_, ident[0:k, 0:k])

            pe.wait_ge(consts_in, 16)
            pe.wait_ge(rows_in, 16 * 7)
            turn(bk(7, 26), rows_vec)
            for j in range(CJ):
                turn(bk(7, CW, at=32 + CW * j), rows_cw[:, P * j:P * j + P])
            pe.matmul(bk(7, NH, at=32 + CJ * CW), ones[0:1, :], row_sink, start=True, stop=True).then_inc(small_ps, 1)
            f = 0
            for i, (t0, nt) in enumerate(TILES):
                pe.wait_ge(xn_ready, i + 1)
                per = 512 // nt
                for q in range(KT // per):
                    if f >= 2:
                        pe.wait_ge(nT_sb, f - 1)
                    for k in range(per):
                        ins = turn(bk(4 + f % 2, nt, at=nt * k),
                                   xn[0:nt, i, :].rearrange("t (p k) -> t k p", k=KT)[:, per * q + k, :])
                    ins.then_inc(nT_ps, 1)
                    f += 1
            pe.wait_ge(state_in, 16)
            for j in range(CJ):
                for i in range(2):
                    ins = turn(bk(j // 2, 4 * PAST, at=8 * PAST * (j % 2) + 4 * PAST * i),
                               state[0:4 * PAST, i, P * j:P * j + P])
                if j % 2:
                    ins.then_inc(st_ps, 1)

            def project(b, m, rhs, done):
                w = view(wbuf[b], 0, KT, GC)
                for k in range(KT):
                    ins = pe.matmul(bk(m, T), w[:, k, P * m:P * m + P], rhs[:, k, :], start=(k == 0), stop=(k == KT - 1))
                ins.then_inc(done, 1)

            pe.wait_ge(nT_sb, 9)
            pe.wait_ge(st_sb, CJ)
            pe.wait_ge(small_sb, 1)
            with pe.Fori(0, 2) as i:
                for b in range(3):
                    for c in range(NCH):
                        pe.wait_ge(w_in_sem[b][c], 16 * i + 16)
                    for m in range(4):
                        pe.wait_ge(proj_sb, 12 * i + 4 * b + m + 1)
                        project(b, m, nT, proj_ps)
            pe.wait_ge(kc_in, 16)
            for q in range(4):
                for b in range(2):
                    for kv in range(NKV):
                        ins = turn(bk(4 + q, P, at=256 * b + 128 * kv), kc[:, 2 * q + b, P * kv:P * kv + P])
                ins.then_inc(kc_ps, 1)
            for c in range(NCH):
                pe.wait_ge(w_in_sem[0][c], 48)
            for m in range(4):
                pe.wait_ge(proj_sb, 24 + m + 1)
                project(0, m, nT, proj_ps)
            pe.wait_ge(kc_sb, 4)
            for h in range(NH + NKV):
                pe.wait_ge(sq_done, h + 1)
                if h >= 2:
                    pe.wait_ge(rt_done, h - 1)
                pe.matmul(bk(4 + h % 2, T), ones, sq[:, h % 2, :], start=True, stop=True).then_inc(ss_ps, 1)
            for i, (t0, nt) in enumerate(TILES):
                for kv in range(NKV):
                    ins = turn(bank[6 + i // 2][0:nt, 256 * (i % 2) + P * kv:256 * (i % 2) + P * kv + P],
                               vT[:, kv, t0:t0 + nt])
            ins.then_inc(tok_ps, 1)
            pe.wait_ge(qk_ready, NH + NKV)
            pe.wait_ge(tok_sb, 2)
            for kv in range(NKV):
                turn(bank[7][:, 256 + P * kv:256 + P * kv + P], qkT[:, NH + kv, P:2 * P])
                ins = turn(bank[0][0:TS, P * kv:P * kv + P], qkT[:, NH + kv, TP:T])
            ins.then_inc(tok_ps, 1)
            pe.wait_ge(u_ready, 4 + CJ)
            for j in range(CJ):
                turn(bank[1 + j // 4][0:PAST, P * (j % 4):P * (j % 4) + P], up[:, j, TP:TP + PAST])
                if j == CJ // 2:
                    pe.wait_ge(tok_sb, 6)
                ins = turn(bank[3 - 3 * (j // 4)][0:TS, P * (j % 4):P * (j % 4) + P],
                           us[:, j, NB * PAST:])
            ins.then_inc(utok_ps, 1)

            pe.wait_ge(tok_sb, 6)

            def scores(u):
                if u >= 2:
                    pe.wait_ge(s_sb, u - 1)
                if u < 8:
                    n, kw = u // 4, P * (u // 4 + 1)
                    for j in range(2):
                        h = 2 * (u % 4) + j
                        ins = pe.matmul(bk(4 + u % 2, kw, at=kw * j), qkT[:, h, P * n:P * n + P],
                                        qkT[:, NH + h // GQA, 0:kw], start=True, stop=True)
                else:
                    for bb in range(4):
                        b = 4 * (u - 8) + bb
                        q = qs[:, b, :]
                        pe.matmul(bank[4 + u % 2][32 * bb:32 * bb + 32, 0:NKV * W], q, keysT[:, b, :],
                                  start=True, stop=True)
                        ins = pe.matmul(bank[4 + u % 2][32 * bb:32 * bb + 32, NKV * W:NKS], q,
                                        qkT[:, NH:NH + NKV, TP:T], start=True, stop=True)
                ins.then_inc(s_ps, 1)

            def turn_probs(u):
                pe.wait_ge(p_ready, u + 1)
                if u:
                    pe.wait_ge(pt_sb, u if u < 9 else 10)
                if u < 8:
                    nb = u // 4 + 1
                    for j in range(2 * nb):
                        ins = turn(bk(6, P, at=P * j), prob[:, u % 2, P * j:P * j + P])
                else:
                    for kv in range(NKV):
                        turn(bk(6, P, at=P * kv), probs[:, u % 2, W * kv:W * kv + W])
                        ins = turn(bank[6][0:TS, 256 + P * kv:256 + P * kv + P],
                                   probs[:, u % 2, NKV * W + TS * kv:NKV * W + TS * kv + TS])
                ins.then_inc(pt_ps, 1)

            def values(u):
                pe.wait_ge(pt_sb, u + 1 if u < 8 else 2 * u - 6)
                if u >= 1:
                    pe.wait_ge(o_sb, u)
                if u < 8:
                    n, nb = u // 4, u // 4 + 1
                    for j in range(2):
                        h = 2 * (u % 4) + j
                        for k in range(nb):
                            ins = pe.matmul(bk(7, P, at=P * j), vtok[:, k, HD * (h // GQA):HD * (h // GQA) + HD],
                                            PT[:, u % 2, P * (nb * j + k):P * (nb * j + k) + P],
                                            start=(k == 0), stop=(k == nb - 1))
                else:
                    pe.wait_ge(vc_in, 16)
                    for bb in range(4):
                        b = 4 * (u - 8) + bb
                        for kv in range(NKV):
                            pe.matmul(bk(7, 32, at=32 * bb), vc[:, b, HD * kv:HD * kv + HD],
                                      PTs[:, u % 2, P * kv + 32 * bb:P * kv + 32 * bb + 32], start=(kv == 0), stop=False)
                        for kv in range(NKV):
                            ins = pe.matmul(bk(7, 32, at=32 * bb), vtok[0:TS, 2, HD * kv:HD * kv + HD],
                                            PTs[0:TS, u % 2, 256 + P * kv + 32 * bb:256 + P * kv + 32 * bb + 32],
                                            start=False, stop=(kv == NKV - 1))
                ins.then_inc(o_ps, 1)

            pe.wait_ge(qk_ready, NH + NKV + 1)
            scores(0)
            for u in range(10):
                if u < 9:
                    scores(u + 1)
                turn_probs(u)
                values(u)

            pe.wait_ge(utok_sb, 4)
            pe.wait_ge(conv_done, CJ)
            for j in range(CJ):
                ins = pe.matmul(bk(2, T), ones, mixT[:, j, :], start=(j == 0), stop=(j == CJ - 1))
            ins.then_inc(ln_ps, 1)
            pe.wait_ge(ln_sq, 1)
            for j in range(CJ):
                ins = pe.matmul(bk(1, T), ones, lsq[:, j, :], start=(j == 0), stop=(j == CJ - 1))
            ins.then_inc(ln_ps, 1)
            pe.wait_ge(mix_ready, CJ)
            pe.wait_ge(o_sb, 10)
            pe.wait_ge(utok_sb, 4)

            def turn_back(g):
                pe.wait_ge(yT_sb, 4 * g + 4)
                if g:
                    pe.wait_ge(x1_part, 3 * g)
                for i, (t0, nt) in enumerate(TILES):
                    for j in range(4):
                        ins = turn(bank[4 + i][0:nt, P * j:P * j + P], yT[:, j, t0:t0 + nt])
                ins.then_inc(yt_ps, 1)

            for g in range(4):
                b = 1 + g % 2
                for c in range(NCH):
                    pe.wait_ge(w_in_sem[b][c], 16 * (3 + g // 2))
                for m in range(4):
                    if g:
                        pe.wait_ge(yT_sb, 4 * g + m - 3)
                    project(b, m, mixT, y_ps)
                turn_back(g)
            f = 0
            for i, (t0, nt) in enumerate(TILES):
                pe.wait_ge(h2_ready, i + 1)
                per = 512 // nt
                for q in range(KT // per):
                    if f >= 2:
                        pe.wait_ge(h2T_sb, f - 1)
                    else:
                        pe.wait_ge(x1_part, 12)
                    for k in range(per):
                        ins = turn(bk(4 + f % 2, nt, at=nt * k), h2[0:nt, i, P * (per * q + k):P * (per * q + k) + P])
                    ins.then_inc(h2T_ps, 1)
                    f += 1
            pe.wait_ge(h2T_sb, 9)
            pe.wait_ge(wr_in, 64)
            for i, (t0, nt) in enumerate(TILES):
                o = bank[6][0:nt, 64 * i:64 * i + NG + NE]
                for k in range(KT):
                    pe.matmul(o, h2T[:, k, t0:t0 + nt], wr3[:, k, :], start=(k == 0), stop=False)
                ins = pe.matmul(o, ones[0:1, 0:nt], rbias[0:1, :], start=False, stop=True)
            ins.then_inc(lg_ps, 1)
            pe.wait_ge(hot_ready, 1)
            for i, (t0, nt) in enumerate(TILES):
                o = bank[7][0:nt, NE * i:NE * i + NE]
                for j in range(i):
                    pe.matmul(o, ones[:, 0:nt], hot[:, j, :], start=(j == 0), stop=False)
                pe.matmul(o, tri[0:nt, 0:nt], hot[0:nt, i, :], start=(i == 0), stop=True)
            for i, (t0, nt) in enumerate(TILES):
                ins = pe.matmul(bank[7][:, 3 * NE:4 * NE], ones[0:nt, :], hot[0:nt, i, :], start=(i == 0), stop=(i == 2))
            ins.then_inc(rank_ps, 1)
            pe.wait_ge(tab_ready, 1)
            for j in range(2):
                ins = pe.matmul(bank[6][0:1, 256 + 64 * j:256 + 64 * j + NSTEP], tab[0:NSTEP, j:j + 1],
                                ident[0:NSTEP, 0:NSTEP], start=True, stop=True)
            ins.then_inc(tab_ps, 1)
            pe.wait_ge(pick_ready, 3)
            pe.wait_ge(steps_ready, 1)
            for k in range(KT):
                for half in range(2):
                    n = 2 * k + half
                    if n >= 8:
                        pe.wait_ge((xd_a, xd_v)[half], k - 3)
                    for i, (t0, nt) in enumerate(TILES):
                        ins = pe.matmul(bk(n % 8, T), h2[0:nt, i, P * k:P * k + P],
                                        pick[0:nt, i, T * half:T * half + T], start=(i == 0), stop=(i == 2))
                    ins.then_inc(xd_ps, 1)
            pe.wait_ge(xd_a, KT)
            pe.wait_ge(xd_v, KT)
            pe.wait_ge(pool_set, 4)
            n = step_count(pe)
            with pe.Fori(0, NSTEP) as s:
                with pe.If(s < n):
                    at = pe.value_load(steps_i[0:1, bass.ds(s + 64, 1)], min_val=0, max_val=NA)
                    for b in range(2):
                        done = (h1_ps, h3_ps)[b]
                        base = (3, 4)[b] * 16
                        w = view(wbuf[b], 0, KT, GC)
                        pe.wait_ge(hT_ready, s + 1)
                        for c in range(NCH):
                            pe.wait_ge(w_in_sem[b][c], base + 16 * s + 16)
                            for k in range(CK * c, CK * c + CK):
                                for m in range(4):
                                    ins = pe.matmul(bk(b, BLK, at=BLK * m), w[:, k, P * m:P * m + P],
                                                    xd[:, k, bass.ds(at, BLK)], start=(k == 0 and m == 0),
                                                    stop=(k == KT - 1), skip_group_check=True)
                            if c < NCH - 1:
                                ins.then_inc(w_free[b][c], 1)
                        ins.then_inc(done, 1)
                    pe.wait_ge(hT_ready, s + 2)
                    pe.wait_ge(ye_a, s + 1)
                    pe.wait_ge(ye_v, s + 1)
                    w = view(wbuf[2], 0, NCH, D)
                    for c in range(NCH):
                        pe.wait_ge(w_in_sem[2][c], 64 + 16 * s + 16)
                        for q in range(4):
                            half, part = q // 2, q % 2
                            ins = pe.matmul(bank[2 + part][BLK * half:BLK * half + BLK, :], hT[:, c, :],
                                            w[:, c, 512 * q:512 * q + 512], start=(c == 0), stop=(c == NCH - 1))
                        if c < NCH - 1:
                            ins.then_inc(w_free[2][c], 1)
                    ins.then_inc(ye_ps, 1)

        @block.vector
        def _(dve):
            dve.sem_inc(u_ready, 4)
            dve.sem_inc(hT_ready, 1)
            dve.sem_inc(ye_v, 1)
            count = [0]

            def link(ins):
                count[0] += 1
                ins.then_inc(dchain, 1)
                dve.wait_ge(dchain, count[0])

            def mul(out, a, b):
                return dve.tensor_tensor(out, a, b, ALU.mult)

            def add(out, a, b):
                return dve.tensor_tensor(out, a, b, ALU.add)

            for i, (t0, nt) in enumerate(TILES):
                dve.wait_ge(x_rstd, i + 1)
                link(dve.reciprocal(misc[0:nt, 13 + i:14 + i], misc[0:nt, 4 + i:5 + i]))
                dve.tensor_scalar(xn[0:nt, i, :], x3[0:nt, i, :], misc[0:nt, 13 + i:14 + i], None, ALU.mult
                                  ).then_inc(xn_ready, 1)
            dve.wait_ge(small_ps, 1)
            link(dve.tensor_copy(small[:, 0:26], bk(7, 26)))
            link(dve.tensor_copy(small[:, 32:], bk(7, CJ * CW + NH, at=32)))
            link(dve.tensor_scalar(small[:, 24:25], small[:, 24:25], SCALE, None, ALU.mult))
            dve.wait_ge(consts_in, 16)
            link(mul(misc[:, 40:48], sinks, hsel))
            dve.tensor_reduce(misc[:, 48:49], misc[:, 40:48], AX.X, ALU.add).then_inc(small_sb, 1)
            f = 0
            dve.wait_ge(g_in, 32)
            for i, (t0, nt) in enumerate(TILES):
                per = 512 // nt
                for q in range(KT // per):
                    dve.wait_ge(nT_ps, f + 1)
                    mul(nT[:, per * q:per * q + per, t0:t0 + nt], bk(4 + f % 2, per, nt),
                        g1[:, per * q:per * q + per].unsqueeze(2).to_broadcast([P, per, nt])).then_inc(nT_sb, 1)
                    f += 1

            dve.wait_ge(pool_set, 3)
            dve.wait_ge(st_sb, CJ)
            per_tile = 2 * CW
            with dve.Fori(0, 2) as i:
                with dve.Fori(0, 4) as m:
                    j = i * 4 + m
                    dve.wait_ge(proj_sb, 12 * i + 8 + m + 1)
                    a_t = aT[:, bass.ds(m, 1), :].rearrange("p o t -> p (o t)")
                    s_t = sgT[:, bass.ds(m, 1), :].rearrange("p o t -> p (o t)")
                    u_t = up[:, bass.ds(j, 1), :].rearrange("p o t -> p (o t)")
                    us_t = us[:, bass.ds(j, 1), :].rearrange("p o (r b) -> p (o r) b", b=NB)
                    mul(u_t[:, PAST:PAST + TP], a_t[:, 0:TP], s_t[:, 0:TP])
                    mul(us_t[:, PAST:, :], a_t[:, TP:T].rearrange("p (b r) -> p r b", b=NB),
                        s_t[:, TP:T].rearrange("p (b r) -> p r b", b=NB)).then_inc(u_ready, 1)
                    dve.wait_ge(u_ready, j + 5)
                    c_t = mixT[:, bass.ds(j, 1), :].rearrange("p o t -> p (o t)")
                    cs_t = c_t[:, TP:T].rearrange("p (b r) -> p r b", b=NB)
                    tap = taps[:, bass.ds(j, 1), :].rearrange("p o w -> p (o w)")
                    cb = convb[:, bass.ds(j, 1)]
                    base = j * per_tile
                    for w in range(CW):
                        pairs = ((c_t[:, 0:TP], u_t[:, w:w + TP]), (cs_t, us_t[:, w:w + TB, :]))
                        for q, (acc, src) in enumerate(pairs):
                            if w:
                                dve.wait_ge(cchain, base + 2 * w - 1 + q)
                                ins = dve.scalar_tensor_tensor(acc, src, tap[:, w:w + 1], acc, ALU.mult, ALU.add)
                            else:
                                ins = dve.tensor_scalar(acc, src, tap[:, 0:1], cb, ALU.mult, ALU.add)
                            ins.then_inc(cchain, 1)
                    dve.wait_ge(cchain, base + per_tile)
                    dve.sem_inc(conv_done, 1)

            for h in range(NH + NKV):
                dve.wait_ge(rt_done, h + 1)
                link(dve.reciprocal(rr[:, h % 2, :], rr[:, h % 2, :]))
                dve.scalar_tensor_tensor(qkT[:, h, :], qkT[:, h, :], qg if h < NH else kg, rr[:, h % 2, :],
                                         ALU.mult, ALU.mult).then_inc(qk_ready, 1)
            dve.wait_ge(qk_ready, NH + NKV)
            for b in range(NB):
                ins = dve.tensor_copy(qs[:, b, :].rearrange("p (h t) -> p h t", h=NH),
                                      qkT[:, 0:NH, TP + TB * b:TP + TB * b + TB])
            ins.then_inc(qk_ready, 1)
            dve.wait_ge(tok_ps, 2)
            dve.wait_ge(bias_in, 16)
            dve.wait_ge(tok_sb, 2)
            dve.wait_ge(rows_zero, 16 * (NSTEP * BLK // P))
            dve.tensor_copy(ktok[:, 0, :], bank[7][:, 256:512]).then_inc(tok_sb, 2)
            dve.tensor_copy(ktok[0:TS, 1, :], bank[0][0:TS, 0:256]).then_inc(tok_sb, 2)
            dve.wait_ge(utok_ps, 1)
            for g in range(2):
                dve.tensor_copy(utok[0:PAST, 0, 512 * g:512 * g + 512], bank[1 + g][0:PAST, :]).then_inc(utok_sb, 1)
                dve.tensor_copy(utok[0:TS, 1, 512 * g:512 * g + 512], bank[3 - 3 * g][0:TS, :]).then_inc(utok_sb, 1)

            def logits(u):
                k = 20 + 8 * (u % 2)
                m = misc[:, 50 + 2 * (u % 2):52 + 2 * (u % 2)]
                dve.wait_ge(s_ps, u + 1)
                if u >= 2:
                    dve.wait_ge(pt_ps, u - 1)
                if u < 8:
                    kw, w, h = P * (u // 4 + 1), 2, 2 * (u % 4)
                    v = prob[:, u % 2, 0:2 * kw].rearrange("p (h k) -> p h k", h=2)
                    src, tbl, sk = bk(4 + u % 2, 2, kw), abias[:, h:h + 2, 2 * P - kw:2 * P], sinks[:, h:h + 2]
                else:
                    w, v, sk = 1, probs[:, u % 2, :], misc[:, 48:49]
                    src, tbl = bk(4 + u % 2, NKS), sbias[:, u - 8, :]
                m = m[:, 0:w]
                add(v, src, tbl).then_inc(s_sb, 1)
                dve.wait_ge(s_sb, u + 1)
                link(dve.tensor_reduce(m, v, AX.X, ALU.max))
                link(dve.tensor_tensor(m, m, sk, ALU.max))
                link(dve.tensor_scalar(misc[:, k:k + w], m, -1.0, None, ALU.mult))
                dve.tensor_tensor(misc[:, k + 6:k + 6 + w], sk, m, ALU.subtract).then_inc(s_max, 1)

            def normalise(u):
                k, w = 20 + 8 * (u % 2), 2 if u < 8 else 1
                dve.wait_ge(p_exp, 3 * u + 3)
                den = misc[:, k + 2:k + 2 + w]
                link(add(den, den, misc[:, k + 4:k + 4 + w]))
                link(dve.reciprocal(den, den))
                if u < 8:
                    kw = P * (u // 4 + 1)
                    v = prob[:, u % 2, 0:2 * kw].rearrange("p (h k) -> p h k", h=2)
                    mul(v, v, den.unsqueeze(2).to_broadcast([P, 2, kw])).then_inc(p_ready, 1)
                else:
                    v = probs[:, u % 2, :]
                    dve.tensor_scalar(v, v, den, None, ALU.mult).then_inc(p_ready, 1)

            def heads_out(u):
                dve.wait_ge(o_ps, u + 1)
                if u < 8:
                    h = CJ + 2 * (u % 4)
                    dve.tensor_copy(mixT[:, h:h + 2, P * (u // 4):P * (u // 4) + P], bk(7, 2, P)).then_inc(o_sb, 1)
                else:
                    t0 = TP + 4 * TB * (u - 8)
                    for b in range(4):
                        ins = dve.tensor_copy(mixT[:, CJ:KT, t0 + TB * b:t0 + TB * b + TB], bk(7, NH, TB, at=32 * b))
                    ins.then_inc(o_sb, 1)

            logits(0)
            for u in range(10):
                if u < 9:
                    logits(u + 1)
                normalise(u)
                if u:
                    heads_out(u - 1)
            heads_out(9)

            dve.wait_ge(ln_ps, 1)
            link(dve.tensor_scalar(lmean, bk(2, T), 1.0 / DC, None, ALU.mult))
            dve.tensor_tensor(mixT[:, 0:CJ, :], mixT[:, 0:CJ, :], lmean.unsqueeze(1).to_broadcast([P, CJ, T]),
                              ALU.subtract).then_inc(ln_n, 1)
            dve.wait_ge(ln_rt, 1)
            link(dve.reciprocal(lrstd, lrstd))
            mul(mixT[:, 0:CJ, :], mixT[:, 0:CJ, :], lrstd.unsqueeze(1).to_broadcast([P, CJ, T])).then_inc(ln_n, 1)

            dve.wait_ge(x_again, 48)
            for g in range(4):
                dve.wait_ge(yt_ps, g + 1)
                for i, (t0, nt) in enumerate(TILES):
                    xs = x3[0:nt, i, 512 * g:512 * g + 512]
                    add(xs, xs, bank[4 + i][0:nt, :]).then_inc(x1_part, 1)
            for i, (t0, nt) in enumerate(TILES):
                dve.wait_ge(h2_rt, i + 1)
                ins = dve.reciprocal(misc[0:nt, 13 + i:14 + i], misc[0:nt, 10 + i:11 + i])
            ins.then_inc(h2_rec, 1)
            f = 0
            for i, (t0, nt) in enumerate(TILES):
                per = 512 // nt
                for q in range(KT // per):
                    dve.wait_ge(h2T_ps, f + 1)
                    mul(h2T[:, per * q:per * q + per, t0:t0 + nt], bk(4 + f % 2, per, nt),
                        g2[:, per * q:per * q + per].unsqueeze(2).to_broadcast([P, per, nt])).then_inc(h2T_sb, 1)
                    f += 1

            def over(i):
                return slice(0, TILES[i][1])

            link(dve.memset(reg[:, rt0:R_SIZE], 0.0))
            link(dve.memset(lg8[:, :, NG:], -3e38))
            dve.wait_ge(lg_ps, 1)
            for i in range(3):
                dve.tensor_copy(lg8[over(i), i, 0:NG], bank[6][over(i), 64 * i:64 * i + NG])
                link(dve.tensor_copy(le[over(i), i, :], bank[6][over(i), 64 * i + NG:64 * i + NG + NE]))
            for i in range(3):
                link(dve.max(mg[over(i), i, :], lg8[over(i), i, :]))
                link(dve.max_index(ui[over(i), 8 * i:8 * i + 8], mg[over(i), i, :], lg8[over(i), i, :]))
            link(dve.tensor_copy(gf, ui[:, 0:24].rearrange("p (i e) -> p i e", i=3)[:, :, 0]))
            link(dve.tensor_tensor(gone, row[:, 0:NG].unsqueeze(1).to_broadcast([P, 3, NG]),
                                   gf.unsqueeze(2).to_broadcast([P, 3, NG]), ALU.is_equal))
            for i in range(3):
                link(mul(prod[:, i, :].rearrange("p (g e) -> p g e", g=NG), le[:, i, :].rearrange("p (g e) -> p g e", g=NG),
                         gone[:, i, :].unsqueeze(2).to_broadcast([P, NG, EG])))
                link(dve.tensor_reduce(ein[:, i, :], prod[:, i, :].rearrange("p (g e) -> p e g", g=NG), AX.X, ALU.add))
                link(dve.max(me[over(i), i, :], ein[over(i), i, :]))
                link(dve.max_index(ui[over(i), 24 + 8 * i:32 + 8 * i], me[over(i), i, :], ein[over(i), i, :]))
            dg = expd.rearrange("p (i c) -> p i c", i=3)
            link(dve.tensor_tensor(dg[:, :, 0:NG], lg8[:, :, 0:NG], mg[:, :, 0:1].to_broadcast([P, 3, NG]), ALU.subtract))
            dve.tensor_tensor(dg[:, :, NG:NG + 1], me[:, :, 1:2], me[:, :, 0:1], ALU.subtract).then_inc(r_sub, 1)
            for e, c in ((e1, 0), (e2, 1)):
                link(dve.tensor_copy(e, ui[:, 24:48].rearrange("p (i e) -> p i e", i=3)[:, :, c]))
                link(dve.scalar_tensor_tensor(e, gf, float(EG), e, ALU.mult, ALU.add))
            for h, e in ((hot1, e1), (hot2, e2)):
                link(dve.tensor_tensor(h, row[:, 0:NE].unsqueeze(1).to_broadcast([P, 3, NE]),
                                       e.unsqueeze(2).to_broadcast([P, 3, NE]), ALU.is_equal))
            add(hot, hot1, hot2).then_inc(hot_ready, 1)
            dve.wait_ge(r_exp, 1)
            link(dve.tensor_reduce(gsum, dg[:, :, 0:NG], AX.X, ALU.add))
            link(dve.tensor_scalar(gate2, dg[:, :, NG], 1.0, None, ALU.add))
            link(mul(gsum, gsum, gate2))
            link(dve.reciprocal(gate1, gsum))
            link(mul(gate2, gate1, dg[:, :, NG]))
            dve.wait_ge(rank_ps, 1)
            link(dve.tensor_copy(cnt, bk(7, NE, at=3 * NE)))
            link(dve.tensor_tensor_scan(start, ones[:, 0:NE], cnt, 0.0, ALU.mult, ALU.add))
            link(dve.tensor_tensor(start, start, cnt, ALU.subtract))
            link(dve.tensor_scalar(nblk, cnt, 0.0, None, ALU.is_gt))
            for m in range(1, -(-T // BLK)):
                link(dve.scalar_tensor_tensor(nblk, cnt, float(m * BLK), nblk, ALU.is_gt, ALU.add))
            link(dve.tensor_scalar(nblk[:, 0:1], nblk[:, 0:1], 1.0, None, ALU.max))
            link(dve.tensor_tensor_scan(cum, ones[:, 0:NE], nblk, 0.0, ALU.mult, ALU.add))
            link(dve.tensor_tensor(sid, cum, nblk, ALU.subtract))
            link(dve.scalar_tensor_tensor(off, sid, -float(BLK), start, ALU.mult, ALU.add))
            cs = col[0:NSTEP]
            link(dve.tensor_scalar(tle[0:NSTEP], cum[0:NSTEP], cs, None, ALU.is_le))
            link(dve.tensor_scalar(tid[0:NSTEP], sid[0:NSTEP], cs, None, ALU.is_le))
            link(dve.tensor_reduce(tab[0:NSTEP, 0:1], tle[0:NSTEP], AX.X, ALU.add))
            link(dve.tensor_tensor(tid[0:NSTEP], tid[0:NSTEP], tle[0:NSTEP], ALU.subtract))
            link(mul(tid[0:NSTEP], tid[0:NSTEP], off[0:NSTEP]))
            link(dve.tensor_reduce(tab[0:NSTEP, 1:2], tid[0:NSTEP], AX.X, ALU.add))
            dve.scalar_tensor_tensor(tab[0:NSTEP, 1:2], cs, float(BLK), tab[0:NSTEP, 1:2], ALU.mult, ALU.add
                                     ).then_inc(tab_ready, 1)
            link(dve.tensor_copy(steps_i[0:1, 128:129], cum[0:1, NE - 1:NE]))
            for i in range(3):
                rank = bank[7][over(i), NE * i:NE * i + NE]
                add(xpos[over(i), i, :], rank, start[over(i)])
                link(dve.scalar_tensor_tensor(xslot[over(i), i, :], sid[over(i)], float(BLK), rank, ALU.mult, ALU.add))
            for c, h in enumerate((hot1, hot2)):
                for x, out in ((xpos, pos), (xslot, slot)):
                    link(mul(prod, x, h))
                    link(dve.tensor_reduce(out[:, :, c], prod, AX.X, ALU.add))
            for i in range(3):
                n = over(i)
                link(dve.tensor_scalar(pick[n, i, 0:NA], row[n, 0:NA], pos[n, i, 0:1], None, ALU.is_equal))
                dve.scalar_tensor_tensor(pick[n, i, 0:NA], row[n, 0:NA], pos[n, i, 1:2], pick[n, i, 0:NA],
                                         ALU.is_equal, ALU.add).then_inc(pick_ready, 1)
            dve.wait_ge(tab_ps, 1)
            link(dve.tensor_copy(steps_i[0:1, 0:NSTEP], bank[6][0:1, 256:256 + NSTEP]))
            dve.tensor_copy(steps_i[0:1, 64:64 + NSTEP], bank[6][0:1, 320:320 + NSTEP]).then_inc(steps_ready, 1)
            dve.wait_ge(steps_ready, 1)
            dve.tensor_copy(ui[:, 48:54], slot.rearrange("p i c -> p (i c)")).then_inc(slots_ready, 1)
            for k in range(KT):
                dve.wait_ge(xd_ps, 2 * k + 2)
                dve.tensor_scalar(xd[:, k, T:NA], bk(2 * (k % 4) + 1, T), g2[:, k:k + 1], None, ALU.mult).then_inc(xd_v, 1)

            n = step_count(dve)
            with dve.Fori(0, NSTEP) as s:
                with dve.If(s < n):
                    dve.wait_ge(h1_sb, s + 1)
                    dve.wait_ge(h3_ps, s + 1)
                    mul(hT.rearrange("p m t -> p (m t)"), h1s.rearrange("p m t -> p (m t)"), bk(1, 256)).then_inc(hT_ready, 1)
                    dve.wait_ge(ye_ps, s + 1)
                    dve.wait_ge(ye_out, 32 * s + 32)
                    dve.tensor_copy(ystage[:, 512:1024], bk(3, 512)).then_inc(ye_v, 1)
            for i in range(3):
                v = over(i)
                for c, gt in enumerate((gate1, gate2)):
                    dve.wait_ge(got_in[2 * i + c], 16)
                    ins = dve.scalar_tensor_tensor(x3[v, i, :], got[v, 2 * i + c, :], gt[v, i:i + 1], x3[v, i, :],
                                                   ALU.mult, ALU.add)
                    if c:
                        ins.then_inc(y_ready, 1)
                    else:
                        link(ins)


OUTS_MIX = 16 * (3 + 2 + 2 * NB + 1 + TB)

_INS = ["x_prompt", "x_sample", "state_conv", "cache_k", "cache_v", "norm1_g", "w_in", "conv_w", "conv_b",
        "conv_norm_g", "conv_norm_b", "q_norm_g", "k_norm_g", "attn_sinks", "w_out", "norm2_g",
        "w_router_group", "b_router_group", "w_router_expert", "b_router_expert", "w1", "w3", "w2"]
_SHAPES = {"x_prompt": (TP, D), "x_sample": (TS, D), "state_conv": (NB, PAST, DC), "cache_k": (NB, W, NKV * HD),
           "cache_v": (NB, W, NKV * HD)}
_OUTS = [((TP, D), (1, TP, D)), ((TS, D), (NB, TB, D)), ((PAST, DC), (1, 1, PAST, DC)),
         ((W, NKV * HD), (1, 1, W, NKV, HD)), ((W, NKV * HD), (1, 1, W, NKV, HD)),
         ((NB, PAST, DC), (1, NB, PAST, DC)), ((NB, W, NKV * HD), (1, NB, W, NKV, HD)),
         ((NB, W, NKV * HD), (1, NB, W, NKV, HD))]


def kernel(**inputs):
    import concourse.bacc as bacc
    from concourse.bass_utils import run_bass_kernel_spmd

    nc = bacc.Bacc("TRN2", target_bir_lowering=False, num_devices=1)
    arrays, args = {}, []
    for name in _INS:
        a = np.ascontiguousarray(inputs[name])
        a = a.reshape(_SHAPES.get(name, a.shape[1:]))
        arrays[f"in_{name}"] = a
        args.append(nc.dram_tensor(f"in_{name}", a.shape, F32, kind="ExternalInput").ap())
    for name, a in zip(("const_small", "const_attn"), shape_constants()):
        arrays[name] = a
        args.append(nc.dram_tensor(name, a.shape, F32, kind="ExternalInput").ap())
    for i, (shape, _) in enumerate(_OUTS):
        args.append(nc.dram_tensor(f"out_{i}", shape, F32, kind="ExternalOutput").ap())
    hybrid_layer(nc, *args)
    r = run_bass_kernel_spmd(nc, [arrays], core_ids=[0])
    return tuple(np.asarray(r.results[0][f"out_{i}"]).reshape(full) for i, (_, full) in enumerate(_OUTS))
```

```python
from contextlib import ExitStack

import concourse.bass as bass
import numpy as np
from concourse import mybir

F32 = mybir.dt.float32
I32 = mybir.dt.int32
U32 = mybir.dt.uint32
ALU = mybir.AluOpType
ACT = mybir.ActivationFunctionType
AX = mybir.AxisListType

P = 128
D = 2048
KT = D // P
DC = 1024
CJ = DC // P
CW = 31
PAST = CW - 1
NH, NKV, HD = 8, 2, 128
GQA = NH // NKV
W = 128
TP = 256
NB, TB = 8, 4
TS = NB * TB
T = TP + TS
TILES = [(0, P), (P, P), (TP, TS)]
NG, EG = 4, 8
NE = NG * EG
DE = 512
NA = 2 * T
BLK = 64
NSTEP = NE + NA // BLK - 1
XW = NA + BLK
GC = 512
CK = 4
NCH = KT // CK
EPS = 1e-6
SCALE = 1.0 / float(np.sqrt(HD))
MASKED = -1e30
FAR = 1e30
SLOPES = [2.0 ** (-8.0 * (h + 1) / NH) for h in range(NH)]
NONE = 8192
NKS = NKV * W + NKV * TS


def shape_constants():
    cs = np.zeros((P, C_SIZE), np.float32)
    cs[:, C_ID:C_ID + P] = np.eye(P)
    cs[:, C_ONE:C_ONE + P] = 1.0
    cs[:, C_TRI:C_TRI + P] = np.triu(np.ones((P, P)), 1)
    cs[:, C_ROW:C_ROW + NA] = np.arange(NA)
    cs[:, C_COL] = np.arange(P)
    rows = np.arange(P)
    cs[rows, C_HSEL + (rows % 32) // TB] = 1.0
    slope = SLOPES
    dist = np.arange(P)[:, None] + P - np.arange(2 * P)[None, :]
    ok = (dist >= 0) & (dist < W)
    cs[:, C_DIST:C_DIST + 2 * P] = np.where(ok, dist, FAR)
    sample = np.full((P, 2, NKS), MASKED)
    for r in range(P):
        h, t = (r % 32) // TB, r % TB
        kv = h // GQA
        for i in range(2):
            b = 4 * i + r // 32
            for c in range(W):
                if W + t - c < W:
                    sample[r, i, kv * W + c] = -slope[h] * (W + t - c)
            for u in range(t + 1):
                sample[r, i, NKV * W + kv * TS + TB * b + u] = -slope[h] * (t - u)
    cs[:, C_SAMP:C_SAMP + 2 * NKS] = sample.reshape(P, -1)
    return cs


C_ID, C_ONE, C_TRI = 0, P, 2 * P
C_ROW = 3 * P
C_COL = C_ROW + NA
C_HSEL = C_COL + 1
C_DIST = C_HSEL + NH
C_SAMP = C_DIST + 2 * P
C_SIZE = C_SAMP + 2 * NKS


def hybrid_layer(nc, x_prompt, x_sample, state_conv, cache_k, cache_v, norm1_g, w_in, conv_w, conv_b,
                 conv_norm_g, conv_norm_b, q_norm_g, k_norm_g, attn_sinks, w_out, norm2_g,
                 w_router_group, b_router_group, w_router_expert, b_router_expert, w1, w3, w2, const_small,
                 y_all, conv_prompt, k_prompt, v_prompt, conv_sample, k_sample, v_sample):
    with ExitStack() as ctx:
        def sem(name):
            return ctx.enter_context(nc.semaphore(name))

        def sb(name, n, dt=F32):
            return ctx.enter_context(nc.sbuf_tensor(name, [P, n], dt))

        wbuf = [sb(f"wbuf{b}", KT * GC) for b in range(3)]
        x_sb = sb("x_sb", 3 * D)
        cst = sb("cst", C_SIZE)
        small = sb("small", 32 + CJ * CW + NH)
        gains = sb("gains", 2 * KT)
        misc = sb("misc", 64)
        tmpc = sb("tmpc", 4 * TS)
        ui = sb("ui", 48, U32)
        idx_now = sb("idx_now", 1, U32)[:, :]
        steps_i = sb("steps_i", 2 * 64 + 1, I32)
        R_SIZE = 2 * KT * T + (NH + NKV) * T + CJ * (PAST + TP) + CJ * NB * (PAST + TB) + 8 * T + 1024
        reg = sb("reg", R_SIZE)

        def view(t, at, *dims):
            n = int(np.prod(dims))
            v = t[:, at:at + n]
            if len(dims) == 1:
                return v
            names = "abc"[:len(dims)]
            return v.rearrange(f"p ({' '.join(names)}) -> p {' '.join(names)}", **dict(zip(names, dims)))

        x3 = view(x_sb, 0, 3, D)
        ident = cst[:, C_ID:C_ID + P]
        ones = cst[:, C_ONE:C_ONE + P]
        tri = cst[:, C_TRI:C_TRI + P]
        row = cst[:, C_ROW:C_ROW + NA]
        col = cst[:, C_COL:C_COL + 1]
        hsel = cst[:, C_HSEL:C_HSEL + NH]
        dist = cst[:, C_DIST:C_DIST + 2 * P]
        sbias = view(cst, C_SAMP, 2, NKS)
        taps = view(small, 32, CJ, CW)
        sinks = small[:, 32 + CJ * CW:32 + CJ * CW + NH]
        convb, lng, lnb = (small[:, CJ * i:CJ * i + CJ] for i in range(3))
        qg, kg = small[:, 24:25], small[:, 25:26]
        g1, g2 = gains[:, 0:KT], gains[:, KT:2 * KT]
        o = 0
        nT = view(reg, o, KT, T)
        lsq = view(reg, o, CJ, T)
        lmean, lrstd = view(reg, o + CJ * T, T), view(reg, o + CJ * T + T, T)
        yT = view(reg, o, 8, T)
        o += KT * T
        mixT = view(reg, o, KT, T)
        xn = view(reg, o, 3, D)
        kc = view(reg, o, NB, NKV * HD)
        ktok = view(reg, o + 12 * T, 2, NKV * HD)
        o += KT * T
        qkT = view(reg, o, NH + NKV, T)
        utok = view(reg, o, 2, DC)
        o += (NH + NKV) * T
        up = view(reg, o, CJ, PAST + TP)
        o += CJ * (PAST + TP)
        us = view(reg, o, CJ, NB * (PAST + TB))
        rows_cw = reg[0:CW, o:o + DC]
        rows_vec = reg[0:26, o + DC:o + DC + P]
        row_sink = reg[0:1, o + DC + P:o + DC + P + NH]
        o += CJ * NB * (PAST + TB)
        state = view(reg, o, 2, DC)
        wr3 = view(reg, o, KT, NG + NE)
        rbias = reg[0:1, o + KT * (NG + NE):o + (KT + 1) * (NG + NE)]
        aT, sgT = view(reg, o, 2, T), view(reg, o + 2 * T, 2, T)
        o += 4 * T
        sq, rr = view(reg, o, 2, T), view(reg, o + 2 * T, 2, T)
        o += 4 * T
        prob = view(reg, o, 2, 512)
        vT = view(reg, o, NKV, T)
        o += 1024
        assert o == R_SIZE
        keysT = view(x_sb, 0, NB, NKV * W)
        vc = view(x_sb, 2048, NB, NKV * HD)
        vtok = view(x_sb, 4096, 3, NKV * HD)
        qs = view(x_sb, 4864, NB, NH * TB)
        PT = view(x_sb, 5120, 2, 512)
        h2 = view(reg, 0, 3, D)
        x1T = view(reg, 3 * D, KT, T)
        o = 3 * D + KT * T
        pick = view(reg, o, 3, XW)
        o += 3 * XW
        xw = view(reg, o, KT, BLK)
        o += KT * BLK
        ystage = reg[:, o:o + 1024]
        o += 1024
        h1s, hg, hT = reg[:, o:o + 256], reg[:, o + 256:o + 512], view(reg, o + 512, 2, 2, BLK)
        o += 768
        rt0 = o = 2 * KT * T + (NH + NKV) * T + CJ * (PAST + TP) + CJ * NB * (PAST + TB) + 4 * T
        at = [0]

        def part(*dims):
            at[0] += int(np.prod(dims))
            assert rt0 + at[0] <= R_SIZE
            return view(reg, rt0 + at[0] - int(np.prod(dims)), *dims)

        expd = part(15)
        lg8, mg = part(3, 8), part(3, 8)
        le, ein, me = part(3, NE), part(3, EG), part(3, 8)
        gf, e1, e2 = part(3), part(3), part(3)
        gone, prod = part(3, NG), part(3, NE)
        hot1, hot2, hot = part(3, NE), part(3, NE), part(3, NE)
        cnt, start, nblk, cum, sid, off = (part(NE) for _ in range(6))
        pos, rnk, blk, stp, tmp6 = (part(3, 2) for _ in range(5))
        tle, tid, tab = part(NE), part(NE), part(2)
        gsum, gates, tokid = part(3), part(3, 2), part(3)
        rbc = part(NG + NE)
        junk = view(reg, rt0 + at[0], 18, NE)
        ohr = part(2, P)
        ohs = part(2, 3 * NSTEP)
        gate_of, idx_f, half = part(NSTEP), part(NSTEP), part(1)
        idx_all = part(NSTEP).bitcast(U32)
        eps = misc[:, 0:1]
        sq_junk = view(reg, R_SIZE - 1024, 512)
        bank = [ctx.enter_context(nc.psum_tensor(f"bank{b}", [P, 512], F32)) for b in range(8)]

        def bk(b, *dims, at=0):
            return view(bank[b], at, *dims)

        consts_in, x_in, g_in, rows_in, state_in, kc_in, vc_in, wr_in, x_again, outs, k_out = (
            sem(n) for n in ("consts_in", "x_in", "g_in", "rows_in", "state_in", "kc_in", "vc_in",
                             "wr_in", "x_again", "outs", "k_out"))
        w_in_sem = [[sem(f"w_landed{b}{c}") for c in range(NCH)] for b in range(3)]
        w_free = [[sem(f"w_free{b}{c}") for c in range(NCH - 1)] for b in range(3)]
        pool_set = sem("pool_set")
        x_ms, x_rstd, xn_ready = sem("x_ms"), sem("x_rstd"), sem("xn_ready")
        small_ps, small_sb = sem("small_ps"), sem("small_sb")
        nT_ps, nT_sb, st_ps, st_sb = sem("nT_ps"), sem("nT_sb"), sem("st_ps"), sem("st_sb")
        kc_ps, kc_sb = sem("kc_ps"), sem("kc_sb")
        proj_ps, proj_sb, u_ready = sem("proj_ps"), sem("proj_sb"), sem("u_ready")
        conv_done, pool_conv = sem("conv_done"), sem("pool_conv")
        sq_done, ss_ps, rt_done, qk_ready = sem("sq_done"), sem("ss_ps"), sem("rt_done"), sem("qk_ready")
        v_ps, v_sb, ktok_ps, ktok_sb = sem("v_ps"), sem("v_sb"), sem("ktok_ps"), sem("ktok_sb")
        utok_ps, utok_sb = sem("utok_ps"), sem("utok_sb")
        s_ps, s_sb, s_max, p_exp, p_ready = sem("s_ps"), sem("s_sb"), sem("s_max"), sem("p_exp"), sem("p_ready")
        pt_ps, pt_sb, o_ps, o_sb = sem("pt_ps"), sem("pt_sb"), sem("o_ps"), sem("o_sb")
        ln_ps, ln_sq, ln_rt, ln_n, mix_ready = sem("ln_ps"), sem("ln_sq"), sem("ln_rt"), sem("ln_n"), sem("mix_ready")
        y_ps, yT_sb, yt_ps, x1_part = sem("y_ps"), sem("yT_sb"), sem("yt_ps"), sem("x1_part")
        h2_ms, h2_sum, h2_rt, h2_rec, h2_ready = (sem(n) for n in ("h2_ms", "h2_sum", "h2_rt", "h2_rec", "h2_ready"))
        x1T_ps, x1T_sb, lg_ps, r_sub, r_exp = sem("x1T_ps"), sem("x1T_sb"), sem("lg_ps"), sem("r_sub"), sem("r_exp")
        hot_ready, rank_ps, pick_ready, tab_ready, tab_ps, steps_ready = (
            sem(n) for n in ("hot_ready", "rank_ps", "pick_ready", "tab_ready", "tab_ps", "steps_ready"))
        ohs_ready, rows_ps, rows_ready = sem("ohs_ready"), sem("rows_ps"), sem("rows_ready")
        x1_stored = sem("x1_stored")
        xw_ps, xw_a, xw_v = sem("xw_ps"), sem("xw_a"), sem("xw_v")
        h1_ps, h3_ps, h1_sb, hT_ready, ye_ps, ye_a, ye_v, ye_out, idx_set = (
            sem(n) for n in ("h1_ps", "h3_ps", "h1_sb", "hT_ready", "ye_ps", "ye_a", "ye_v", "ye_out", "idx_set"))
        pool_go, ye_free, hg_ready, hT_ps = sem("pool_go"), sem("ye_free"), sem("hg_ready"), sem("hT_ps")
        dchain, cchain, pchain = sem("vector_chain"), sem("conv_chain"), sem("pool_chain")

        block = ctx.enter_context(nc.Block())

        def step_count(eng):
            return eng.value_load(steps_i[0:1, 128:129], min_val=1, max_val=NSTEP)

        GROUPS = [3072, 2048, 2560, 0, 1024, 512, 1536]
        TILE = [(0, m) for m in range(4)] + [(1 + i, m) for i in range(2) for m in range(4)]
        TILE += [(3 + 2 * i + g, m) for i in range(2) for m in range(4) for g in range(2)]
        LAST = [max(n for n, (g, _) in enumerate(TILE) if g == k) for k in range(len(GROUPS))]

        @block.sync
        def _(sp):
            def group(b, src, first):
                for c in range(NCH):
                    sp.dma_start(view(wbuf[b], c * CK * GC, CK, GC), src(c, first)).then_inc(w_in_sem[b][c], 16)

            def in_cols(c, first):
                return w_in.rearrange("(p k) n -> p k n", k=KT)[:, CK * c:CK * c + CK, first:first + GC]

            def out_cols(c, first):
                return w_out.rearrange("(k p) n -> p k n", p=P)[:, CK * c:CK * c + CK, first:first + GC]

            sp.wait_ge(x_in, 48)
            for k, first in enumerate(GROUPS):
                if k >= 3:
                    sp.wait_ge(proj_ps, LAST[k - 3] + 1)
                group(k % 3, in_cols, first)
            for b in (1, 2):
                sp.wait_ge(proj_ps, LAST[3 + b] + 1)
                group(b, out_cols, GC * (b - 1))

            def expert(b, e, free):
                for c in range(NCH):
                    free(c)
                    if b < 2:
                        src = (w1, w3)[b][bass.ds(e, 1)].rearrange("o (p k) n -> p (o k n)", k=KT)
                        src = src[:, CK * GC * c:CK * GC * c + CK * GC]
                    else:
                        src = w2[bass.ds(e, 1)].rearrange("o (c p) n -> p (o c) n", p=P)[:, c, :]
                    sp.dma_start(view(wbuf[b], c * CK * GC, CK * GC), src).then_inc(w_in_sem[b][c], 16)

            sp.wait_ge(proj_ps, 28)
            expert(0, 0, lambda c: None)
            for b in (1, 2):
                sp.wait_ge(y_ps, 4 * b)
                group(b, out_cols, GC * (b + 1))
            for b in (1, 2):
                sp.wait_ge(y_ps, 8 + 4 * b)
                expert(b, 0, lambda c: None)
            sp.wait_ge(steps_ready, 1)
            n = step_count(sp)
            with sp.Fori(1, NSTEP) as s:
                with sp.If(s < n):
                    e = sp.value_load(steps_i[0:1, bass.ds(s, 1)], min_val=0, max_val=NE - 1)
                    for b in range(3):
                        expert(b, e, lambda c: sp.wait_ge(w_free[b][c] if c < NCH - 1 else (h1_ps, h3_ps, ye_ps)[b], s))

        @block.gpsimd
        def _(pool):
            pool.memset(misc[:, 1:64], 0.0).then_inc(pool_set, 1)
            pool.memset(eps, EPS).then_inc(pool_set, 1)
            pool.memset(up[:, :, 0:PAST], 0.0).then_inc(pool_set, 1)
            pool.wait_ge(u_ready, 4 + 2)
            pool.wait_ge(k_out, KV_OUT)
            acc = mixT[:, 0:4, TP:T].rearrange("p j (b t) -> p j t b", b=NB)
            tmp = tmpc[:, :].rearrange("p (j t b) -> p j t b", j=4, t=TB)
            v = us[:, 0:4, :].rearrange("p j (r b) -> p j r b", b=NB)
            shape = [P, TB, NB]
            n = 0
            for w in range(CW):
                for j in range(4):
                    if w == 0 and j:
                        pool.wait_ge(u_ready, 4 + j + 1)
                    pool.tensor_scalar(tmp[:, j] if w else acc[:, j], v[:, j, w:w + TB, :], taps[:, j, w:w + 1],
                                       None if w else convb[:, j:j + 1], ALU.mult, ALU.bypass if w else ALU.add
                                       ).then_inc(pchain, 1)
                n += 4
                pool.wait_ge(pchain, n)
                if w:
                    pool.tensor_tensor(acc, acc, tmp, ALU.add).then_inc(pchain, 1)
                    n += 1
                    pool.wait_ge(pchain, n)
            pool.sem_inc(pool_conv, 1)
            y_rows = y_all.rearrange("t (h c) -> (t h) c", h=2)
            pool.wait_ge(x1_stored, 48)
            pool.wait_ge(rows_ready, 1)
            n = step_count(pool)
            with pool.Fori(0, NSTEP) as s:
                with pool.If(s < n):
                    pool.tensor_copy(idx_now, idx_all[:, bass.ds(s, 1)]).then_inc(idx_set, 1)
                    pool.wait_ge(idx_set, s + 1)
                    pool.sem_inc(pool_go, 1)
                    pool.wait_ge(ye_a, s + 2)
                    pool.sem_inc(pool_go, 1)
                    pool.wait_ge(ye_v, s + 2)
                    pool.sem_inc(pool_go, 1)
                    pool.indirect_dma_start(y_rows, bass.IndirectOffsetOnAxis(ap=idx_now, axis=0), ystage, None,
                                            bounds_check=2 * T - 1, oob_is_err=False, compute_op=ALU.add
                                            ).then_inc(ye_out, 16)
                    pool.wait_ge(ye_out, 16 * s + 16)
                    pool.sem_inc(ye_free, 1)

        @block.scalar
        def _(act):
            act.sem_inc(proj_sb, 4)
            act.sem_inc(ye_a, 1)
            act.sem_inc(xw_a, 1)
            act.sem_inc(ye_free, 1)
            act.dma_start(x3[:, 0, :], x_prompt[0:P, :]).then_inc(x_in, 16)
            act.dma_start(x3[:, 1, :], x_prompt[P:TP, :]).then_inc(x_in, 16)
            act.dma_start(x3[0:TS, 2, :], x_sample).then_inc(x_in, 16)
            act.dma_start(cst[:, :], const_small).then_inc(consts_in, 16)
            act.dma_start(g1, norm1_g.rearrange("(p k) -> p k", k=KT)).then_inc(g_in, 16)
            act.dma_start(g2, norm2_g.rearrange("(p k) -> p k", k=KT)).then_inc(g_in, 16)
            act.dma_start(rows_cw, conv_w).then_inc(rows_in, 16)
            for i, v in enumerate((conv_b, conv_norm_g, conv_norm_b)):
                act.dma_start(rows_vec[CJ * i:CJ * i + CJ, :], v.rearrange("(j p) -> j p", p=P)).then_inc(rows_in, 16)
            for i, v in enumerate((q_norm_g, k_norm_g)):
                act.dma_start(rows_vec[24 + i:25 + i, :], v.rearrange("(o p) -> o p", o=1)).then_inc(rows_in, 16)
            act.dma_start(row_sink, attn_sinks.rearrange("(o h) -> o h", o=1)).then_inc(rows_in, 16)
            act.dma_start(state[0:4 * PAST, :, :], state_conv.rearrange("(i b) r c -> (b r) i c", i=2)
                          ).then_inc(state_in, 16)

            act.wait_ge(x_in, 48)
            act.wait_ge(pool_set, 2)
            for i, (t0, nt) in enumerate(TILES):
                act.activation(xn[0:nt, i, :], x3[0:nt, i, :], ACT.Square, accum_out=misc[0:nt, 1 + i:2 + i]
                               ).then_inc(x_ms, 1)
            act.wait_ge(x_ms, 3)
            for i, (t0, nt) in enumerate(TILES):
                act.activation(misc[0:nt, 4 + i:5 + i], misc[0:nt, 1 + i:2 + i], ACT.Sqrt, bias=eps[0:nt],
                               scale=1.0 / D).then_inc(x_rstd, 1)
            for j in range(CJ):
                act.wait_ge(st_ps, j // 2 + 1)
                act.wait_ge(small_sb, 1)
                act.activation(us[:, j, 0:NB * PAST].rearrange("p (r b) -> p b r", b=NB),
                               bk(j // 2, 2, NB, PAST)[:, j % 2], ACT.Copy).then_inc(st_sb, 1)
            act.wait_ge(nT_ps, 9)
            act.dma_start(kc, cache_k.rearrange("b s c -> s b c")).then_inc(kc_in, 16)
            act.wait_ge(xn_ready, 3)
            act.dma_start(vc, cache_v.rearrange("b s c -> s b c")).then_inc(vc_in, 16)
            act.dma_start(k_sample[:, 0:W - TB, :], cache_k[:, TB:W, :]).then_inc(outs, 16)
            act.dma_start(v_sample[:, 0:W - TB, :], cache_v[:, TB:W, :]).then_inc(outs, 16)
            act.dma_start(conv_sample[:, 0:PAST - TB, :], state_conv[:, TB:PAST, :]).then_inc(outs, 16)

            def norm_root(r):
                act.wait_ge(ss_ps, r + 1)
                if r >= 2:
                    act.wait_ge(qk_ready, r - 1)
                act.activation(rr[:, r % 2, :], bk(4 + r % 2, T), ACT.Sqrt, bias=eps, scale=1.0 / HD
                               ).then_inc(rt_done, 1)

            def square(r):
                if r >= 2:
                    act.wait_ge(ss_ps, r - 1)
                act.activation(sq[:, r % 2, :], qkT[:, NORM_ORDER[r], :], ACT.Square).then_inc(sq_done, 1)

            def exps(u):
                act.wait_ge(s_max, u + 1)
                k, w = 20 + 8 * (u % 2), 2 if u < 8 else 1
                n = P * (u // 4 + 1) if u < 8 else NKS
                for j in range(w):
                    v = prob[:, u % 2, n * j:n * j + n]
                    act.activation(v, v, ACT.Exp, bias=misc[:, k + j:k + j + 1],
                                   accum_out=misc[:, k + 2 + j:k + 3 + j]).then_inc(p_exp, 2 // w)
                act.activation(misc[:, k + 4:k + 4 + w], misc[:, k + 6:k + 6 + w], ACT.Exp).then_inc(p_exp, 1)

            def probs_out(u):
                act.wait_ge(pt_ps, u + 1)
                if u >= 2:
                    act.wait_ge(o_ps, u - 1)
                if u < 8:
                    n = 256 * (u // 4 + 1)
                    act.activation(PT[:, u % 2, 0:n], bk(6, 512)[:, 0:n], ACT.Copy).then_inc(pt_sb, 2)
                else:
                    act.activation(PT[:, u % 2, 0:256], bk(6, 512)[:, 0:256], ACT.Copy).then_inc(pt_sb, 1)
                    act.activation(PT[0:TS, u % 2, 256:512], bank[6][0:TS, 256:512], ACT.Copy).then_inc(pt_sb, 1)

            for n in range(28):
                act.wait_ge(proj_ps, n + 1)
                src = bk(n % 4, T)
                if n < 2:
                    act.activation(qkT[:, NH + n, :], src, ACT.Copy).then_inc(proj_sb, 1)
                elif n < 4:
                    act.activation(vT[:, n - 2, :], src, ACT.Copy).then_inc(proj_sb, 1)
                elif n < 12:
                    act.activation(qkT[:, n - 4, :], src, ACT.Copy).then_inc(proj_sb, 1)
                else:
                    j = (n - 12) // 2
                    if j >= 2 and n % 2 == 0:
                        act.wait_ge(u_ready, 4 + j - 1)
                    if n == 12:
                        act.wait_ge(st_ps, 4)
                    act.activation((aT, sgT)[n % 2][:, j % 2, :], src, ACT.Copy if n % 2 == 0 else ACT.Sigmoid
                                   ).then_inc(proj_sb, 1)
                if n in NORM_AT:
                    r = NORM_AT.index(n)
                    act.wait_ge(proj_sb, n + 5)
                    square(r)
                if n - 1 in NORM_AT:
                    norm_root(NORM_AT.index(n - 1))
                if n == 4:
                    act.wait_ge(v_ps, 1)
                    act.activation(vtok[:, 0:2, :].rearrange("p i c -> p (i c)"), bk(6, 512), ACT.Copy).then_inc(v_sb, 1)
                    act.activation(vtok[0:TS, 2, :], bank[7][0:TS, 0:256], ACT.Copy).then_inc(v_sb, 1)
                if n == 6:
                    act.wait_ge(ktok_sb, 2)
                    act.wait_ge(v_sb, 2)
                    act.dma_start(k_prompt, ktok[:, 0, :]).then_inc(k_out, 16)
                    act.dma_start(v_prompt, vtok[:, 1, :]).then_inc(k_out, 16)
                    for b in range(NB):
                        act.dma_start(k_sample[b, W - TB:W, :], ktok[TB * b:TB * b + TB, 1, :]).then_inc(k_out, 16)
                        act.dma_start(v_sample[b, W - TB:W, :], vtok[TB * b:TB * b + TB, 2, :]).then_inc(k_out, 16)
                if 13 <= n < 23:
                    exps(n - 13)
                if 15 <= n < 25:
                    probs_out(n - 15)
            act.wait_ge(u_ready, 4 + CJ)
            act.wait_ge(o_ps, 10)
            act.dma_start(wr3[:, :, 0:NG], w_router_group.rearrange("(p k) g -> p k g", k=KT)).then_inc(wr_in, 16)
            act.dma_start(wr3[:, :, NG:], w_router_expert.rearrange("(p k) g -> p k g", k=KT)).then_inc(wr_in, 16)
            act.dma_start(rbias[:, 0:NG], b_router_group.rearrange("(o g) -> o g", o=1)).then_inc(wr_in, 16)
            act.dma_start(rbias[:, NG:], b_router_expert.rearrange("(o g) -> o g", o=1)).then_inc(wr_in, 16)
            act.dma_start(x3[:, 0, :], x_prompt[0:P, :]).then_inc(x_again, 16)
            act.dma_start(x3[:, 1, :], x_prompt[P:TP, :]).then_inc(x_again, 16)
            act.dma_start(x3[0:TS, 2, :], x_sample).then_inc(x_again, 16)
            act.wait_ge(utok_sb, 4)
            act.dma_start(conv_prompt, utok[0:PAST, 0, :]).then_inc(outs, 16)
            for t in range(TB):
                act.dma_start(conv_sample[:, PAST - TB + t, :], utok[NB * t:NB * t + NB, 1, :]).then_inc(outs, 16)

            act.wait_ge(ln_n, 1)
            act.activation(lsq.rearrange("p j t -> p (j t)"), mixT[:, 0:CJ, :].rearrange("p j t -> p (j t)"), ACT.Square
                           ).then_inc(ln_sq, 1)
            act.wait_ge(ln_ps, 2)
            act.activation(lrstd, bk(7, T), ACT.Sqrt, bias=eps, scale=1.0 / DC).then_inc(ln_rt, 1)
            for j in range(CJ):
                act.wait_ge(ln_n, 2 + j // 4)
                act.activation(mixT[:, j, :], mixT[:, j, :], ACT.Silu, bias=lnb[:, j:j + 1], scale=lng[:, j:j + 1]
                               ).then_inc(mix_ready, 1)
            def yT_out(m):
                act.wait_ge(y_ps, m + 1)
                if m % 4 == 0 and m >= 8:
                    act.wait_ge(yt_ps, m // 4 - 1)
                act.activation(yT[:, m % 8, :], bk(Y_BANK[m], T), ACT.Copy).then_inc(yT_sb, 1)

            def partial_squares(g):
                for i, (t0, nt) in enumerate(TILES):
                    act.wait_ge(x1_part, 3 * g + i + 1)
                    if g or i:
                        act.wait_ge(h2_ms, 3 * g + i)
                    act.activation(sq_junk[0:nt, :], x3[0:nt, i, 512 * g:512 * g + 512], ACT.Square,
                                   accum_out=misc[0:nt, 50 + 4 * i + g:51 + 4 * i + g]).then_inc(h2_ms, 1)

            for m in range(KT):
                yT_out(m)
                if m >= 6 and m % 4 == 2:
                    partial_squares((m - 6) // 4)
            partial_squares(3)
            act.wait_ge(h2_sum, 1)
            act.activation(misc[:, 10:13], misc[:, 7:10], ACT.Sqrt, bias=eps, scale=1.0 / D).then_inc(h2_rt, 1)
            act.wait_ge(h2_rec, 1)
            act.wait_ge(outs, OUTS_MIX)
            for i, (t0, nt) in enumerate(TILES):
                act.wait_ge(x1_part, 12)
                act.dma_start(y_all[t0:t0 + nt, :], x3[0:nt, i, :]).then_inc(x1_stored, 16)
            for i, (t0, nt) in enumerate(TILES):
                act.activation(h2[0:nt, i, :].rearrange("t (k p) -> t k p", k=KT),
                               x3[0:nt, i, :].rearrange("t (p k) -> t k p", k=KT), ACT.Copy,
                               scale=misc[0:nt, 13 + i:14 + i]).then_inc(h2_ready, 1)
            act.wait_ge(r_sub, 1)
            act.activation(expd, expd, ACT.Exp).then_inc(r_exp, 1)

            act.wait_ge(rows_ready, 1)
            n = step_count(act)
            with act.Fori(0, NSTEP) as s:
                with act.If(s < n):
                    act.wait_ge(h1_ps, s + 1)
                    act.wait_ge(hg_ready, s + 1)
                    act.activation(h1s, bk(0, 256), ACT.Silu).then_inc(h1_sb, 1)
                    act.wait_ge(ye_ps, s + 1)
                    act.wait_ge(ye_free, s + 1)
                    act.activation(ystage[:, 0:512], bk(2, 512), ACT.Copy, scale=gate_of[:, bass.ds(s, 1)]
                                   ).then_inc(ye_a, 1)
            act.wait_ge(k_out, KV_OUT)

        @block.tensor
        def _(pe):
            def turn(out, in_):
                k = in_.shape[0]
                return pe.transpose(out, in_, ident[0:k, 0:k])

            pe.wait_ge(consts_in, 16)
            f = 0
            for i, (t0, nt) in enumerate(TILES):
                pe.wait_ge(xn_ready, i + 1)
                per = 512 // nt
                for q in range(KT // per):
                    if f >= 2:
                        pe.wait_ge(nT_sb, f - 1)
                    for k in range(per):
                        ins = turn(bk(4 + f % 2, nt, at=nt * k),
                                   xn[0:nt, i, :].rearrange("t (p k) -> t k p", k=KT)[:, per * q + k, :])
                    ins.then_inc(nT_ps, 1)
                    f += 1
            pe.wait_ge(rows_in, 16 * 7)
            turn(bk(7, 26), rows_vec)
            for j in range(CJ):
                turn(bk(7, CW, at=32 + CW * j), rows_cw[:, P * j:P * j + P])
            pe.matmul(bk(7, NH, at=32 + CJ * CW), ones[0:1, :], row_sink, start=True, stop=True).then_inc(small_ps, 1)
            pe.wait_ge(state_in, 16)
            for j in range(CJ):
                for i in range(2):
                    ins = turn(bk(j // 2, 4 * PAST, at=8 * PAST * (j % 2) + 4 * PAST * i),
                               state[0:4 * PAST, i, P * j:P * j + P])
                if j % 2:
                    ins.then_inc(st_ps, 1)

            def project(b, m, out, rhs, done):
                w = view(wbuf[b], 0, KT, GC)
                for k in range(KT):
                    ins = pe.matmul(bk(out, T), w[:, k, P * m:P * m + P], rhs[:, k, :], start=(k == 0),
                                    stop=(k == KT - 1))
                ins.then_inc(done, 1)

            def scores(u):
                if u >= 2:
                    pe.wait_ge(s_sb, u - 1)
                else:
                    pe.wait_ge(rt_done, NH + NKV)
                    pe.wait_ge(kc_sb, 4)
                if u < 8:
                    pe.wait_ge(qk_ready, 4 + 2 * (u % 4))
                    n, kw = u // 4, P * (u // 4 + 1)
                    for j in range(2):
                        h = 2 * (u % 4) + j
                        ins = pe.matmul(bk(4 + u % 2, kw, at=kw * j), qkT[:, h, P * n:P * n + P],
                                        qkT[:, NH + h // GQA, 0:kw], start=True, stop=True)
                else:
                    pe.wait_ge(qk_ready, NH + NKV + 1)
                    for bb in range(4):
                        q = qs[:, 4 * (u - 8) + bb, :]
                        pe.matmul(bank[4 + u % 2][32 * bb:32 * bb + 32, 0:NKV * W], q, keysT[:, 4 * (u - 8) + bb, :],
                                  start=True, stop=True)
                        ins = pe.matmul(bank[4 + u % 2][32 * bb:32 * bb + 32, NKV * W:NKS], q,
                                        qkT[:, NH:NH + NKV, TP:T], start=True, stop=True)
                ins.then_inc(s_ps, 1)

            def turn_probs(u):
                pe.wait_ge(p_ready, u + 1)
                if u:
                    pe.wait_ge(pt_sb, 2 * u)
                else:
                    pe.wait_ge(ktok_sb, 2)
                    pe.wait_ge(v_sb, 2)
                    pe.wait_ge(kc_sb, 4)
                if u < 8:
                    for j in range(2 * (u // 4 + 1)):
                        ins = turn(bk(6, P, at=P * j), prob[:, u % 2, P * j:P * j + P])
                else:
                    for kv in range(NKV):
                        turn(bk(6, P, at=P * kv), prob[:, u % 2, W * kv:W * kv + W])
                        ins = turn(bank[6][0:TS, 256 + P * kv:256 + P * kv + P],
                                   prob[:, u % 2, NKV * W + TS * kv:NKV * W + TS * kv + TS])
                ins.then_inc(pt_ps, 1)

            def values(u):
                pe.wait_ge(pt_sb, 2 * u + 2)
                if u >= 1:
                    pe.wait_ge(o_sb, u)
                if u < 8:
                    nb = u // 4 + 1
                    for j in range(2):
                        h = 2 * (u % 4) + j
                        for k in range(nb):
                            ins = pe.matmul(bk(7, P, at=P * j), vtok[:, k, HD * (h // GQA):HD * (h // GQA) + HD],
                                            PT[:, u % 2, P * (nb * j + k):P * (nb * j + k) + P],
                                            start=(k == 0), stop=(k == nb - 1))
                else:
                    pe.wait_ge(vc_in, 16)
                    for bb in range(4):
                        b = 4 * (u - 8) + bb
                        for kv in range(NKV):
                            pe.matmul(bk(7, 32, at=32 * bb), vc[:, b, HD * kv:HD * kv + HD],
                                      PT[:, u % 2, P * kv + 32 * bb:P * kv + 32 * bb + 32], start=(kv == 0), stop=False)
                        for kv in range(NKV):
                            ins = pe.matmul(bk(7, 32, at=32 * bb), vtok[0:TS, 2, HD * kv:HD * kv + HD],
                                            PT[0:TS, u % 2, 256 + P * kv + 32 * bb:256 + P * kv + 32 * bb + 32],
                                            start=False, stop=(kv == NKV - 1))
                ins.then_inc(o_ps, 1)

            pe.wait_ge(nT_sb, 9)
            pe.wait_ge(st_sb, CJ)
            pe.wait_ge(small_sb, 1)
            for n, (g, m) in enumerate(TILE):
                if m == 0:
                    for c in range(NCH):
                        pe.wait_ge(w_in_sem[g % 3][c], 16 * (g // 3 + 1))
                pe.wait_ge(proj_sb, n + 1)
                project(g % 3, m, n % 4, nT, proj_ps)
                if n - 1 in NORM_AT:
                    r = NORM_AT.index(n - 1)
                    pe.wait_ge(sq_done, r + 1)
                    if r >= 2:
                        pe.wait_ge(rt_done, r - 1)
                    pe.matmul(bk(4 + r % 2, T), ones, sq[:, r % 2, :], start=True, stop=True).then_inc(ss_ps, 1)
                if n == 3:
                    pe.wait_ge(proj_sb, 4 + 4)
                    for i, (t0, nt) in enumerate(TILES):
                        for kv in range(NKV):
                            ins = turn(bank[6 + i // 2][0:nt, 256 * (i % 2) + P * kv:256 * (i % 2) + P * kv + P],
                                       vT[:, kv, t0:t0 + nt])
                    ins.then_inc(v_ps, 1)
                if n == 5:
                    pe.wait_ge(qk_ready, 2)
                    pe.wait_ge(v_sb, 2)
                    for kv in range(NKV):
                        turn(bank[6][:, P * kv:P * kv + P], qkT[:, NH + kv, P:2 * P])
                        ins = turn(bank[6][0:TS, 256 + P * kv:256 + P * kv + P], qkT[:, NH + kv, TP:T])
                    ins.then_inc(ktok_ps, 1)
                if n in (7, 9):
                    q0 = n - 7
                    if n == 7:
                        pe.wait_ge(kc_in, 16)
                        pe.wait_ge(ktok_sb, 2)
                    else:
                        pe.wait_ge(kc_sb, 2)
                    for q in (q0, q0 + 1):
                        for b in range(2):
                            for kv in range(NKV):
                                ins = turn(bk(6 + q % 2, P, at=256 * b + 128 * kv), kc[:, 2 * q + b, P * kv:P * kv + P])
                        ins.then_inc(kc_ps, 1)
                if 12 <= n < 22:
                    scores(n - 12)
                if 14 <= n < 24:
                    turn_probs(n - 14)
                if 15 <= n < 25:
                    values(n - 15)

            def out_tile(m, ks, done=None):
                g = m // 4
                b = 1 + g % 2
                if m % 4 == 0:
                    for c in range(NCH):
                        pe.wait_ge(w_in_sem[b][c], 16 * ((3, 3, 4, 4)[g]))
                w = view(wbuf[b], 0, KT, GC)
                for k in ks:
                    ins = pe.matmul(bk(Y_BANK[m], T), w[:, k, P * (m % 4):P * (m % 4) + P], mixT[:, k, :],
                                    start=(k == (CJ if m < 6 else 0)), stop=(done is not None and k == ks[-1]),
                                    skip_group_check=(m < 6))
                if done is not None:
                    ins.then_inc(done, 1)

            pe.wait_ge(o_sb, 10)
            pe.wait_ge(proj_sb, 32)
            for m in range(4):
                out_tile(m, range(CJ, KT))
            pe.wait_ge(u_ready, 4 + CJ)
            for j in range(CJ):
                turn(bank[4 + j // 4][0:PAST, P * (j % 4):P * (j % 4) + P], up[:, j, TP:TP + PAST])
                ins = turn(bank[6 + j // 4][0:TS, P * (j % 4):P * (j % 4) + P], us[:, j, NB * PAST:])
            ins.then_inc(utok_ps, 1)
            pe.wait_ge(utok_sb, 4)
            pe.wait_ge(conv_done, CJ)
            pe.wait_ge(pool_conv, 1)
            for j in range(CJ):
                ins = pe.matmul(bk(6, T), ones, mixT[:, j, :], start=(j == 0), stop=(j == CJ - 1))
            ins.then_inc(ln_ps, 1)
            for m in (4, 5):
                out_tile(m, range(CJ, KT))
            pe.wait_ge(ln_sq, 1)
            for j in range(CJ):
                ins = pe.matmul(bk(7, T), ones, lsq[:, j, :], start=(j == 0), stop=(j == CJ - 1))
            ins.then_inc(ln_ps, 1)
            pe.wait_ge(ln_rt, 1)
            pe.wait_ge(mix_ready, CJ)

            def turn_back(g):
                pe.wait_ge(yT_sb, 4 * g + 4)
                if g:
                    pe.wait_ge(x1_part, 3 * g)
                for i, (t0, nt) in enumerate(TILES):
                    for j in range(4):
                        ins = turn(bank[(6, 7, 3)[i]][0:nt, P * j:P * j + P], yT[:, 4 * (g % 2) + j, t0:t0 + nt])
                ins.then_inc(yt_ps, 1)

            for m in range(KT):
                if m < 6:
                    w = view(wbuf[1 + m // 4], 0, KT, GC)
                    for k in range(CJ):
                        ins = pe.matmul(bk(Y_BANK[m], T), w[:, k, P * (m % 4):P * (m % 4) + P], mixT[:, k, :],
                                        start=False, stop=(k == CJ - 1), skip_group_check=True)
                    ins.then_inc(y_ps, 1)
                else:
                    before = max(q for q in range(m) if Y_BANK[q] == Y_BANK[m])
                    pe.wait_ge(yT_sb, before + 1)
                    out_tile(m, range(KT), y_ps)
                if m >= 4 and m % 4 == 0:
                    turn_back(m // 4 - 1)
            turn_back(3)
            pe.wait_ge(x1_part, 12)
            f = 0
            for i, (t0, nt) in enumerate(TILES):
                per = 512 // nt
                for q in range(KT // per):
                    if f >= 4:
                        pe.wait_ge(x1T_sb, f - 3)
                    for k in range(per):
                        ins = turn(bk(4 + f % 4, nt, at=nt * k),
                                   x3[0:nt, i, :].rearrange("t (p k) -> t k p", k=KT)[:, per * q + k, :])
                    ins.then_inc(x1T_ps, 1)
                    f += 1
            pe.wait_ge(wr_in, 64)
            pe.matmul(bk(0, NG + NE, at=256), ones[0:1, :], rbias, start=True, stop=True)
            for i, (t0, nt) in enumerate(TILES):
                pe.wait_ge(x1T_sb, (4, 8, 9)[i])
                o = bank[0][0:nt, 64 * i:64 * i + NG + NE]
                for k in range(KT):
                    ins = pe.matmul(o, x1T[:, k, t0:t0 + nt], wr3[:, k, :], start=(k == 0), stop=(k == KT - 1))
            ins.then_inc(lg_ps, 1)
            pe.wait_ge(hot_ready, 1)
            for i, (t0, nt) in enumerate(TILES):
                ins = pe.matmul(bank[1][:, 3 * NE:4 * NE], ones[0:nt, :], hot[0:nt, i, :], start=(i == 0), stop=(i == 2))
            for i, (t0, nt) in enumerate(TILES):
                o = bank[1][0:nt, NE * i:NE * i + NE]
                for j in range(i):
                    pe.matmul(o, ones[:, 0:nt], hot[:, j, :], start=(j == 0), stop=False)
                ins = pe.matmul(o, tri[0:nt, 0:nt], hot[0:nt, i, :], start=(i == 0), stop=True)
            ins.then_inc(rank_ps, 1)
            pe.wait_ge(tab_ready, 1)
            for j in range(2):
                ins = pe.matmul(bank[2][0:1, 64 * j:64 * j + NSTEP], tab[0:NSTEP, j:j + 1],
                                ident[0:NSTEP, 0:NSTEP], start=True, stop=True)
            ins.then_inc(tab_ps, 1)
            pe.wait_ge(pick_ready, 3)
            pe.wait_ge(h2_ready, 3)
            pe.wait_ge(steps_ready, 1)

            def dispatch(first, half):
                for k in range(8 * half, 8 * half + 8):
                    for i, (t0, nt) in enumerate(TILES):
                        ins = pe.matmul(bk(4 + k // 8, BLK, at=BLK * (k % 8)),
                                        h2[0:nt, i, P * k:P * k + P],
                                        pick[0:nt, i, bass.ds(first, BLK)], start=(i == 0), stop=(i == 2))
                ins.then_inc(xw_ps, 1)

            pe.wait_ge(x1T_sb, 9)
            dispatch(0, 0)
            dispatch(0, 1)
            for i, (t0, nt) in enumerate(TILES):
                pe.wait_ge(ohs_ready, i + 1)
                for c in range(2):
                    ins = pe.matmul(bk(2, 3 * NSTEP, at=128), ohr[0:nt, c, :], ohs[0:nt, c, :],
                                    start=(i == 0 and c == 0), stop=(i == 2 and c == 1))
                ins.then_inc(rows_ps, 1)
            n = step_count(pe)
            pe.wait_ge(rows_ready, 1)
            with pe.Fori(0, NSTEP) as s:
                with pe.If(s < n):
                    at = pe.value_load(steps_i[0:1, bass.ds(s + 65, 1)], min_val=0, max_val=NA)
                    pe.wait_ge(xw_a, s + 2)
                    pe.wait_ge(xw_v, s + 2)
                    for b in range(2):
                        done = (h1_ps, h3_ps)[b]
                        base = (3, 4)[b] * 16
                        w = view(wbuf[b], 0, KT, GC)
                        pe.wait_ge(hg_ready, s + 1)
                        for c in range(NCH):
                            pe.wait_ge(w_in_sem[b][c], base + 16 * s + 16)
                            for k in range(CK * c, CK * c + CK):
                                for half_ in range(2):
                                    ins = pe.matmul(bank[b][BLK * half_:BLK * half_ + BLK, 0:256], xw[:, k, :],
                                                    w[:, k, 256 * half_:256 * half_ + 256], start=(k == 0),
                                                    stop=(k == KT - 1))
                            if c < NCH - 1:
                                ins.then_inc(w_free[b][c], 1)
                        ins.then_inc(done, 1)
                    dispatch(at, 0)
                    pe.wait_ge(hg_ready, s + 2)
                    for j in range(2):
                        ins = turn(bk(6, P, at=P * j), hg[:, P * j:P * j + P])
                    ins.then_inc(hT_ps, 1)
                    dispatch(at, 1)
                    pe.wait_ge(hT_ready, s + 1)
                    pe.wait_ge(ye_a, s + 1)
                    pe.wait_ge(ye_v, s + 1)
                    w = view(wbuf[2], 0, NCH, D)
                    for c in range(NCH):
                        pe.wait_ge(w_in_sem[2][c], 64 + 16 * s + 16)
                        for q in range(4):
                            half_, part_ = q % 2, q // 2
                            ins = pe.matmul(bank[2 + part_][BLK * half_:BLK * half_ + BLK, :], hT[:, c % 2, c // 2, :],
                                            w[:, c, 1024 * half_ + 512 * part_:1024 * half_ + 512 * part_ + 512], start=(c == 0), stop=(c == NCH - 1))
                        if c < NCH - 1:
                            ins.then_inc(w_free[2][c], 1)
                    ins.then_inc(ye_ps, 1)

        @block.vector
        def _(dve):
            dve.sem_inc(u_ready, 4)
            dve.sem_inc(hg_ready, 1)
            dve.sem_inc(ye_v, 1)
            dve.sem_inc(xw_v, 1)
            count = [0]

            def link(ins):
                count[0] += 1
                ins.then_inc(dchain, 1)
                dve.wait_ge(dchain, count[0])

            def mul(out, a, b):
                return dve.tensor_tensor(out, a, b, ALU.mult)

            def add(out, a, b):
                return dve.tensor_tensor(out, a, b, ALU.add)

            for i, (t0, nt) in enumerate(TILES):
                dve.wait_ge(x_rstd, i + 1)
                link(dve.reciprocal(misc[0:nt, 13 + i:14 + i], misc[0:nt, 4 + i:5 + i]))
                dve.tensor_scalar(xn[0:nt, i, :], x3[0:nt, i, :], misc[0:nt, 13 + i:14 + i], None, ALU.mult
                                  ).then_inc(xn_ready, 1)
            f = 0
            dve.wait_ge(g_in, 32)
            for i, (t0, nt) in enumerate(TILES):
                per = 512 // nt
                for q in range(KT // per):
                    dve.wait_ge(nT_ps, f + 1)
                    mul(nT[:, per * q:per * q + per, t0:t0 + nt], bk(4 + f % 2, per, nt),
                        g1[:, per * q:per * q + per].unsqueeze(2).to_broadcast([P, per, nt])).then_inc(nT_sb, 1)
                    f += 1
            dve.wait_ge(small_ps, 1)
            link(dve.tensor_copy(small[:, 0:26], bk(7, 26)))
            link(dve.tensor_copy(small[:, 32:], bk(7, CJ * CW + NH, at=32)))
            link(dve.tensor_scalar(small[:, 24:25], small[:, 24:25], SCALE, None, ALU.mult))
            dve.wait_ge(consts_in, 16)
            link(mul(misc[:, 40:48], sinks, hsel))
            dve.tensor_reduce(misc[:, 48:49], misc[:, 40:48], AX.X, ALU.add).then_inc(small_sb, 1)

            def norm(r):
                h = NORM_ORDER[r]
                dve.wait_ge(rt_done, r + 1)
                link(dve.reciprocal(rr[:, r % 2, :], rr[:, r % 2, :]))
                dve.scalar_tensor_tensor(qkT[:, h, :], qkT[:, h, :], qg if h < NH else kg, rr[:, r % 2, :],
                                         ALU.mult, ALU.mult).then_inc(qk_ready, 1)

            def logits(u):
                k = 20 + 8 * (u % 2)
                dve.wait_ge(s_ps, u + 1)
                if u >= 2:
                    dve.wait_ge(pt_ps, u - 1)
                if u < 8:
                    kw, w, h = P * (u // 4 + 1), 2, 2 * (u % 4)
                    v = prob[:, u % 2, 0:2 * kw].rearrange("p (h k) -> p h k", h=2)
                    sk = sinks[:, h:h + 2]
                    for j in range(2):
                        ins = dve.scalar_tensor_tensor(v[:, j, :], dist[:, 2 * P - kw:2 * P], -SLOPES[h + j],
                                                       bk(4 + u % 2, kw, at=kw * j), ALU.mult, ALU.add)
                else:
                    w, v, sk = 1, prob[:, u % 2, 0:NKS], misc[:, 48:49]
                    ins = add(v, bk(4 + u % 2, NKS), sbias[:, u - 8, :])
                ins.then_inc(s_sb, 1)
                m = misc[:, 36 + 2 * (u % 2):36 + 2 * (u % 2) + w]
                dve.wait_ge(s_sb, u + 1)
                link(dve.tensor_reduce(m, v, AX.X, ALU.max))
                link(dve.tensor_tensor(m, m, sk, ALU.max))
                link(dve.tensor_scalar(misc[:, k:k + w], m, -1.0, None, ALU.mult))
                dve.tensor_tensor(misc[:, k + 6:k + 6 + w], sk, m, ALU.subtract).then_inc(s_max, 1)

            def normalise(u):
                k, w = 20 + 8 * (u % 2), 2 if u < 8 else 1
                dve.wait_ge(p_exp, 3 * u + 3)
                den = misc[:, k + 2:k + 2 + w]
                link(add(den, den, misc[:, k + 4:k + 4 + w]))
                link(dve.reciprocal(den, den))
                if u < 8:
                    kw = P * (u // 4 + 1)
                    v = prob[:, u % 2, 0:2 * kw].rearrange("p (h k) -> p h k", h=2)
                    mul(v, v, den.unsqueeze(2).to_broadcast([P, 2, kw])).then_inc(p_ready, 1)
                else:
                    v = prob[:, u % 2, 0:NKS]
                    dve.tensor_scalar(v, v, den, None, ALU.mult).then_inc(p_ready, 1)

            def heads_out(u):
                dve.wait_ge(o_ps, u + 1)
                if u < 8:
                    h = CJ + 2 * (u % 4)
                    dve.tensor_copy(mixT[:, h:h + 2, P * (u // 4):P * (u // 4) + P], bk(7, 2, P)).then_inc(o_sb, 1)
                else:
                    t0 = TP + 4 * TB * (u - 8)
                    for b in range(4):
                        ins = dve.tensor_copy(mixT[:, CJ:KT, t0 + TB * b:t0 + TB * b + TB], bk(7, NH, TB, at=32 * b))
                    ins.then_inc(o_sb, 1)

            convs = [0]

            def glu(j):
                dve.wait_ge(proj_sb, 4 + 12 + 2 * j + 2)
                mul(up[:, j, PAST:PAST + TP], aT[:, j % 2, 0:TP], sgT[:, j % 2, 0:TP])
                mul(us[:, j, NB * PAST:].rearrange("p (r b) -> p r b", b=NB),
                    aT[:, j % 2, TP:T].rearrange("p (b r) -> p r b", b=NB),
                    sgT[:, j % 2, TP:T].rearrange("p (b r) -> p r b", b=NB)).then_inc(u_ready, 1)
                dve.wait_ge(u_ready, 4 + j + 1)

            def conv(j, taps_):
                pairs = [(mixT[:, j, 0:TP], lambda w: up[:, j, w:w + TP])]
                if j >= 4:
                    pairs.append((mixT[:, j, TP:T].rearrange("p (b t) -> p t b", b=NB),
                                  lambda w: us[:, j, NB * w:NB * (w + TB)].rearrange("p (t b) -> p t b", b=NB)))
                for w in taps_:
                    for acc, src in pairs:
                        if w:
                            dve.wait_ge(cchain, convs[0] - len(pairs) + 1)
                            ins = dve.scalar_tensor_tensor(acc, src(w), taps[:, j, w:w + 1], acc, ALU.mult, ALU.add)
                        else:
                            ins = dve.tensor_scalar(acc, src(w), taps[:, j, 0:1], convb[:, j:j + 1], ALU.mult, ALU.add)
                        ins.then_inc(cchain, 1)
                        convs[0] += 1
                if taps_[-1] == CW - 1:
                    dve.wait_ge(cchain, convs[0])
                    dve.sem_inc(conv_done, 1)

            for n in range(28):
                if n - 2 in NORM_AT:
                    norm(NORM_AT.index(n - 2))
                if n == 6:
                    dve.wait_ge(ktok_ps, 1)
                    dve.tensor_copy(ktok[:, 0, :], bank[6][:, 0:256]).then_inc(ktok_sb, 1)
                    dve.tensor_copy(ktok[0:TS, 1, :], bank[6][0:TS, 256:512]).then_inc(ktok_sb, 1)
                if n in (8, 10):
                    for q in (n - 8, n - 7):
                        dve.wait_ge(kc_ps, q + 1)
                        dve.tensor_copy(keysT[:, 2 * q:2 * q + 2, :].rearrange("p b k -> p (b k)"), bk(6 + q % 2, 512)
                                        ).then_inc(kc_sb, 1)
                if n == 14:
                    dve.wait_ge(pool_set, 3)
                    dve.wait_ge(k_out, KV_OUT)
                    dve.wait_ge(qk_ready, NH + NKV)
                    for b in range(NB):
                        ins = dve.tensor_copy(qs[:, b, :].rearrange("p (h t) -> p h t", h=NH),
                                              qkT[:, 0:NH, TP + TB * b:TP + TB * b + TB])
                    ins.then_inc(qk_ready, 1)
                if n >= 14 and n % 2 == 0:
                    glu((n - 14) // 2)
                if 13 <= n < 23:
                    logits(n - 13)
                if 14 <= n < 24:
                    normalise(n - 14)
                if 16 <= n < 26:
                    heads_out(n - 16)
                if n >= 14:
                    conv((n - 14) // 2, range(0, 16) if n % 2 == 0 else range(16, CW))
            glu(7)
            dve.wait_ge(utok_ps, 1)
            for g in range(2):
                dve.tensor_copy(utok[0:PAST, 0, 512 * g:512 * g + 512], bank[4 + g][0:PAST, :]).then_inc(utok_sb, 1)
                dve.tensor_copy(utok[0:TS, 1, 512 * g:512 * g + 512], bank[6 + g][0:TS, :]).then_inc(utok_sb, 1)
            conv(7, range(CW))

            dve.wait_ge(ln_ps, 1)
            link(dve.tensor_scalar(lmean, bk(6, T), 1.0 / DC, None, ALU.mult))
            dve.tensor_tensor(mixT[:, 0:CJ, :], mixT[:, 0:CJ, :], lmean.unsqueeze(1).to_broadcast([P, CJ, T]),
                              ALU.subtract).then_inc(ln_n, 1)
            dve.wait_ge(ln_rt, 1)
            link(dve.reciprocal(lrstd, lrstd))
            for q in range(2):
                v = mixT[:, 4 * q:4 * q + 4, :]
                mul(v, v, lrstd.unsqueeze(1).to_broadcast([P, 4, T])).then_inc(ln_n, 1)

            dve.wait_ge(x_again, 48)
            for g in range(4):
                dve.wait_ge(yt_ps, g + 1)
                for i, (t0, nt) in enumerate(TILES):
                    xs = x3[0:nt, i, 512 * g:512 * g + 512]
                    add(xs, xs, bank[(6, 7, 3)[i]][0:nt, :]).then_inc(x1_part, 1)
            dve.wait_ge(outs, OUTS_MIX)
            dve.wait_ge(y_ps, KT)
            f = 0
            for i, (t0, nt) in enumerate(TILES):
                per = 512 // nt
                for q in range(KT // per):
                    dve.wait_ge(x1T_ps, f + 1)
                    mul(x1T[:, per * q:per * q + per, t0:t0 + nt], bk(4 + f % 4, per, nt),
                        g2[:, per * q:per * q + per].unsqueeze(2).to_broadcast([P, per, nt])).then_inc(x1T_sb, 1)
                    f += 1
                    if f == 4:
                        dve.wait_ge(h2_ms, 12)
                        dve.tensor_reduce(misc[:, 7:10], misc[:, 50:62].rearrange("p (i g) -> p i g", i=3), AX.X, ALU.add
                                          ).then_inc(h2_sum, 1)
                    if f == 6:
                        dve.wait_ge(h2_rt, 1)
                        link(dve.tensor_scalar(misc[:, 13:16], misc[:, 10:13], 1e-30, None, ALU.max))
                        dve.reciprocal(misc[:, 13:16], misc[:, 13:16]).then_inc(h2_rec, 1)

            def over(i):
                return slice(0, TILES[i][1])

            def all3(v):
                return v.rearrange("p (i e) -> p i e", i=3)

            link(dve.memset(reg[:, rt0:R_SIZE], 0.0))
            link(dve.memset(lg8[:, :, NG:], -3e38))
            link(dve.memset(pick[:, :, NA:XW], 0.0))
            link(dve.memset(ui[:, :], 0))
            dve.wait_ge(h2_rec, 1)
            dve.wait_ge(lg_ps, 1)
            link(dve.tensor_copy(rbc, bk(0, NG + NE, at=256)))
            for i in range(3):
                for out, a, w in ((lg8, 0, NG), (le, NG, NE)):
                    ins = dve.scalar_tensor_tensor(out[over(i), i, 0:w], bank[0][over(i), 64 * i + a:64 * i + a + w],
                                                   misc[over(i), 13 + i:14 + i], rbc[over(i), a:a + w], ALU.mult, ALU.add)
            link(ins)
            for i in range(3):
                ins = dve.max(mg[over(i), i, :], lg8[over(i), i, :])
            link(ins)
            for i in range(3):
                ins = dve.max_index(ui[over(i), 8 * i:8 * i + 8], mg[over(i), i, :], lg8[over(i), i, :])
            link(ins)
            link(dve.tensor_copy(gf, all3(ui[:, 0:24])[:, :, 0]))
            link(dve.tensor_tensor(gone, row[:, 0:NG].unsqueeze(1).to_broadcast([P, 3, NG]),
                                   gf.unsqueeze(2).to_broadcast([P, 3, NG]), ALU.is_equal))
            for i in range(3):
                ins = mul(prod[:, i, :].rearrange("p (g e) -> p g e", g=NG), le[:, i, :].rearrange("p (g e) -> p g e", g=NG),
                          gone[:, i, :].unsqueeze(2).to_broadcast([P, NG, EG]))
            link(ins)
            for i in range(3):
                ins = dve.tensor_reduce(ein[:, i, :], prod[:, i, :].rearrange("p (g e) -> p e g", g=NG), AX.X, ALU.add)
            link(ins)
            for i in range(3):
                ins = dve.max(me[over(i), i, :], ein[over(i), i, :])
            link(ins)
            for i in range(3):
                ins = dve.max_index(ui[over(i), 24 + 8 * i:32 + 8 * i], me[over(i), i, :], ein[over(i), i, :])
            link(ins)
            for e, c in ((e1, 0), (e2, 1)):
                ins = dve.tensor_copy(e, all3(ui[:, 24:48])[:, :, c])
            link(ins)
            for e in (e1, e2):
                ins = dve.scalar_tensor_tensor(e, gf, float(EG), e, ALU.mult, ALU.add)
            link(ins)
            for h, e in ((hot1, e1), (hot2, e2)):
                ins = dve.tensor_tensor(h, row[:, 0:NE].unsqueeze(1).to_broadcast([P, 3, NE]),
                                        e.unsqueeze(2).to_broadcast([P, 3, NE]), ALU.is_equal)
            link(ins)
            add(hot, hot1, hot2).then_inc(hot_ready, 1)
            dg = expd.rearrange("p (i c) -> p i c", i=3)
            dve.tensor_tensor(dg[:, :, 0:NG], lg8[:, :, 0:NG], mg[:, :, 0:1].to_broadcast([P, 3, NG]), ALU.subtract)
            dve.tensor_tensor(dg[:, :, NG:NG + 1], me[:, :, 1:2], me[:, :, 0:1], ALU.subtract).then_inc(r_sub, 1)
            dve.wait_ge(rank_ps, 1)
            link(dve.tensor_copy(cnt, bk(1, NE, at=3 * NE)))
            dve.tensor_tensor_scan(start, ones[:, 0:NE], cnt, 0.0, ALU.mult, ALU.add)
            link(dve.tensor_scalar(nblk, cnt, 0.0, None, ALU.is_gt))
            for m in range(1, -(-T // BLK)):
                link(dve.scalar_tensor_tensor(nblk, cnt, float(m * BLK), nblk, ALU.is_gt, ALU.add))
            link(dve.tensor_scalar(nblk[:, 0:1], nblk[:, 0:1], 1.0, None, ALU.max))
            dve.tensor_tensor(start, start, cnt, ALU.subtract)
            link(dve.tensor_tensor_scan(cum, ones[:, 0:NE], nblk, 0.0, ALU.mult, ALU.add))
            link(dve.tensor_tensor(sid, cum, nblk, ALU.subtract))
            link(dve.scalar_tensor_tensor(off, sid, -float(BLK), start, ALU.mult, ALU.add))
            cs = col[0:NSTEP]
            dve.tensor_scalar(tle[0:NSTEP], cum[0:NSTEP], cs, None, ALU.is_le)
            link(dve.tensor_scalar(tid[0:NSTEP], sid[0:NSTEP], cs, None, ALU.is_le))
            dve.tensor_reduce(tab[0:NSTEP, 0:1], tle[0:NSTEP], AX.X, ALU.add)
            link(dve.tensor_tensor(tid[0:NSTEP], tid[0:NSTEP], tle[0:NSTEP], ALU.subtract))
            link(mul(tid[0:NSTEP], tid[0:NSTEP], off[0:NSTEP]))
            link(dve.tensor_reduce(tab[0:NSTEP, 1:2], tid[0:NSTEP], AX.X, ALU.add))
            link(dve.scalar_tensor_tensor(tab[0:NSTEP, 1:2], cs, float(BLK), tab[0:NSTEP, 1:2], ALU.mult, ALU.add))
            dve.tensor_scalar(tab[0:NSTEP, 1:2], tab[0:NSTEP, 1:2], float(NA), None, ALU.min).then_inc(tab_ready, 1)
            link(dve.tensor_copy(steps_i[0:1, 128:129], cum[0:1, NE - 1:NE]))
            q = 0
            for i in range(3):
                rank = bank[1][over(i), NE * i:NE * i + NE]
                for c, h in enumerate((hot1, hot2)):
                    for out, per_expert in ((rnk, rank), (pos, start[over(i)]), (stp, sid[over(i)])):
                        ins = dve.tensor_tensor_reduce(junk[over(i), q, :], h[over(i), i, :], per_expert, 1.0, 0.0, ALU.mult,
                                                       ALU.add, out[over(i), i, c:c + 1])
                        q += 1
            link(ins)
            link(add(pos, pos, rnk))
            for i in range(3):
                n = over(i)
                link(dve.tensor_scalar(pick[n, i, 0:NA], row[n, 0:NA], pos[n, i, 0:1], None, ALU.is_equal))
                dve.scalar_tensor_tensor(pick[n, i, 0:NA], row[n, 0:NA], pos[n, i, 1:2], pick[n, i, 0:NA],
                                         ALU.is_equal, ALU.add).then_inc(pick_ready, 1)
            dve.wait_ge(tab_ps, 1)
            link(dve.tensor_copy(steps_i[0:1, 0:NSTEP], bank[2][0:1, 0:NSTEP]))
            dve.tensor_copy(steps_i[0:1, 64:64 + NSTEP], bank[2][0:1, 64:64 + NSTEP]).then_inc(steps_ready, 1)
            dve.wait_ge(r_exp, 1)
            link(dve.tensor_reduce(gsum, dg[:, :, 0:NG], AX.X, ALU.add))
            link(dve.tensor_scalar(gates[:, :, 1], dg[:, :, NG], 1.0, None, ALU.add))
            link(mul(gsum, gsum, gates[:, :, 1]))
            link(dve.reciprocal(gates[:, :, 0], gsum))
            link(mul(gates[:, :, 1], gates[:, :, 0], dg[:, :, NG]))
            link(dve.tensor_scalar(blk, rnk, float(BLK), None, ALU.is_ge))
            for m in range(2, -(-T // BLK)):
                link(dve.scalar_tensor_tensor(blk, rnk, float(m * BLK), blk, ALU.is_ge, ALU.add))
            link(add(stp, stp, blk))
            link(dve.scalar_tensor_tensor(rnk, blk, -float(BLK), rnk, ALU.mult, ALU.add))
            for i in range(3):
                link(dve.tensor_scalar(tokid[:, i:i + 1], col, float(TILES[i][0]), None, ALU.add))
            for i in range(3):
                n = over(i)
                if i:
                    dve.wait_ge(rows_ps, i)
                for c in range(2):
                    dve.tensor_scalar(ohr[n, c, :].rearrange("p (h r) -> p h r", h=2),
                                      row[n, 0:BLK].unsqueeze(1).to_broadcast([TILES[i][1], 2, BLK]), rnk[n, i, c:c + 1],
                                      None, ALU.is_equal)
                    link(dve.tensor_scalar(ohs[n, c, 2 * NSTEP:], row[n, 0:NSTEP], stp[n, i, c:c + 1], None, ALU.is_equal))
                    dve.tensor_scalar(ohs[n, c, 0:NSTEP], ohs[n, c, 2 * NSTEP:], tokid[n, i:i + 1], None, ALU.mult)
                    ins = dve.tensor_scalar(ohs[n, c, NSTEP:2 * NSTEP], ohs[n, c, 2 * NSTEP:], gates[n, i, c:c + 1], None,
                                            ALU.mult)
                    if c:
                        ins.then_inc(ohs_ready, 1)
                    else:
                        link(ins)

            def step_tokens(turn, half):
                dve.wait_ge(xw_ps, 2 * turn + 1 + half)
                mul(xw[:, 8 * half:8 * half + 8, :], bk(4 + half, 8, BLK),
                    g2[:, 8 * half:8 * half + 8].unsqueeze(2).to_broadcast([P, 8, BLK])).then_inc((xw_a, xw_v)[half], 1)

            step_tokens(0, 0)
            step_tokens(0, 1)
            dve.wait_ge(rows_ps, 3)
            R = bk(2, 3, NSTEP, at=128)
            link(dve.tensor_copy(gate_of, R[:, 1, :]))
            link(dve.tensor_scalar(half, col, float(BLK), float(-NONE), ALU.is_ge, ALU.subtract))
            link(dve.tensor_scalar(idx_f, R[:, 0, :], 2.0, half, ALU.mult, ALU.add))
            link(dve.scalar_tensor_tensor(idx_f, R[:, 2, :], -float(NONE), idx_f, ALU.mult, ALU.add))
            dve.tensor_copy(idx_all, idx_f).then_inc(rows_ready, 1)

            n = step_count(dve)
            with dve.Fori(0, NSTEP) as s:
                with dve.If(s < n):
                    dve.wait_ge(h1_sb, s + 1)
                    dve.wait_ge(h3_ps, s + 1)
                    mul(hg, h1s, bk(1, 256)).then_inc(hg_ready, 1)
                    step_tokens(s + 1, 0)
                    dve.wait_ge(hT_ps, s + 1)
                    dve.tensor_copy(hT.rearrange("p j h t -> p (j h t)"), bk(6, 256)).then_inc(hT_ready, 1)
                    step_tokens(s + 1, 1)
                    dve.wait_ge(ye_ps, s + 1)
                    dve.wait_ge(ye_free, s + 1)
                    dve.tensor_scalar(ystage[:, 512:1024], bk(3, 512), gate_of[:, bass.ds(s, 1)], None, ALU.mult
                                      ).then_inc(ye_v, 1)


NORM_ORDER = [NH, NH + 1] + list(range(NH))
NORM_AT = [0, 1] + list(range(4, 12))
Y_BANK = [0, 1, 2, 3, 4, 5] + [(0, 1, 2, 4, 5)[i % 5] for i in range(KT - 6)]
KV_OUT = 16 * (2 + 2 * NB)
OUTS_MIX = 16 * (3 + 1 + TB)


_INS = ["x_prompt", "x_sample", "state_conv", "cache_k", "cache_v", "norm1_g", "w_in", "conv_w", "conv_b",
        "conv_norm_g", "conv_norm_b", "q_norm_g", "k_norm_g", "attn_sinks", "w_out", "norm2_g",
        "w_router_group", "b_router_group", "w_router_expert", "b_router_expert", "w1", "w3", "w2"]
_SHAPES = {"x_prompt": (TP, D), "x_sample": (TS, D), "state_conv": (NB, PAST, DC), "cache_k": (NB, W, NKV * HD),
           "cache_v": (NB, W, NKV * HD)}
_OUTS = [((T, D), (T, D)), ((PAST, DC), (1, 1, PAST, DC)),
         ((W, NKV * HD), (1, 1, W, NKV, HD)), ((W, NKV * HD), (1, 1, W, NKV, HD)),
         ((NB, PAST, DC), (1, NB, PAST, DC)), ((NB, W, NKV * HD), (1, NB, W, NKV, HD)),
         ((NB, W, NKV * HD), (1, NB, W, NKV, HD))]


def kernel(**inputs):
    import concourse.bacc as bacc
    from concourse.bass_utils import run_bass_kernel_spmd

    nc = bacc.Bacc("TRN2", target_bir_lowering=False, num_devices=1)
    arrays, args = {}, []
    for name in _INS:
        a = np.ascontiguousarray(inputs[name])
        a = a.reshape(_SHAPES.get(name, a.shape[1:]))
        arrays[f"in_{name}"] = a
        args.append(nc.dram_tensor(f"in_{name}", a.shape, F32, kind="ExternalInput").ap())
    arrays["shape_tables"] = a = shape_constants()
    args.append(nc.dram_tensor("shape_tables", a.shape, F32, kind="ExternalInput").ap())
    for i, (shape, _) in enumerate(_OUTS):
        args.append(nc.dram_tensor(f"out_{i}", shape, F32, kind="ExternalOutput").ap())
    hybrid_layer(nc, *args)
    r = run_bass_kernel_spmd(nc, [arrays], core_ids=[0])
    y, *rest = (np.asarray(r.results[0][f"out_{i}"]).reshape(full) for i, (_, full) in enumerate(_OUTS))
    return (y[:TP].reshape(1, TP, D), y[TP:].reshape(NB, TB, D), *rest)
```

```python
from contextlib import ExitStack

import concourse.bass as bass
import numpy as np
from concourse import mybir

F32 = mybir.dt.float32
I32 = mybir.dt.int32
U32 = mybir.dt.uint32
ALU = mybir.AluOpType
ACT = mybir.ActivationFunctionType
AX = mybir.AxisListType

P = 128
D = 2048
KT = D // P
DC = 1024
CJ = DC // P
CW = 31
PAST = CW - 1
NH, NKV, HD = 8, 2, 128
GQA = NH // NKV
W = 128
TP = 256
NB, TB = 8, 4
TS = NB * TB
T = TP + TS
TILES = [(0, P), (P, P), (TP, TS)]
NG, EG = 4, 8
NE = NG * EG
DE = 512
NA = 2 * T
BLK = 64
NSTEP = NE + NA // BLK - 1
XW = NA + BLK
GC = 512
CK = 4
NCH = KT // CK
EPS = 1e-6
SCALE = 1.0 / float(np.sqrt(HD))
MASKED = -1e30
FAR = 1e30
SLOPES = [2.0 ** (-8.0 * (h + 1) / NH) for h in range(NH)]
NONE = 8192
RC = 64
NKS = NKV * W + NKV * TS


def shape_constants():
    cs = np.zeros((P, C_SIZE), np.float32)
    cs[:, C_ID:C_ID + P] = np.eye(P)
    cs[:, C_ONE:C_ONE + P] = 1.0
    cs[:, C_TRI:C_TRI + P] = np.triu(np.ones((P, P)), 1)
    cs[:, C_ROW:C_ROW + NA] = np.arange(NA)
    cs[:, C_COL] = np.arange(P)
    rows = np.arange(P)
    cs[rows, C_HSEL + (rows % 32) // TB] = 1.0
    slope = SLOPES
    dist = np.arange(P)[:, None] + P - np.arange(2 * P)[None, :]
    ok = (dist >= 0) & (dist < W)
    cs[:, C_DIST:C_DIST + 2 * P] = np.where(ok, dist, FAR)
    sample = np.full((P, 2, NKS), MASKED)
    for r in range(P):
        h, t = (r % 32) // TB, r % TB
        kv = h // GQA
        for i in range(2):
            b = 4 * i + r // 32
            for c in range(W):
                if W + t - c < W:
                    sample[r, i, kv * W + c] = -slope[h] * (W + t - c)
            for u in range(t + 1):
                sample[r, i, NKV * W + kv * TS + TB * b + u] = -slope[h] * (t - u)
    cs[:, C_SAMP:C_SAMP + 2 * NKS] = sample.reshape(P, -1)
    return cs


C_ID, C_ONE, C_TRI = 0, P, 2 * P
C_ROW = 3 * P
C_COL = C_ROW + NA
C_HSEL = C_COL + 1
C_DIST = C_HSEL + NH
C_SAMP = C_DIST + 2 * P
C_SIZE = C_SAMP + 2 * NKS


def hybrid_layer(nc, x_prompt, x_sample, state_conv, cache_k, cache_v, norm1_g, w_in, conv_w, conv_b,
                 conv_norm_g, conv_norm_b, q_norm_g, k_norm_g, attn_sinks, w_out, norm2_g,
                 w_router_group, b_router_group, w_router_expert, b_router_expert, w1, w3, w2, const_small,
                 y_all, conv_prompt, k_prompt, v_prompt, conv_sample, k_sample, v_sample):
    with ExitStack() as ctx:
        def sem(name):
            return ctx.enter_context(nc.semaphore(name))

        def sb(name, n, dt=F32):
            return ctx.enter_context(nc.sbuf_tensor(name, [P, n], dt))

        wbuf = [sb(f"wbuf{b}", KT * GC) for b in range(3)]
        x_sb = sb("x_sb", 3 * D)
        cst = sb("cst", C_SIZE)
        small = sb("small", 32 + CJ * CW + NH)
        gains = sb("gains", 2 * KT)
        misc = sb("misc", 64)
        tmpc = sb("tmpc", 4 * TS)
        ui = sb("ui", 48, U32)
        idx_now = sb("idx_now", 1, U32)[:, :]
        steps_i = sb("steps_i", 2 * 64 + 1, I32)
        R_SIZE = 2 * KT * T + (NH + NKV) * T + CJ * (PAST + TP) + CJ * NB * (PAST + TB) + 8 * T + 1024
        reg = sb("reg", R_SIZE)

        def view(t, at, *dims):
            n = int(np.prod(dims))
            v = t[:, at:at + n]
            if len(dims) == 1:
                return v
            names = "abc"[:len(dims)]
            return v.rearrange(f"p ({' '.join(names)}) -> p {' '.join(names)}", **dict(zip(names, dims)))

        x3 = view(x_sb, 0, 3, D)
        ident = cst[:, C_ID:C_ID + P]
        ones = cst[:, C_ONE:C_ONE + P]
        tri = cst[:, C_TRI:C_TRI + P]
        row = cst[:, C_ROW:C_ROW + NA]
        col = cst[:, C_COL:C_COL + 1]
        hsel = cst[:, C_HSEL:C_HSEL + NH]
        dist = cst[:, C_DIST:C_DIST + 2 * P]
        sbias = view(cst, C_SAMP, 2, NKS)
        taps = view(small, 32, CJ, CW)
        sinks = small[:, 32 + CJ * CW:32 + CJ * CW + NH]
        convb, lng, lnb = (small[:, CJ * i:CJ * i + CJ] for i in range(3))
        qg, kg = small[:, 24:25], small[:, 25:26]
        g1, g2 = gains[:, 0:KT], gains[:, KT:2 * KT]
        o = 0
        nT = view(reg, o, KT, T)
        lsq = view(reg, o, CJ, T)
        lmean, lrstd = view(reg, o + CJ * T, T), view(reg, o + CJ * T + T, T)
        yT = view(reg, o, 8, T)
        o += KT * T
        mixT = view(reg, o, KT, T)
        xn = view(reg, o, 3, D)
        kc = view(reg, o, NB, NKV * HD)
        ktok = view(reg, o + 12 * T, 2, NKV * HD)
        o += KT * T
        qkT = view(reg, o, NH + NKV, T)
        utok = view(reg, o, 2, DC)
        o += (NH + NKV) * T
        up = view(reg, o, CJ, PAST + TP)
        o += CJ * (PAST + TP)
        us = view(reg, o, CJ, NB * (PAST + TB))
        rows_cw = reg[0:CW, o:o + DC]
        rows_vec = reg[0:26, o + DC:o + DC + P]
        row_sink = reg[0:1, o + DC + P:o + DC + P + NH]
        o += CJ * NB * (PAST + TB)
        state = view(reg, o, 2, DC)
        wr3 = view(reg, o, KT, RC)
        rbias = reg[0:1, o + KT * RC:o + KT * RC + NG + NE]
        aT, sgT = view(reg, o, 2, T), view(reg, o + 2 * T, 2, T)
        o += 4 * T
        sq, rr = view(reg, o, 2, T), view(reg, o + 2 * T, 2, T)
        o += 4 * T
        odd_taps = reg[:, o - 4 * T:o - 3 * T]
        lsum = odd_taps
        prob = view(reg, o - 512, 3, 512)
        vT = view(reg, o, NKV, T)
        o += 1024
        assert o == R_SIZE
        keysT = view(x_sb, 0, NB, NKV * W)
        vc = view(x_sb, 2048, NB, NKV * HD)
        vtok = view(x_sb, 4096, 3, NKV * HD)
        qs = view(x_sb, 4864, NB, NH * TB)
        PT = view(x_sb, 5120, 2, 512)
        part_y = [view(reg, (CJ + 2 + m) * T, T) for m in range(6)]
        part_y += [view(reg, R_SIZE - 1024 - 3 * T + m * T, T) for m in range(6)]
        assert 6 * T <= 1024 + 3 * T
        h2 = view(reg, 0, 3, D)
        x1T = view(reg, 3 * D, KT, T)
        o = 3 * D + KT * T
        pick = view(reg, o, 3, XW)
        o += 3 * XW
        lT = view(reg, o - 3 * XW, T)
        xd = x_sb[:, 0:1024]
        xw = view(reg, o, KT, BLK)
        o += KT * BLK
        ystage = reg[:, o:o + 1024]
        o += 1024
        h1s, hg, hT = reg[:, o:o + 256], reg[:, o + 256:o + 512], view(reg, o + 512, 2, 2, BLK)
        o += 768
        window = view(reg, o, 3, BLK)
        o += 3 * BLK
        ohr = view(reg, o, 6, P)
        ohs = view(reg, o + 6 * P, 6, 3 * NSTEP)
        o += 6 * (P + 3 * NSTEP)
        g2w = reg[:, o:o + KT]
        assert o + KT <= 2 * KT * T + (NH + NKV) * T + CJ * (PAST + TP) + CJ * NB * (PAST + TB) + 4 * T
        rt0 = o = 2 * KT * T + (NH + NKV) * T + CJ * (PAST + TP) + CJ * NB * (PAST + TB) + 4 * T
        at = [0]

        def part(*dims):
            at[0] += int(np.prod(dims))
            assert rt0 + at[0] <= R_SIZE
            return view(reg, rt0 + at[0] - int(np.prod(dims)), *dims)

        expd = part(15)
        lg8, mg = part(3, 8), part(3, 8)
        le, ein, me = part(3, NE), part(3, EG), part(3, 8)
        gf, e1, e2 = part(3), part(3), part(3)
        gone, prod = part(3, NG), part(3, NE)
        hot1, hot2, hot = part(3, NE), part(3, NE), part(3, NE)
        cnt, start, nblk, cum, sid, off = (part(NE) for _ in range(6))
        pos, rnk, blk, stp = (part(3, 2) for _ in range(4))
        tle, tid, tab, rank0 = part(NE), part(NE), part(2), part(3)
        gsum, gates, tokid = part(3), part(3, 2), part(3)
        rbc = part(NG + NE)
        junk = part(18, NE)
        gate_of, idx_f, half = part(NSTEP), part(NSTEP), part(1)
        idx_all = part(NSTEP).bitcast(U32)
        eps = misc[:, 0:1]
        sq_junk = view(reg, CJ * T, 512)
        bank = [ctx.enter_context(nc.psum_tensor(f"bank{b}", [P, 512], F32)) for b in range(8)]

        def bk(b, *dims, at=0):
            return view(bank[b], at, *dims)

        consts_in, x_in, g_in, rows_in, state_in, kc_in, vc_in, wr_in, x_again, outs, k_out = (
            sem(n) for n in ("consts_in", "x_in", "g_in", "rows_in", "state_in", "kc_in", "vc_in",
                             "wr_in", "x_again", "outs", "k_out"))
        w_in_sem = [[sem(f"w_landed{b}{c}") for c in range(NCH)] for b in range(3)]
        w_free = [[sem(f"w_free{b}{c}") for c in range(NCH - 1)] for b in range(3)]
        pool_set = sem("pool_set")
        x_ms, x_rstd, x_rec, xn_ready, xn_mid = (sem(n) for n in ("x_ms", "x_rstd", "x_rec", "xn_ready", "xn_mid"))
        small_ps, small_sb = sem("small_ps"), sem("small_sb")
        nT_ps, nT_sb, st_ps, st_sb = sem("nT_ps"), sem("nT_sb"), sem("st_ps"), sem("st_sb")
        kc_ps, kc_sb = sem("kc_ps"), sem("kc_sb")
        proj_ps, proj_sb, u_ready = sem("proj_ps"), sem("proj_sb"), sem("u_ready")
        conv_done, pool_conv = sem("conv_done"), sem("pool_conv")
        sq_done, ss_ps, rt_done, qk_ready = sem("sq_done"), sem("ss_ps"), sem("rt_done"), sem("qk_ready")
        v_ps, v_sb, ktok_ps, ktok_sb = sem("v_ps"), sem("v_sb"), sem("ktok_ps"), sem("ktok_sb")
        utok_ps, utok_sb = sem("utok_ps"), sem("utok_sb")
        s_ps, s_sb, s_max, p_exp, p_ready = sem("s_ps"), sem("s_sb"), sem("s_max"), sem("p_exp"), sem("p_ready")
        pt_ps, pt_sb, o_ps, o_sb = sem("pt_ps"), sem("pt_sb"), sem("o_ps"), sem("o_sb")
        ln_ps, ln_sq, ln_rt, ln_n, mix_ready = sem("ln_ps"), sem("ln_sq"), sem("ln_rt"), sem("ln_n"), sem("mix_ready")
        yh_ps, yh_sb, y_ps, yT_a, yT_v, yt_ps, x1_part, wr_zero, lT_ps, lT_sb = (
            sem(n) for n in ("yh_ps", "yh_sb", "y_ps", "yT_a", "yT_v", "yt_ps", "x1_part", "wr_zero", "lT_ps", "lT_sb"))
        h2_ms, h2_sum, h2_rt, h2_rec, h2_ready = (sem(n) for n in ("h2_ms", "h2_sum", "h2_rt", "h2_rec", "h2_ready"))
        x1T_ps, x1T_v, x1T_a, wr_gain = sem("x1T_ps"), sem("x1T_v"), sem("x1T_a"), sem("wr_gain")
        lg_ps, r_sub, r_exp = sem("lg_ps"), sem("r_sub"), sem("r_exp")
        cnt_ps, ln_red, ranks_read = sem("cnt_ps"), sem("ln_red"), sem("ranks_read")
        hot_ready, rank_ps, pick_ready, tab_ready, tab_ps, steps_ready = (
            sem(n) for n in ("hot_ready", "rank_ps", "pick_ready", "tab_ready", "tab_ps", "steps_ready"))
        ohs_ready, rows_ps, rows_ready = sem("ohs_ready"), sem("rows_ps"), sem("rows_ready")
        x1_stored = sem("x1_stored")
        xd_ps, xd_a, xd_v, xw_ps, xw_ready = (sem(n) for n in ("xd_ps", "xd_a", "xd_v", "xw_ps", "xw_ready"))
        h1_ps, h3_ps, h1_sb, hT_ready, ye_ps, ye_a, ye_v, ye_out, idx_set = (
            sem(n) for n in ("h1_ps", "h3_ps", "h1_sb", "hT_ready", "ye_ps", "ye_a", "ye_v", "ye_out", "idx_set"))
        window_ready = sem("window_ready")
        pool_go, ye_free, hg_ready, hT_ps = sem("pool_go"), sem("ye_free"), sem("hg_ready"), sem("hT_ps")
        dchain, cchain, pchain = sem("vector_chain"), sem("conv_chain"), sem("pool_chain")

        block = ctx.enter_context(nc.Block())

        def step_count(eng):
            return eng.value_load(steps_i[0:1, 128:129], min_val=1, max_val=NSTEP)

        GROUPS = [3072, 2048, 2560, 0, 1024, 512, 1536]
        TILE = [(0, m) for m in range(4)] + [(1 + i, m) for i in range(2) for m in range(4)]
        TILE += [(3 + 2 * i + g, m) for i in range(2) for m in range(4) for g in range(2)]
        LAST = [max(n for n, (g, _) in enumerate(TILE) if g == k) for k in range(len(GROUPS))]

        @block.sync
        def _(sp):
            def group(b, src, first):
                for c in range(NCH):
                    part_ = src(c, first)
                    sp.dma_start(view(wbuf[b], c * CK * GC, part_.shape[1], part_.shape[2]), part_).then_inc(w_in_sem[b][c], 16)

            def in_cols(c, first):
                return w_in.rearrange("(p k) n -> p k n", k=KT)[:, CK * c:CK * c + CK, first:first + GC]

            def out_part(half, cols):
                def src(c, first):
                    k = CJ * half + 2 * c
                    return w_out.rearrange("(k p) n -> p k n", p=P)[:, k:k + 2, 2 * GC * cols:2 * GC * cols + 2 * GC]
                return src

            sp.wait_ge(x_in, 48)
            for k, first in enumerate(GROUPS):
                if k >= 3:
                    sp.wait_ge(proj_ps, LAST[k - 3] + 1)
                group(k % 3, in_cols, first)
            for b in (1, 2):
                sp.wait_ge(proj_ps, LAST[3 + b] + 1)
                group(b, out_part(1, b - 1), 0)
            sp.wait_ge(proj_ps, 28)
            group(0, out_part(0, 0), 0)
            sp.wait_ge(yh_ps, 8)
            group(1, out_part(0, 1), 0)

            def expert(b, e, free):
                for c in range(NCH):
                    free(c)
                    if b < 2:
                        src = (w1, w3)[b][bass.ds(e, 1)].rearrange("o (p k) n -> p (o k n)", k=KT)
                        src = src[:, CK * GC * c:CK * GC * c + CK * GC]
                    else:
                        src = w2[bass.ds(e, 1)].rearrange("o (c p) n -> p (o c) n", p=P)[:, c, :]
                    sp.dma_start(view(wbuf[b], c * CK * GC, CK * GC), src).then_inc(w_in_sem[b][c], 16)

            for b, done, count in ((2, yh_ps, KT), (0, y_ps, 12), (1, y_ps, KT)):
                sp.wait_ge(done, count)
                expert(b, 0, lambda c: None)
            sp.wait_ge(steps_ready, 1)
            n = step_count(sp)
            with sp.Fori(1, NSTEP) as s:
                with sp.If(s < n):
                    e = sp.value_load(steps_i[0:1, bass.ds(s, 1)], min_val=0, max_val=NE - 1)
                    for b in range(3):
                        expert(b, e, lambda c: sp.wait_ge(w_free[b][c] if c < NCH - 1 else (h1_ps, h3_ps, ye_ps)[b], s))

        @block.gpsimd
        def _(pool):
            pool.memset(misc[:, 1:64], 0.0).then_inc(pool_set, 1)
            pool.memset(eps, EPS).then_inc(pool_set, 1)
            pool.memset(up[:, :, 0:PAST], 0.0).then_inc(pool_set, 1)
            pool.wait_ge(u_ready, 4 + 2)
            pool.wait_ge(k_out, KV_OUT)
            acc = mixT[:, 0:4, TP:T].rearrange("p j (b t) -> p j t b", b=NB)
            tmp = tmpc[:, :].rearrange("p (j t b) -> p j t b", j=4, t=TB)
            v = us[:, 0:4, :].rearrange("p j (r b) -> p j r b", b=NB)
            shape = [P, TB, NB]
            n = 0
            for w in range(CW):
                for j in range(4):
                    if w == 0 and j:
                        pool.wait_ge(u_ready, 4 + j + 1)
                    pool.tensor_scalar(tmp[:, j] if w else acc[:, j], v[:, j, w:w + TB, :], taps[:, j, w:w + 1],
                                       None if w else convb[:, j:j + 1], ALU.mult, ALU.bypass if w else ALU.add
                                       ).then_inc(pchain, 1)
                n += 4
                pool.wait_ge(pchain, n)
                if w:
                    pool.tensor_tensor(acc, acc, tmp, ALU.add).then_inc(pchain, 1)
                    n += 1
                    pool.wait_ge(pchain, n)
            pool.sem_inc(pool_conv, 1)
            pool.wait_ge(yT_v, 12)
            pool.wait_ge(outs, OUTS_MIX)
            pool.memset(reg[:, rt0:R_SIZE], 0.0).then_inc(pool_set, 1)
            pool.memset(pick[:, :, NA:XW], 0.0).then_inc(pool_set, 1)
            pool.memset(ui[:, :], 0).then_inc(pool_set, 1)
            pool.memset(steps_i[:, :], 0).then_inc(pool_set, 1)
            pool.wait_ge(pool_set, 7)
            pool.memset(lg8[:, :, NG:], -3e38).then_inc(pool_set, 1)
            y_rows = y_all.rearrange("t (h c) -> (t h) c", h=2)
            pool.wait_ge(x1_stored, 48)
            pool.wait_ge(rows_ready, 1)
            n = step_count(pool)

            def add_rows(s):
                pool.tensor_copy(idx_now, idx_all[:, bass.ds(s, 1)]).then_inc(idx_set, 1)
                pool.wait_ge(idx_set, s + 1)
                pool.sem_inc(pool_go, 1)
                pool.wait_ge(ye_a, s + 2)
                pool.sem_inc(pool_go, 1)
                pool.wait_ge(ye_v, s + 2)
                pool.sem_inc(pool_go, 1)
                pool.indirect_dma_start(y_rows, bass.IndirectOffsetOnAxis(ap=idx_now, axis=0), ystage, None,
                                        bounds_check=2 * T - 1, oob_is_err=False, compute_op=ALU.add
                                        ).then_inc(ye_out, 16)

            add_rows(0)
            with pool.Fori(1, NSTEP) as s:
                with pool.If(s < n):
                    pool.wait_ge(ye_out, 16 * s)
                    pool.sem_inc(ye_free, 1)
                    add_rows(s)
            pool.wait_ge(ye_out, 16 * n)
            pool.sem_inc(pool_go, 1)

        @block.scalar
        def _(act):
            act.sem_inc(proj_sb, 4)
            act.sem_inc(ye_a, 1)
            act.sem_inc(ye_free, 1)
            act.dma_start(x3[:, 0, :], x_prompt[0:P, :]).then_inc(x_in, 16)
            act.dma_start(x3[:, 1, :], x_prompt[P:TP, :]).then_inc(x_in, 16)
            act.dma_start(x3[0:TS, 2, :], x_sample).then_inc(x_in, 16)
            act.dma_start(cst[:, :], const_small).then_inc(consts_in, 16)
            act.dma_start(g1, norm1_g.rearrange("(p k) -> p k", k=KT)).then_inc(g_in, 16)
            act.dma_start(g2, norm2_g.rearrange("(p k) -> p k", k=KT)).then_inc(g_in, 16)
            act.dma_start(rows_cw, conv_w).then_inc(rows_in, 16)
            for i, v in enumerate((conv_b, conv_norm_g, conv_norm_b)):
                act.dma_start(rows_vec[CJ * i:CJ * i + CJ, :], v.rearrange("(j p) -> j p", p=P)).then_inc(rows_in, 16)
            for i, v in enumerate((q_norm_g, k_norm_g)):
                act.dma_start(rows_vec[24 + i:25 + i, :], v.rearrange("(o p) -> o p", o=1)).then_inc(rows_in, 16)
            act.dma_start(row_sink, attn_sinks.rearrange("(o h) -> o h", o=1)).then_inc(rows_in, 16)
            act.dma_start(state[0:4 * PAST, :, :], state_conv.rearrange("(i b) r c -> (b r) i c", i=2)
                          ).then_inc(state_in, 16)

            act.wait_ge(x_in, 48)
            act.wait_ge(pool_set, 2)
            for i in (0, 2):
                nt = TILES[i][1]
                act.activation(xn[0:nt, i, :], x3[0:nt, i, :], ACT.Square, accum_out=misc[0:nt, 1 + i:2 + i]
                               ).then_inc(x_ms, 1)
            act.wait_ge(x_ms, 3)
            act.activation(misc[:, 4:7], misc[:, 1:4], ACT.Sqrt, bias=eps, scale=1.0 / D).then_inc(x_rstd, 1)
            act.wait_ge(x_rec, 1)
            act.activation(xn[:, 1, :], x3[:, 1, :], ACT.Copy, scale=misc[:, 14:15]).then_inc(xn_mid, 1)
            for j in range(CJ):
                act.wait_ge(st_ps, j // 2 + 1)
                act.wait_ge(small_sb, 1)
                act.activation(us[:, j, 0:NB * PAST].rearrange("p (r b) -> p b r", b=NB),
                               bk(j // 2, 2, NB, PAST)[:, j % 2], ACT.Copy).then_inc(st_sb, 1)
            act.wait_ge(nT_ps, 9)
            act.dma_start(kc, cache_k.rearrange("b s c -> s b c")).then_inc(kc_in, 16)
            act.wait_ge(xn_ready, 2)
            act.dma_start(vc, cache_v.rearrange("b s c -> s b c")).then_inc(vc_in, 16)
            act.dma_start(k_sample[:, 0:W - TB, :], cache_k[:, TB:W, :]).then_inc(outs, 16)
            act.dma_start(v_sample[:, 0:W - TB, :], cache_v[:, TB:W, :]).then_inc(outs, 16)
            act.dma_start(conv_sample[:, 0:PAST - TB, :], state_conv[:, TB:PAST, :]).then_inc(outs, 16)

            def norm_root(r):
                act.wait_ge(ss_ps, r + 1)
                if r >= 2:
                    act.wait_ge(qk_ready, r - 1)
                act.activation(rr[:, r % 2, :], bk(4 + r % 2, T), ACT.Sqrt, bias=eps, scale=1.0 / HD
                               ).then_inc(rt_done, 1)

            def square(r):
                if r >= 2:
                    act.wait_ge(ss_ps, r - 1)
                act.activation(sq[:, r % 2, :], qkT[:, NORM_ORDER[r], :], ACT.Square).then_inc(sq_done, 1)

            def exps(u):
                act.wait_ge(s_max, u + 1)
                k, w = 20 + 8 * (u % 2), 2 if u < 8 else 1
                n = P * (u // 4 + 1) if u < 8 else NKS
                for j in range(w):
                    v = prob[:, (u + 1) % 3, n * j:n * j + n]
                    act.activation(v, v, ACT.Exp, bias=misc[:, k + j:k + j + 1],
                                   accum_out=misc[:, k + 2 + j:k + 3 + j]).then_inc(p_exp, 2 // w)
                act.activation(misc[:, k + 4:k + 4 + w], misc[:, k + 6:k + 6 + w], ACT.Exp).then_inc(p_exp, 1)

            def probs_out(u):
                act.wait_ge(pt_ps, u + 1)
                if u >= 2:
                    act.wait_ge(o_ps, u - 1)
                if u < 8:
                    n = 256 * (u // 4 + 1)
                    act.activation(PT[:, u % 2, 0:n], bk(6, 512)[:, 0:n], ACT.Copy).then_inc(pt_sb, 2)
                else:
                    act.activation(PT[:, u % 2, 0:256], bk(6, 512)[:, 0:256], ACT.Copy).then_inc(pt_sb, 1)
                    act.activation(PT[0:TS, u % 2, 256:512], bank[6][0:TS, 256:512], ACT.Copy).then_inc(pt_sb, 1)

            def heads_out(u):
                act.wait_ge(o_ps, u + 1)
                if u == 0:
                    act.wait_ge(k_out, KV_OUT)
                if u < 8:
                    h = CJ + 2 * (u % 4)
                    act.activation(mixT[:, h:h + 2, P * (u // 4):P * (u // 4) + P], bk(7, 2, P), ACT.Copy).then_inc(o_sb, 1)
                else:
                    t0 = TP + 4 * TB * (u - 8)
                    act.activation(mixT[:, CJ:KT, t0:t0 + 4 * TB].rearrange("p h (b t) -> p b h t", b=4),
                                   bk(7, 4, NH, TB), ACT.Copy).then_inc(o_sb, 1)

            for n in range(28):
                act.wait_ge(proj_ps, n + 1)
                src = bk(n % 4, T)
                if n < 2:
                    act.activation(qkT[:, NH + n, :], src, ACT.Copy).then_inc(proj_sb, 1)
                elif n < 4:
                    act.activation(vT[:, n - 2, :], src, ACT.Copy).then_inc(proj_sb, 1)
                elif n < 12:
                    act.activation(qkT[:, n - 4, :], src, ACT.Copy).then_inc(proj_sb, 1)
                else:
                    j = (n - 12) // 2
                    if j >= 2 and n % 2 == 0:
                        act.wait_ge(u_ready, 4 + j - 1)
                    if n == 12:
                        act.wait_ge(st_ps, 4)
                    act.activation((aT, sgT)[n % 2][:, j % 2, :], src, ACT.Copy if n % 2 == 0 else ACT.Sigmoid
                                   ).then_inc(proj_sb, 1)
                if n in NORM_AT:
                    r = NORM_AT.index(n)
                    act.wait_ge(proj_sb, n + 5)
                    square(r)
                if n - 1 in NORM_AT:
                    norm_root(NORM_AT.index(n - 1))
                if n == 4:
                    act.wait_ge(v_ps, 1)
                    act.activation(vtok[:, 0:2, :].rearrange("p i c -> p (i c)"), bk(6, 512), ACT.Copy).then_inc(v_sb, 1)
                    act.activation(vtok[0:TS, 2, :], bank[7][0:TS, 0:256], ACT.Copy).then_inc(v_sb, 1)
                if n == 6:
                    act.wait_ge(ktok_sb, 2)
                    act.wait_ge(v_sb, 2)
                    act.dma_start(k_prompt, ktok[:, 0, :]).then_inc(k_out, 16)
                    act.dma_start(v_prompt, vtok[:, 1, :]).then_inc(k_out, 16)
                    for b in range(NB):
                        act.dma_start(k_sample[b, W - TB:W, :], ktok[TB * b:TB * b + TB, 1, :]).then_inc(k_out, 16)
                        act.dma_start(v_sample[b, W - TB:W, :], vtok[TB * b:TB * b + TB, 2, :]).then_inc(k_out, 16)
                if 15 <= n < 25:
                    probs_out(n - 15)
                if 16 <= n < 26:
                    heads_out(n - 16)
                if 13 <= n < 23:
                    exps(n - 13)
            act.wait_ge(wr_zero, 1)
            act.wait_ge(o_ps, 10)
            act.dma_start(wr3[:, :, 0:NG], w_router_group.rearrange("(p k) g -> p k g", k=KT)).then_inc(wr_in, 16)
            act.dma_start(wr3[:, :, NG:NG + NE], w_router_expert.rearrange("(p k) g -> p k g", k=KT)).then_inc(wr_in, 16)
            act.dma_start(rbias[:, 0:NG], b_router_group.rearrange("(o g) -> o g", o=1)).then_inc(wr_in, 16)
            act.dma_start(rbias[:, NG:], b_router_expert.rearrange("(o g) -> o g", o=1)).then_inc(wr_in, 16)
            act.dma_start(x3[:, 0, :], x_prompt[0:P, :]).then_inc(x_again, 16)
            act.dma_start(x3[:, 1, :], x_prompt[P:TP, :]).then_inc(x_again, 16)
            act.dma_start(x3[0:TS, 2, :], x_sample).then_inc(x_again, 16)
            def heads_half(m):
                act.wait_ge(yh_ps, m + 1)
                act.activation(part_y[m], bk(m % 4, T), ACT.Copy).then_inc(yh_sb, 1)

            for m in range(5):
                heads_half(m)
            act.wait_ge(utok_sb, 4)
            act.dma_start(conv_prompt, utok[0:PAST, 0, :]).then_inc(outs, 16)
            for t in range(TB):
                act.dma_start(conv_sample[:, PAST - TB + t, :], utok[NB * t:NB * t + NB, 1, :]).then_inc(outs, 16)
            for m in (5, 6):
                heads_half(m)
            act.wait_ge(ln_n, 1)
            act.activation(lsq.rearrange("p j t -> p (j t)"), mixT[:, 0:CJ, :].rearrange("p j t -> p (j t)"), ACT.Square
                           ).then_inc(ln_sq, 1)
            for m in (7, 8, 9):
                heads_half(m)
            act.wait_ge(ln_ps, 2)
            act.activation(lrstd, bk(7, T), ACT.Sqrt, bias=eps, scale=1.0 / DC).then_inc(ln_rt, 1)
            for j in range(CJ):
                act.wait_ge(ln_n, 2 + j // 4)
                act.activation(mixT[:, j, :], mixT[:, j, :], ACT.Silu, bias=lnb[:, j:j + 1], scale=lng[:, j:j + 1]
                               ).then_inc(mix_ready, 1)
                if j == 3:
                    heads_half(10)
            heads_half(11)
            for q in range(4):
                act.wait_ge(y_ps, q + 1)
                act.activation(yT[:, q, :], bk(q, T), ACT.Copy).then_inc(yT_a, 1)

            for q in range(4):
                g = 4 * GROUP_AT[q]
                for i, (t0, nt) in enumerate(TILES):
                    act.wait_ge(x1_part, 3 * q + i + 1)
                    if q or i:
                        act.wait_ge(h2_ms, 3 * q + i)
                    act.activation(sq_junk[0:nt, :], x3[0:nt, i, P * g:P * g + 512], ACT.Square,
                                   accum_out=misc[0:nt, 50 + 4 * i + q:51 + 4 * i + q]).then_inc(h2_ms, 1)
            act.wait_ge(outs, OUTS_MIX)
            for f in range(1, 8, 2):
                i, q = f // 4, f % 4
                act.wait_ge(x1T_ps, f + 1)
                act.activation(x1T[:, 4 * q:4 * q + 4, P * i:P * i + P], bk(4 + f % 4, 4, P), ACT.Copy).then_inc(x1T_a, 1)
            act.wait_ge(h2_sum, 1)
            act.activation(misc[:, 10:13], misc[:, 7:10], ACT.Sqrt, bias=eps, scale=1.0 / D).then_inc(h2_rt, 1)
            act.wait_ge(h2_rec, 1)
            act.wait_ge(outs, OUTS_MIX)
            for i, (t0, nt) in enumerate(TILES):
                act.wait_ge(x1_part, 12)
                act.dma_start(y_all[t0:t0 + nt, :], x3[0:nt, i, :]).then_inc(x1_stored, 16)
            for i, (t0, nt) in enumerate(TILES):
                act.activation(h2[0:nt, i, :].rearrange("t (k p) -> t k p", k=KT),
                               x3[0:nt, i, :].rearrange("t (p k) -> t k p", k=KT), ACT.Copy,
                               scale=misc[0:nt, 13 + i:14 + i]).then_inc(h2_ready, 1)
            act.wait_ge(r_sub, 1)
            act.activation(expd, expd, ACT.Exp).then_inc(r_exp, 1)

            def tokens_out(s, part_, done):
                act.wait_ge(xd_ps, 2 * s + 1 + part_)
                act.activation(xd[:, 512 * part_:512 * part_ + 512], bk(4 + part_, 512), ACT.Copy).then_inc(done, 1)

            def output(s):
                act.wait_ge(rows_ready, 1)
                act.wait_ge(ye_ps, s)
                act.wait_ge(ye_free, s)
                act.activation(ystage[:, 0:512], bk(2, 512), ACT.Copy, scale=gate_of[:, bass.ds(s - 1, 1)]
                               ).then_inc(ye_a, 1)

            def swish(s):
                act.wait_ge(h1_ps, s + 1)
                act.wait_ge(hg_ready, s + 1)
                act.activation(h1s, bk(0, 256), ACT.Silu).then_inc(h1_sb, 1)

            act.wait_ge(x1_stored, 48)
            act.wait_ge(h2_ready, 3)
            tokens_out(0, 0, xd_a)
            tokens_out(0, 1, xd_v)
            swish(0)
            act.wait_ge(steps_ready, 1)
            n = step_count(act)
            with act.Fori(1, NSTEP + 1) as s:
                with act.If(s < n + 1):
                    with act.If(s < n):
                        tokens_out(s, 0, xd_a)
                    output(s)
                    with act.If(s < n):
                        swish(s)
            act.wait_ge(k_out, KV_OUT)

        @block.tensor
        def _(pe):
            def turn(out, in_):
                k = in_.shape[0]
                return pe.transpose(out, in_, ident[0:k, 0:k])

            pe.wait_ge(consts_in, 16)
            f = 0
            for i, (t0, nt) in enumerate(TILES):
                pe.wait_ge((xn_ready, xn_mid, xn_ready)[i], (1, 1, 2)[i])
                per = 512 // nt
                for q in range(KT // per):
                    if f >= 4:
                        pe.wait_ge(nT_sb, f - 3)
                    for k in range(per):
                        ins = turn(bk(3 + f % 4, nt, at=nt * k),
                                   xn[0:nt, i, :].rearrange("t (p k) -> t k p", k=KT)[:, per * q + k, :])
                    ins.then_inc(nT_ps, 1)
                    f += 1
            pe.wait_ge(rows_in, 16 * 7)
            turn(bk(7, 26), rows_vec)
            for j in range(CJ):
                turn(bk(7, CW, at=32 + CW * j), rows_cw[:, P * j:P * j + P])
            pe.matmul(bk(7, NH, at=32 + CJ * CW), ones[0:1, :], row_sink, start=True, stop=True).then_inc(small_ps, 1)
            pe.wait_ge(state_in, 16)
            pe.wait_ge(nT_sb, 9)
            for j in range(CJ):
                for i in range(2):
                    ins = turn(bk(j // 2, 4 * PAST, at=8 * PAST * (j % 2) + 4 * PAST * i),
                               state[0:4 * PAST, i, P * j:P * j + P])
                if j % 2:
                    ins.then_inc(st_ps, 1)

            def project(b, m, out, rhs, done):
                w = view(wbuf[b], 0, KT, GC)
                for k in range(KT):
                    ins = pe.matmul(bk(out, T), w[:, k, P * m:P * m + P], rhs[:, k, :], start=(k == 0),
                                    stop=(k == KT - 1))
                ins.then_inc(done, 1)

            def scores(u):
                if u >= 2:
                    pe.wait_ge(s_sb, u - 1)
                else:
                    pe.wait_ge(rt_done, NH + NKV)
                    pe.wait_ge(kc_sb, 4)
                if u < 8:
                    pe.wait_ge(qk_ready, 4 + 2 * (u % 4))
                    n, kw = u // 4, P * (u // 4 + 1)
                    for j in range(2):
                        h = 2 * (u % 4) + j
                        ins = pe.matmul(bk(4 + u % 2, kw, at=kw * j), qkT[:, h, P * n:P * n + P],
                                        qkT[:, NH + h // GQA, 0:kw], start=True, stop=True)
                else:
                    pe.wait_ge(qk_ready, NH + NKV + 1)
                    for bb in range(4):
                        q = qs[:, 4 * (u - 8) + bb, :]
                        pe.matmul(bank[4 + u % 2][32 * bb:32 * bb + 32, 0:NKV * W], q, keysT[:, 4 * (u - 8) + bb, :],
                                  start=True, stop=True)
                        ins = pe.matmul(bank[4 + u % 2][32 * bb:32 * bb + 32, NKV * W:NKS], q,
                                        qkT[:, NH:NH + NKV, TP:T], start=True, stop=True)
                ins.then_inc(s_ps, 1)

            def turn_probs(u):
                pe.wait_ge(p_ready, u + 1)
                if u:
                    pe.wait_ge(pt_sb, 2 * u)
                else:
                    pe.wait_ge(ktok_sb, 2)
                    pe.wait_ge(v_sb, 2)
                    pe.wait_ge(kc_sb, 4)
                if u < 8:
                    for j in range(2 * (u // 4 + 1)):
                        ins = turn(bk(6, P, at=P * j), prob[:, (u + 1) % 3, P * j:P * j + P])
                else:
                    for kv in range(NKV):
                        turn(bk(6, P, at=P * kv), prob[:, (u + 1) % 3, W * kv:W * kv + W])
                        ins = turn(bank[6][0:TS, 256 + P * kv:256 + P * kv + P],
                                   prob[:, (u + 1) % 3, NKV * W + TS * kv:NKV * W + TS * kv + TS])
                ins.then_inc(pt_ps, 1)

            def values(u):
                pe.wait_ge(pt_sb, 2 * u + 2)
                if u >= 1:
                    pe.wait_ge(o_sb, u)
                if u < 8:
                    nb = u // 4 + 1
                    for j in range(2):
                        h = 2 * (u % 4) + j
                        for k in range(nb):
                            ins = pe.matmul(bk(7, P, at=P * j), vtok[:, k, HD * (h // GQA):HD * (h // GQA) + HD],
                                            PT[:, u % 2, P * (nb * j + k):P * (nb * j + k) + P],
                                            start=(k == 0), stop=(k == nb - 1))
                else:
                    pe.wait_ge(vc_in, 16)
                    for kv in range(NKV):
                        pe.matmul(bk(7, P), vtok[0:TS, 2, HD * kv:HD * kv + HD],
                                  PT[0:TS, u % 2, 256 + P * kv:256 + P * kv + P], start=(kv == 0), stop=False,
                                  skip_group_check=True)
                    for bb in range(4):
                        for kv in range(NKV):
                            ins = pe.matmul(bk(7, 32, at=32 * bb), vc[:, 4 * (u - 8) + bb, HD * kv:HD * kv + HD],
                                            PT[:, u % 2, P * kv + 32 * bb:P * kv + 32 * bb + 32], start=False,
                                            stop=(kv == NKV - 1), skip_group_check=True)
                ins.then_inc(o_ps, 1)

            pe.wait_ge(nT_sb, 9)
            pe.wait_ge(st_sb, CJ)
            pe.wait_ge(small_sb, 1)
            for n, (g, m) in enumerate(TILE):
                if m == 0:
                    for c in range(NCH):
                        pe.wait_ge(w_in_sem[g % 3][c], 16 * (g // 3 + 1))
                pe.wait_ge(proj_sb, n + 1)
                project(g % 3, m, n % 4, nT, proj_ps)
                if n - 1 in NORM_AT:
                    r = NORM_AT.index(n - 1)
                    pe.wait_ge(sq_done, r + 1)
                    if r >= 2:
                        pe.wait_ge(rt_done, r - 1)
                    pe.matmul(bk(4 + r % 2, T), ones, sq[:, r % 2, :], start=True, stop=True).then_inc(ss_ps, 1)
                if n == 3:
                    pe.wait_ge(proj_sb, 4 + 4)
                    for i, (t0, nt) in enumerate(TILES):
                        for kv in range(NKV):
                            ins = turn(bank[6 + i // 2][0:nt, 256 * (i % 2) + P * kv:256 * (i % 2) + P * kv + P],
                                       vT[:, kv, t0:t0 + nt])
                    ins.then_inc(v_ps, 1)
                if n == 5:
                    pe.wait_ge(qk_ready, 2)
                    pe.wait_ge(v_sb, 2)
                    for kv in range(NKV):
                        turn(bank[6][:, P * kv:P * kv + P], qkT[:, NH + kv, P:2 * P])
                        ins = turn(bank[6][0:TS, 256 + P * kv:256 + P * kv + P], qkT[:, NH + kv, TP:T])
                    ins.then_inc(ktok_ps, 1)
                if n in (7, 9):
                    q0 = n - 7
                    if n == 7:
                        pe.wait_ge(kc_in, 16)
                        pe.wait_ge(ktok_sb, 2)
                    else:
                        pe.wait_ge(kc_sb, 2)
                    for q in (q0, q0 + 1):
                        for b in range(2):
                            for kv in range(NKV):
                                ins = turn(bk(6 + q % 2, P, at=256 * b + 128 * kv), kc[:, 2 * q + b, P * kv:P * kv + P])
                        ins.then_inc(kc_ps, 1)
                if 12 <= n < 22:
                    scores(n - 12)
                if 15 <= n < 25:
                    turn_probs(n - 15)
                if 16 <= n < 26:
                    values(n - 16)

            def half_product(b, landed, m, out, rows_, first):
                for c in range(NCH):
                    pe.wait_ge(w_in_sem[b][c], landed)
                w = view(wbuf[b], 0, CJ, 2 * GC)
                for k in range(CJ):
                    ins = pe.matmul(bk(out, T), w[:, k, P * (m % 8):P * (m % 8) + P], mixT[:, rows_ + k, :],
                                    start=(first and k == 0), stop=(k == CJ - 1), skip_group_check=True)
                return ins

            pe.wait_ge(o_sb, 10)
            for m in range(KT):
                pe.wait_ge(proj_sb, 4 + 24 + m % 4 + 1)
                if m >= 4:
                    pe.wait_ge(yh_sb, m - 3)
                half_product(1 + m // 8, 48, m, m % 4, CJ, True).then_inc(yh_ps, 1)
                if m == 0:
                    pe.wait_ge(u_ready, 4 + CJ)
                    for j in range(CJ):
                        turn(bank[4 + j // 4][0:PAST, P * (j % 4):P * (j % 4) + P], up[:, j, TP:TP + PAST])
                        ins = turn(bank[6 + j // 4][0:TS, P * (j % 4):P * (j % 4) + P], us[:, j, NB * PAST:])
                    ins.then_inc(utok_ps, 1)
                if m == 6:
                    pe.wait_ge(utok_sb, 4)
                    pe.wait_ge(ln_red, 1)
                    pe.matmul(bk(6, T), ones, lsum, start=True, stop=True).then_inc(ln_ps, 1)
                if m == 9:
                    pe.wait_ge(ln_red, 2)
                    pe.matmul(bk(7, T), ones, lsum, start=True, stop=True).then_inc(ln_ps, 1)
            pe.wait_ge(ln_rt, 1)
            pe.wait_ge(mix_ready, CJ)

            def turn_back(q):
                pe.wait_ge(yT_a, 4)
                if q:
                    pe.wait_ge(yT_v, 4 * q)
                    pe.wait_ge(x1_part, 3 * q)
                for i, (t0, nt) in enumerate(TILES):
                    for j in range(4):
                        ins = turn(bank[(6, 7, 3)[i]][0:nt, P * j:P * j + P], yT[:, 4 * (q % 2) + j, t0:t0 + nt])
                ins.then_inc(yt_ps, 1)

            for q in range(KT):
                m = 4 * GROUP_AT[q // 4] + q % 4
                if 6 <= q < 9:
                    pe.wait_ge(yT_a, q - 5)
                if q >= 9:
                    pe.wait_ge(yT_v, q - 8)
                half_product(m // 8, 64, m, OUT_BANK[q], 0, q >= 4).then_inc(y_ps, 1)
                if q >= 4 and q % 4 == 0:
                    turn_back(q // 4 - 1)
            turn_back(3)
            def logits_by_column(i):
                t0, nt = TILES[i]
                pe.wait_ge(x1T_v, (2, 4, 5)[i])
                pe.wait_ge(x1T_a, (2, 4, 4)[i])
                for k in range(KT):
                    o = bank[(0, 1, 3)[i]][RC * (k % 2):RC * (k % 2) + RC, 0:nt]
                    ins = pe.matmul(o, wr3[:, k, :], x1T[:, k, t0:t0 + nt], start=(k < 2), stop=(k >= KT - 2),
                                    skip_group_check=True)
                ins.then_inc(lT_ps, 1)

            pe.wait_ge(x1_part, 12)
            pe.wait_ge(wr_gain, 1)
            f = 0
            for i, (t0, nt) in enumerate(TILES):
                per = 512 // nt
                for q in range(KT // per):
                    if f >= 4:
                        pe.wait_ge(x1T_a if f % 2 else x1T_v, f // 2 - 1)
                    for k in range(per):
                        ins = turn(bk(4 + f % 4, nt, at=nt * k),
                                   x3[0:nt, i, :].rearrange("t (p k) -> t k p", k=KT)[:, per * q + k, :])
                    ins.then_inc(x1T_ps, 1)
                    f += 1
                if i:
                    logits_by_column(i - 1)
            logits_by_column(2)
            pe.matmul(bk(2, NG + NE, at=3 * RC), ones[0:1, :], rbias, start=True, stop=True)
            for i, (t0, nt) in enumerate(TILES):
                pe.wait_ge(lT_sb, i + 1)
                o = bank[2][0:nt, RC * i:RC * i + NG + NE]
                for h in range(2):
                    ins = pe.matmul(o, lT[:, t0:t0 + nt], ident[:, RC * h:RC * h + NG + NE], start=(h == 0), stop=(h == 1))
            ins.then_inc(lg_ps, 1)
            for i in range(8):
                pe.matmul(bk(7, 512), ones, row[:, 0:512], start=True, stop=True)
            pe.wait_ge(hot_ready, 1)
            for i, (t0, nt) in enumerate(TILES):
                o = bank[1][0:nt, NE * i:NE * i + NE]
                for j in range(i):
                    pe.matmul(o, ones[:, 0:nt], hot[:, j, :], start=(j == 0), stop=False)
                ins = pe.matmul(o, tri[0:nt, 0:nt], hot[0:nt, i, :], start=(i == 0), stop=True)
            ins.then_inc(rank_ps, 1)
            for i, (t0, nt) in enumerate(TILES):
                ins = pe.matmul(bank[3][:, 0:NE], ones[0:nt, :], hot[0:nt, i, :], start=(i == 0), stop=(i == 2))
            ins.then_inc(cnt_ps, 1)
            for i in range(2):
                pe.matmul(bk(7, 512), ones, row[:, 0:512], start=True, stop=True)
            def dispatch(s):
                pe.wait_ge(window_ready, 3 * s + 3)
                for part_ in range(2):
                    for i, (t0, nt) in enumerate(TILES):
                        for half_ in range(2):
                            at = 1024 * half_ + 512 * part_
                            ins = pe.matmul(bank[4 + part_][BLK * half_:BLK * half_ + BLK, :], window[0:nt, i, :],
                                            h2[0:nt, i, at:at + 512], start=(i == 0), stop=(i == 2))
                    ins.then_inc(xd_ps, 1)

            def turn_tokens(s):
                for part_, done in ((0, xd_a), (1, xd_v)):
                    pe.wait_ge(done, s + 1)
                    for j in range(4):
                        c = 4 * part_ + j
                        ins = turn(bk(4 + part_, P, at=P * j), xd[:, P * c:P * c + P])
                    ins.then_inc(xw_ps, 1)

            def head(s):
                pe.wait_ge(xw_ready, 2 * s + 2)
                for b in range(2):
                    done = (h1_ps, h3_ps)[b]
                    base = W_BEFORE[b] + 16
                    w = view(wbuf[b], 0, KT, GC)
                    pe.wait_ge(hg_ready, s + 1)
                    for c in range(NCH):
                        pe.wait_ge(w_in_sem[b][c], base + 16 * s)
                        for k in range(CK * c, CK * c + CK):
                            for half_ in range(2):
                                ins = pe.matmul(bank[b][BLK * half_:BLK * half_ + BLK, 0:256], xw[:, 2 * (k % 8) + k // 8, :],
                                                w[:, k, 256 * half_:256 * half_ + 256], start=(k == 0),
                                                stop=(k == KT - 1))
                        if c < NCH - 1:
                            ins.then_inc(w_free[b][c], 1)
                    ins.then_inc(done, 1)

            def turn_hidden(s):
                pe.wait_ge(hg_ready, s + 1)
                for j in range(2):
                    ins = turn(bk(6, P, at=P * j), hg[:, P * j:P * j + P])
                ins.then_inc(hT_ps, 1)

            def expert_out(s):
                pe.wait_ge(hT_ready, s)
                pe.wait_ge(rows_ready, 1)
                pe.wait_ge(ye_a, s)
                pe.wait_ge(ye_v, s)
                w = view(wbuf[2], 0, NCH, D)
                for c in range(NCH):
                    pe.wait_ge(w_in_sem[2][c], W_BEFORE[2] + 16 * s)
                    for part_ in range(2):
                        for half_ in range(2):
                            ins = pe.matmul(bank[2 + part_][BLK * half_:BLK * half_ + BLK, :], hT[:, c % 2, c // 2, :],
                                            w[:, c, 1024 * half_ + 512 * part_:1024 * half_ + 512 * part_ + 512],
                                            start=(c == 0), stop=(c == NCH - 1))
                    if c < NCH - 1:
                        ins.then_inc(w_free[2][c], 1)
                ins.then_inc(ye_ps, 1)

            pe.wait_ge(h2_ready, 3)
            dispatch(0)
            pe.wait_ge(tab_ready, 1)
            for j in range(2):
                ins = pe.matmul(bank[2][0:1, 64 * j:64 * j + NSTEP], tab[0:NSTEP, j:j + 1],
                                ident[0:NSTEP, 0:NSTEP], start=True, stop=True)
            ins.then_inc(tab_ps, 1)
            turn_tokens(0)
            pe.wait_ge(ranks_read, 1)
            head(0)
            pe.wait_ge(steps_ready, 1)
            for i, (t0, nt) in enumerate(TILES):
                pe.wait_ge(ohs_ready, i + 1)
                for c in range(2):
                    ins = pe.matmul(bk(2, 3 * NSTEP, at=128), ohr[0:nt, 2 * i + c, :], ohs[0:nt, 2 * i + c, :],
                                    start=(i == 0 and c == 0), stop=(i == 2 and c == 1))
            ins.then_inc(rows_ps, 1)
            n = step_count(pe)
            with pe.Fori(1, NSTEP + 1) as s:
                with pe.If(s < n + 1):
                    with pe.If(s < n):
                        dispatch(s)
                        turn_tokens(s)
                    turn_hidden(s)
                    expert_out(s)
                    with pe.If(s < n):
                        head(s)

        @block.vector
        def _(dve):
            dve.sem_inc(u_ready, 4)
            dve.sem_inc(hg_ready, 1)
            dve.sem_inc(ye_v, 1)
            count = [0]

            def link(ins):
                count[0] += 1
                ins.then_inc(dchain, 1)
                dve.wait_ge(dchain, count[0])

            def mul(out, a, b):
                return dve.tensor_tensor(out, a, b, ALU.mult)

            def add(out, a, b):
                return dve.tensor_tensor(out, a, b, ALU.add)

            dve.wait_ge(x_in, 48)
            dve.wait_ge(pool_set, 2)
            dve.tensor_tensor_reduce(xn[:, 1, :], x3[:, 1, :], x3[:, 1, :], 1.0, 0.0, ALU.mult, ALU.add, misc[:, 2:3]
                                     ).then_inc(x_ms, 1)
            dve.wait_ge(x_rstd, 1)
            dve.reciprocal(misc[:, 13:16], misc[:, 4:7]).then_inc(x_rec, 1)
            dve.wait_ge(x_rec, 1)
            for i in (0, 2):
                nt = TILES[i][1]
                dve.tensor_scalar(xn[0:nt, i, :], x3[0:nt, i, :], misc[0:nt, 13 + i:14 + i], None, ALU.mult
                                  ).then_inc(xn_ready, 1)
            f = 0
            dve.wait_ge(g_in, 32)
            for i, (t0, nt) in enumerate(TILES):
                per = 512 // nt
                for q in range(KT // per):
                    dve.wait_ge(nT_ps, f + 1)
                    mul(nT[:, per * q:per * q + per, t0:t0 + nt], bk(3 + f % 4, per, nt),
                        g1[:, per * q:per * q + per].unsqueeze(2).to_broadcast([P, per, nt])).then_inc(nT_sb, 1)
                    f += 1
            dve.wait_ge(small_ps, 1)
            link(dve.tensor_copy(small[:, 0:26], bk(7, 26)))
            link(dve.tensor_copy(small[:, 32:], bk(7, CJ * CW + NH, at=32)))
            link(dve.tensor_scalar(small[:, 24:25], small[:, 24:25], SCALE, None, ALU.mult))
            dve.wait_ge(consts_in, 16)
            link(mul(misc[:, 40:48], sinks, hsel))
            dve.tensor_reduce(misc[:, 48:49], misc[:, 40:48], AX.X, ALU.add).then_inc(small_sb, 1)

            def norm(r):
                h = NORM_ORDER[r]
                dve.wait_ge(rt_done, r + 1)
                link(dve.reciprocal(rr[:, r % 2, :], rr[:, r % 2, :]))
                dve.scalar_tensor_tensor(qkT[:, h, :], qkT[:, h, :], qg if h < NH else kg, rr[:, r % 2, :],
                                         ALU.mult, ALU.mult).then_inc(qk_ready, 1)

            def logits(u):
                k = 20 + 8 * (u % 2)
                dve.wait_ge(s_ps, u + 1)
                if u >= 3:
                    dve.wait_ge(pt_ps, u - 2)
                if u < 8:
                    kw, w, h = P * (u // 4 + 1), 2, 2 * (u % 4)
                    v = prob[:, (u + 1) % 3, 0:2 * kw].rearrange("p (h k) -> p h k", h=2)
                    sk = sinks[:, h:h + 2]
                    for j in range(2):
                        ins = dve.scalar_tensor_tensor(v[:, j, :], dist[:, 2 * P - kw:2 * P], -SLOPES[h + j],
                                                       bk(4 + u % 2, kw, at=kw * j), ALU.mult, ALU.add)
                else:
                    w, v, sk = 1, prob[:, (u + 1) % 3, 0:NKS], misc[:, 48:49]
                    ins = add(v, bk(4 + u % 2, NKS), sbias[:, u - 8, :])
                ins.then_inc(s_sb, 1)
                m = misc[:, 36 + 2 * (u % 2):36 + 2 * (u % 2) + w]
                dve.wait_ge(s_sb, u + 1)
                link(dve.tensor_reduce(m, v, AX.X, ALU.max))
                link(dve.tensor_tensor(m, m, sk, ALU.max))
                link(dve.tensor_scalar(misc[:, k:k + w], m, -1.0, None, ALU.mult))
                dve.tensor_tensor(misc[:, k + 6:k + 6 + w], sk, m, ALU.subtract).then_inc(s_max, 1)

            def normalise(u):
                k, w = 20 + 8 * (u % 2), 2 if u < 8 else 1
                dve.wait_ge(p_exp, 3 * u + 3)
                den = misc[:, k + 2:k + 2 + w]
                link(add(den, den, misc[:, k + 4:k + 4 + w]))
                link(dve.reciprocal(den, den))
                if u < 8:
                    kw = P * (u // 4 + 1)
                    v = prob[:, (u + 1) % 3, 0:2 * kw].rearrange("p (h k) -> p h k", h=2)
                    mul(v, v, den.unsqueeze(2).to_broadcast([P, 2, kw])).then_inc(p_ready, 1)
                else:
                    v = prob[:, (u + 1) % 3, 0:NKS]
                    dve.tensor_scalar(v, v, den, None, ALU.mult).then_inc(p_ready, 1)

            convs = [0]

            def glu(j):
                dve.wait_ge(proj_sb, 4 + 12 + 2 * j + 2)
                mul(up[:, j, PAST:PAST + TP], aT[:, j % 2, 0:TP], sgT[:, j % 2, 0:TP])
                mul(us[:, j, NB * PAST:].rearrange("p (r b) -> p r b", b=NB),
                    aT[:, j % 2, TP:T].rearrange("p (b r) -> p r b", b=NB),
                    sgT[:, j % 2, TP:T].rearrange("p (b r) -> p r b", b=NB)).then_inc(u_ready, 1)
                dve.wait_ge(u_ready, 4 + j + 1)

            def conv(j, taps_):
                srcs = [(slice(0, TP), lambda v: v, lambda w: up[:, j, w:w + TP])]
                if j >= 4:
                    srcs.append((slice(TP, T), lambda v: v.rearrange("p (b t) -> p t b", b=NB),
                                 lambda w: us[:, j, NB * w:NB * (w + TB)].rearrange("p (t b) -> p t b", b=NB)))
                for w in taps_:
                    if w == 1 and j:
                        dve.wait_ge(conv_done, j)
                    for part_, shaped, src in srcs:
                        acc = shaped((odd_taps if w % 2 else mixT[:, j, :])[:, part_])
                        if w >= 2:
                            dve.wait_ge(cchain, convs[0] - 2 * len(srcs) + 1)
                            ins = dve.scalar_tensor_tensor(acc, src(w), taps[:, j, w:w + 1], acc, ALU.mult, ALU.add)
                        else:
                            ins = dve.tensor_scalar(acc, src(w), taps[:, j, w:w + 1], None if w else convb[:, j:j + 1],
                                                    ALU.mult, ALU.bypass if w else ALU.add)
                        ins.then_inc(cchain, 1)
                        convs[0] += 1
                if taps_[-1] == CW - 1:
                    n = TP if j < 4 else T
                    dve.wait_ge(cchain, convs[0])
                    add(mixT[:, j, 0:n], mixT[:, j, 0:n], odd_taps[:, 0:n]).then_inc(conv_done, 1)

            for n in range(28):
                if n - 2 in NORM_AT:
                    norm(NORM_AT.index(n - 2))
                if n == 6:
                    dve.wait_ge(ktok_ps, 1)
                    dve.tensor_copy(ktok[:, 0, :], bank[6][:, 0:256]).then_inc(ktok_sb, 1)
                    dve.tensor_copy(ktok[0:TS, 1, :], bank[6][0:TS, 256:512]).then_inc(ktok_sb, 1)
                if n in (8, 10):
                    for q in (n - 8, n - 7):
                        dve.wait_ge(kc_ps, q + 1)
                        dve.tensor_copy(keysT[:, 2 * q:2 * q + 2, :].rearrange("p b k -> p (b k)"), bk(6 + q % 2, 512)
                                        ).then_inc(kc_sb, 1)
                if n == 14:
                    dve.wait_ge(pool_set, 3)
                    dve.wait_ge(k_out, KV_OUT)
                    dve.wait_ge(qk_ready, NH + NKV)
                    for b in range(NB):
                        ins = dve.tensor_copy(qs[:, b, :].rearrange("p (h t) -> p h t", h=NH),
                                              qkT[:, 0:NH, TP + TB * b:TP + TB * b + TB])
                    ins.then_inc(qk_ready, 1)
                if n >= 14 and n % 2 == 0:
                    glu((n - 14) // 2)
                if 13 <= n < 23:
                    logits(n - 13)
                if 14 <= n < 24:
                    normalise(n - 14)
                if n >= 14:
                    conv((n - 14) // 2, range(0, 16) if n % 2 == 0 else range(16, CW))
            glu(7)
            dve.memset(wr3, 0.0).then_inc(wr_zero, 1)
            conv(7, range(0, 16))
            dve.wait_ge(utok_ps, 1)
            for g in range(2):
                dve.tensor_copy(utok[0:PAST, 0, 512 * g:512 * g + 512], bank[4 + g][0:PAST, :]).then_inc(utok_sb, 1)
                dve.tensor_copy(utok[0:TS, 1, 512 * g:512 * g + 512], bank[6 + g][0:TS, :]).then_inc(utok_sb, 1)
            conv(7, range(16, CW))

            dve.wait_ge(conv_done, CJ)
            dve.wait_ge(pool_conv, 1)
            dve.tensor_reduce(lsum, mixT[:, 0:CJ, :].rearrange("p j t -> p t j"), AX.X, ALU.add).then_inc(ln_red, 1)
            dve.wait_ge(ln_ps, 1)
            link(dve.tensor_scalar(lmean, bk(6, T), 1.0 / DC, None, ALU.mult))
            dve.tensor_tensor(mixT[:, 0:CJ, :], mixT[:, 0:CJ, :], lmean.unsqueeze(1).to_broadcast([P, CJ, T]),
                              ALU.subtract).then_inc(ln_n, 1)
            dve.wait_ge(ln_sq, 1)
            dve.tensor_reduce(lsum, lsq.rearrange("p j t -> p t j"), AX.X, ALU.add).then_inc(ln_red, 1)
            dve.wait_ge(ln_rt, 1)
            link(dve.reciprocal(lrstd, lrstd))
            for q in range(2):
                v = mixT[:, 4 * q:4 * q + 4, :]
                mul(v, v, lrstd.unsqueeze(1).to_broadcast([P, 4, T])).then_inc(ln_n, 1)

            dve.wait_ge(wr_in, 64)
            mul(wr3, wr3, g2.unsqueeze(2).to_broadcast([P, KT, RC])).then_inc(wr_gain, 1)

            dve.wait_ge(x_again, 48)

            def residual(q):
                dve.wait_ge(yt_ps, q + 1)
                g = GROUP_AT[q]
                for i, (t0, nt) in enumerate(TILES):
                    xs = x3[0:nt, i, 512 * g:512 * g + 512]
                    add(xs, xs, bank[(6, 7, 3)[i]][0:nt, :]).then_inc(x1_part, 1)

            for q in range(4, KT):
                dve.wait_ge(y_ps, q + 1)
                add(yT[:, q % 8, :], bk(OUT_BANK[q], T), part_y[q - 4]).then_inc(yT_v, 1)
                if q % 4 == 0:
                    residual(q // 4 - 1)
            residual(3)
            dve.wait_ge(outs, OUTS_MIX)
            f = 0
            for i, (t0, nt) in enumerate(TILES):
                per = 512 // nt
                for q in range(KT // per):
                    if f % 2 == 0:
                        dve.wait_ge(x1T_ps, f + 1)
                        dve.tensor_copy(x1T[:, per * q:per * q + per, t0:t0 + nt], bk(4 + f % 4, per, nt)).then_inc(x1T_v, 1)
                    f += 1
                    if f == 5:
                        dve.wait_ge(h2_ms, 12)
                        dve.tensor_reduce(misc[:, 7:10], misc[:, 50:62].rearrange("p (i g) -> p i g", i=3), AX.X, ALU.add
                                          ).then_inc(h2_sum, 1)
                    if f == 8:
                        dve.wait_ge(h2_rt, 1)
                        link(dve.tensor_scalar(misc[:, 13:16], misc[:, 10:13], 1e-30, None, ALU.max))
                        dve.reciprocal(misc[:, 13:16], misc[:, 13:16]).then_inc(h2_rec, 1)

            def over(i):
                return slice(0, TILES[i][1])

            def all3(v):
                return v.rearrange("p (i e) -> p i e", i=3)

            dve.wait_ge(h2_rec, 1)
            for i, (t0, nt) in enumerate(TILES):
                dve.wait_ge(lT_ps, i + 1)
                dve.tensor_copy(lT[:, t0:t0 + nt], bank[(0, 1, 3)[i]][:, 0:nt]).then_inc(lT_sb, 1)
            dve.wait_ge(pool_set, 8)
            dve.tensor_copy(g2w.rearrange("p (c h) -> p c h", h=2), g2.rearrange("p (h c) -> p c h", h=2))
            dve.wait_ge(lg_ps, 1)
            link(dve.tensor_copy(rbc, bk(2, NG + NE, at=3 * RC)))
            for i in range(3):
                for out, a, w in ((lg8, 0, NG), (le, NG, NE)):
                    ins = dve.scalar_tensor_tensor(out[over(i), i, 0:w], bank[2][over(i), RC * i + a:RC * i + a + w],
                                                   misc[over(i), 13 + i:14 + i], rbc[over(i), a:a + w], ALU.mult, ALU.add)
            link(ins)
            for i in range(3):
                ins = dve.max(mg[over(i), i, :], lg8[over(i), i, :])
            link(ins)
            for i in range(3):
                ins = dve.max_index(ui[over(i), 8 * i:8 * i + 8], mg[over(i), i, :], lg8[over(i), i, :])
            link(ins)
            link(dve.tensor_copy(gf, all3(ui[:, 0:24])[:, :, 0]))
            link(dve.tensor_tensor(gone, row[:, 0:NG].unsqueeze(1).to_broadcast([P, 3, NG]),
                                   gf.unsqueeze(2).to_broadcast([P, 3, NG]), ALU.is_equal))
            for i in range(3):
                ins = mul(prod[:, i, :].rearrange("p (g e) -> p g e", g=NG), le[:, i, :].rearrange("p (g e) -> p g e", g=NG),
                          gone[:, i, :].unsqueeze(2).to_broadcast([P, NG, EG]))
            link(ins)
            for i in range(3):
                ins = dve.tensor_reduce(ein[:, i, :], prod[:, i, :].rearrange("p (g e) -> p e g", g=NG), AX.X, ALU.add)
            link(ins)
            for i in range(3):
                ins = dve.max(me[over(i), i, :], ein[over(i), i, :])
            link(ins)
            for i in range(3):
                ins = dve.max_index(ui[over(i), 24 + 8 * i:32 + 8 * i], me[over(i), i, :], ein[over(i), i, :])
            link(ins)
            for e, c in ((e1, 0), (e2, 1)):
                ins = dve.tensor_copy(e, all3(ui[:, 24:48])[:, :, c])
            link(ins)
            for e in (e1, e2):
                ins = dve.scalar_tensor_tensor(e, gf, float(EG), e, ALU.mult, ALU.add)
            link(ins)
            for h, e in ((hot1, e1), (hot2, e2)):
                ins = dve.tensor_tensor(h, row[:, 0:NE].unsqueeze(1).to_broadcast([P, 3, NE]),
                                        e.unsqueeze(2).to_broadcast([P, 3, NE]), ALU.is_equal)
            link(ins)
            add(hot, hot1, hot2).then_inc(hot_ready, 1)
            dg = expd.rearrange("p (i c) -> p i c", i=3)
            dve.tensor_tensor(dg[:, :, 0:NG], lg8[:, :, 0:NG], mg[:, :, 0:1].to_broadcast([P, 3, NG]), ALU.subtract)
            dve.tensor_tensor(dg[:, :, NG:NG + 1], me[:, :, 1:2], me[:, :, 0:1], ALU.subtract).then_inc(r_sub, 1)
            dve.wait_ge(rank_ps, 1)
            for i in range(3):
                ins = dve.tensor_copy(rank0[over(i), i:i + 1], bank[1][over(i), NE * i:NE * i + 1])
            link(ins)
            for i in range(3):
                dve.tensor_scalar(window[over(i), i, :], row[over(i), 0:BLK], rank0[over(i), i:i + 1],
                                  hot[over(i), i, 0:1], ALU.is_equal, ALU.mult).then_inc(window_ready, 1)
            dve.wait_ge(cnt_ps, 1)
            link(dve.tensor_copy(cnt, bk(3, NE)))
            dve.tensor_tensor_scan(start, ones[:, 0:NE], cnt, 0.0, ALU.mult, ALU.add)
            link(dve.tensor_scalar(nblk, cnt, 0.0, None, ALU.is_gt))
            for m in range(1, -(-T // BLK)):
                link(dve.scalar_tensor_tensor(nblk, cnt, float(m * BLK), nblk, ALU.is_gt, ALU.add))
            link(dve.tensor_scalar(nblk[:, 0:1], nblk[:, 0:1], 1.0, None, ALU.max))
            dve.tensor_tensor(start, start, cnt, ALU.subtract)
            link(dve.tensor_tensor_scan(cum, ones[:, 0:NE], nblk, 0.0, ALU.mult, ALU.add))
            link(dve.tensor_tensor(sid, cum, nblk, ALU.subtract))
            link(dve.scalar_tensor_tensor(off, sid, -float(BLK), start, ALU.mult, ALU.add))
            cs = col[0:NSTEP]
            dve.tensor_scalar(tle[0:NSTEP], cum[0:NSTEP], cs, None, ALU.is_le)
            link(dve.tensor_scalar(tid[0:NSTEP], sid[0:NSTEP], cs, None, ALU.is_le))
            dve.tensor_reduce(tab[0:NSTEP, 0:1], tle[0:NSTEP], AX.X, ALU.add)
            link(dve.tensor_tensor(tid[0:NSTEP], tid[0:NSTEP], tle[0:NSTEP], ALU.subtract))
            link(mul(tid[0:NSTEP], tid[0:NSTEP], off[0:NSTEP]))
            link(dve.tensor_reduce(tab[0:NSTEP, 1:2], tid[0:NSTEP], AX.X, ALU.add))
            link(dve.scalar_tensor_tensor(tab[0:NSTEP, 1:2], cs, float(BLK), tab[0:NSTEP, 1:2], ALU.mult, ALU.add))
            dve.tensor_scalar(tab[0:NSTEP, 1:2], tab[0:NSTEP, 1:2], float(NA), None, ALU.min).then_inc(tab_ready, 1)
            link(dve.tensor_copy(steps_i[0:1, 128:129], cum[0:1, NE - 1:NE]))
            q = 0
            for i in range(3):
                rank = bank[1][over(i), NE * i:NE * i + NE]
                for c, h in enumerate((hot1, hot2)):
                    for out, per_expert in ((rnk, rank), (pos, start[over(i)]), (stp, sid[over(i)])):
                        ins = dve.tensor_tensor_reduce(junk[over(i), q, :], h[over(i), i, :], per_expert, 1.0, 0.0, ALU.mult,
                                                       ALU.add, out[over(i), i, c:c + 1])
                        q += 1
            link(ins)
            link(add(pos, pos, rnk))
            dve.sem_inc(ranks_read, 1)

            def step_tokens(s):
                for part_ in range(2):
                    dve.wait_ge(xw_ps, 2 * s + 1 + part_)
                    mul(xw[:, 8 * part_:8 * part_ + 8, :], bk(4 + part_, 8, BLK),
                        g2w[:, 8 * part_:8 * part_ + 8].unsqueeze(2).to_broadcast([P, 8, BLK])).then_inc(xw_ready, 1)

            def take_window(s):
                at = dve.value_load(steps_i[0:1, bass.ds(s + 64, 1)], min_val=0, max_val=NA)
                dve.tensor_copy(window[:, 0:2, :], pick[:, 0:2, bass.ds(at, BLK)]).then_inc(window_ready, 1)
                dve.tensor_copy(window[0:TS, 2, :], pick[0:TS, 2, bass.ds(at, BLK)]).then_inc(window_ready, 2)

            step_tokens(0)
            dve.wait_ge(tab_ps, 1)
            link(dve.tensor_copy(steps_i[0:1, 0:NSTEP], bank[2][0:1, 0:NSTEP]))
            dve.tensor_copy(steps_i[0:1, 64:64 + NSTEP], bank[2][0:1, 64:64 + NSTEP]).then_inc(steps_ready, 1)
            for i in range(3):
                n = over(i)
                link(dve.tensor_scalar(pick[n, i, 0:NA], row[n, 0:NA], pos[n, i, 0:1], None, ALU.is_equal))
                dve.scalar_tensor_tensor(pick[n, i, 0:NA], row[n, 0:NA], pos[n, i, 1:2], pick[n, i, 0:NA],
                                         ALU.is_equal, ALU.add).then_inc(pick_ready, 1)
            dve.wait_ge(steps_ready, 1)
            dve.wait_ge(xd_ps, 2)
            dve.wait_ge(pick_ready, 3)
            take_window(1)
            dve.wait_ge(r_exp, 1)
            link(dve.tensor_reduce(gsum, dg[:, :, 0:NG], AX.X, ALU.add))
            link(dve.tensor_scalar(gates[:, :, 1], dg[:, :, NG], 1.0, None, ALU.add))
            link(mul(gsum, gsum, gates[:, :, 1]))
            link(dve.reciprocal(gates[:, :, 0], gsum))
            link(mul(gates[:, :, 1], gates[:, :, 0], dg[:, :, NG]))
            link(dve.tensor_scalar(blk, rnk, float(BLK), None, ALU.is_ge))
            for m in range(2, -(-T // BLK)):
                link(dve.scalar_tensor_tensor(blk, rnk, float(m * BLK), blk, ALU.is_ge, ALU.add))
            link(add(stp, stp, blk))
            link(dve.scalar_tensor_tensor(rnk, blk, -float(BLK), rnk, ALU.mult, ALU.add))
            for i in range(3):
                link(dve.tensor_scalar(tokid[:, i:i + 1], col, float(TILES[i][0]), None, ALU.add))
            for i in range(3):
                n = over(i)
                for c in range(2):
                    q = 2 * i + c
                    dve.tensor_scalar(ohr[n, q, :].rearrange("p (h r) -> p h r", h=2),
                                      row[n, 0:BLK].unsqueeze(1).to_broadcast([TILES[i][1], 2, BLK]), rnk[n, i, c:c + 1],
                                      None, ALU.is_equal)
                    ins = dve.tensor_scalar(ohs[n, q, 2 * NSTEP:], row[n, 0:NSTEP], stp[n, i, c:c + 1], None, ALU.is_equal)
            link(ins)
            for i in range(3):
                n = over(i)
                for c in range(2):
                    q = 2 * i + c
                    dve.tensor_scalar(ohs[n, q, 0:NSTEP], ohs[n, q, 2 * NSTEP:], tokid[n, i:i + 1], None, ALU.mult)
                    ins = dve.tensor_scalar(ohs[n, q, NSTEP:2 * NSTEP], ohs[n, q, 2 * NSTEP:], gates[n, i, c:c + 1], None,
                                            ALU.mult)
                ins.then_inc(ohs_ready, 1)

            dve.wait_ge(rows_ps, 1)
            R = bk(2, 3, NSTEP, at=128)
            link(dve.tensor_copy(gate_of, R[:, 1, :]))
            link(dve.tensor_scalar(half, col, float(BLK), float(-NONE), ALU.is_ge, ALU.subtract))
            link(dve.tensor_scalar(idx_f, R[:, 0, :], 2.0, half, ALU.mult, ALU.add))
            link(dve.scalar_tensor_tensor(idx_f, R[:, 2, :], -float(NONE), idx_f, ALU.mult, ALU.add))
            dve.tensor_copy(idx_all, idx_f).then_inc(rows_ready, 1)

            def gated():
                mul(hg, h1s, bk(1, 256)).then_inc(hg_ready, 1)

            def turned(s):
                dve.wait_ge(hT_ps, s)
                dve.tensor_copy(hT.rearrange("p j h t -> p (j h t)"), bk(6, 256)).then_inc(hT_ready, 1)

            def output(s):
                dve.wait_ge(ye_ps, s)
                dve.wait_ge(ye_free, s)
                dve.tensor_scalar(ystage[:, 512:1024], bk(3, 512), gate_of[:, bass.ds(s - 1, 1)], None, ALU.mult
                                  ).then_inc(ye_v, 1)

            dve.wait_ge(h1_sb, 1)
            dve.wait_ge(h3_ps, 1)
            gated()
            n = step_count(dve)
            with dve.Fori(1, NSTEP + 1) as s:
                with dve.If(s < n + 1):
                    with dve.If(s < n):
                        dve.wait_ge(xd_ps, 2 * s + 2)
                        dve.tensor_copy(xd[:, 512:1024], bk(5, 512)).then_inc(xd_v, 1)
                        take_window(s + 1)
                        step_tokens(s)
                    turned(s)
                    output(s)
                    with dve.If(s < n):
                        dve.wait_ge(h1_sb, s + 1)
                        dve.wait_ge(h3_ps, s + 1)
                        gated()


NORM_ORDER = [NH, NH + 1] + list(range(NH))
NORM_AT = [0, 1] + list(range(4, 12))
GROUP_AT = [3, 0, 1, 2]
OUT_BANK = [0, 1, 2, 3] + [(4, 5, 0, 1, 2)[i % 5] for i in range(KT - 4)]
W_BEFORE = [64, 64, 48]
KV_OUT = 16 * (2 + 2 * NB)
OUTS_MIX = 16 * (3 + 1 + TB)


_INS = ["x_prompt", "x_sample", "state_conv", "cache_k", "cache_v", "norm1_g", "w_in", "conv_w", "conv_b",
        "conv_norm_g", "conv_norm_b", "q_norm_g", "k_norm_g", "attn_sinks", "w_out", "norm2_g",
        "w_router_group", "b_router_group", "w_router_expert", "b_router_expert", "w1", "w3", "w2"]
_SHAPES = {"x_prompt": (TP, D), "x_sample": (TS, D), "state_conv": (NB, PAST, DC), "cache_k": (NB, W, NKV * HD),
           "cache_v": (NB, W, NKV * HD)}
_OUTS = [((T, D), (T, D)), ((PAST, DC), (1, 1, PAST, DC)),
         ((W, NKV * HD), (1, 1, W, NKV, HD)), ((W, NKV * HD), (1, 1, W, NKV, HD)),
         ((NB, PAST, DC), (1, NB, PAST, DC)), ((NB, W, NKV * HD), (1, NB, W, NKV, HD)),
         ((NB, W, NKV * HD), (1, NB, W, NKV, HD))]


def kernel(**inputs):
    import concourse.bacc as bacc
    from concourse.bass_utils import run_bass_kernel_spmd

    nc = bacc.Bacc("TRN2", target_bir_lowering=False, num_devices=1)
    arrays, args = {}, []
    for name in _INS:
        a = np.ascontiguousarray(inputs[name])
        a = a.reshape(_SHAPES.get(name, a.shape[1:]))
        arrays[f"in_{name}"] = a
        args.append(nc.dram_tensor(f"in_{name}", a.shape, F32, kind="ExternalInput").ap())
    arrays["shape_tables"] = a = shape_constants()
    args.append(nc.dram_tensor("shape_tables", a.shape, F32, kind="ExternalInput").ap())
    for i, (shape, _) in enumerate(_OUTS):
        args.append(nc.dram_tensor(f"out_{i}", shape, F32, kind="ExternalOutput").ap())
    hybrid_layer(nc, *args)
    r = run_bass_kernel_spmd(nc, [arrays], core_ids=[0])
    y, *rest = (np.asarray(r.results[0][f"out_{i}"]).reshape(full) for i, (_, full) in enumerate(_OUTS))
    return (y[:TP].reshape(1, TP, D), y[TP:].reshape(NB, TB, D), *rest)
```
